# Optimizing a Trainium2 kernel written in Bass

```python
import jax
import jax.numpy as jnp
from jax import lax
import numpy as np

D_MODEL = 1024
BATCH = 1
SEQ = 256
DEPTH = 2

N_MIXERS = 3
CHUNK = 128
Q_BLOCK = 128
NORM_EPS = 1e-6
MEM_TOKENS = 256
MEM_HEADS = 4
MEM_HEAD_DIM = 128
MEM_WIDTH = MEM_HEADS * MEM_HEAD_DIM
GM_GROUPS = 8
GM_GROUP_DIM = 128
GM_WIDTH = GM_GROUPS * GM_GROUP_DIM
MLA_HEADS = 8
MLA_NOPE = 128
MLA_ROPE = 64
MLA_V = 128
MLA_Q_LORA = 768
MLA_KV_LORA = 256
ROPE_THETA = 10000.0
ML_HEADS = 4
ML_DV = 256
ML_DK = 128
CONV_K = 4
FF_DENSE = 2816
N_EXPERTS = 8
TOP_K = 2
FF_EXPERT = 1792

kernel_name = 'hybrid_gmlp_mla_mlstm_memory_moe_trunk'

def rms_norm(x, g):
    xf = x.astype(jnp.float32)
    y = xf * lax.rsqrt(jnp.mean(xf * xf, axis=-1, keepdims=True) + NORM_EPS)
    return (y * g.astype(jnp.float32)).astype(x.dtype)

def swiglu(x, w_gate, w_up, w_down):
    return (jax.nn.silu(x @ w_gate) * (x @ w_up)) @ w_down

def rope_angles(positions, dim):
    inv_freq = 1.0 / (ROPE_THETA ** (jnp.arange(0, dim, 2, dtype=jnp.float32) / dim))
    ang = positions.astype(jnp.float32)[..., None] * inv_freq
    return jnp.cos(ang), jnp.sin(ang)

def apply_rope(x, cos, sin):
    xf = x.astype(jnp.float32)
    x1, x2 = jnp.split(xf, 2, axis=-1)
    c = cos[:, :, None, :]
    s = sin[:, :, None, :]
    return jnp.concatenate([x1 * c - x2 * s, x2 * c + x1 * s], axis=-1).astype(x.dtype)

def memory_cross_attention(q_cols, mem, mem_norm_g, w_mem_kv):
    b, s, _ = q_cols.shape
    q = q_cols.reshape(b, s, MEM_HEADS, MEM_HEAD_DIM)
    kv = rms_norm(mem, mem_norm_g) @ w_mem_kv
    k, v = jnp.split(kv, 2, axis=-1)
    k = k.reshape(b, -1, MEM_HEADS, MEM_HEAD_DIM)
    v = v.reshape(b, -1, MEM_HEADS, MEM_HEAD_DIM)
    scores = jnp.einsum('bshd,bmhd->bhsm', q, k).astype(jnp.float32) * MEM_HEAD_DIM ** -0.5
    p = jax.nn.softmax(scores, axis=-1).astype(v.dtype)
    return jnp.einsum('bhsm,bmhd->bshd', p, v).reshape(b, s, MEM_WIDTH)

def gmlp_mixer(cols, v_norm_g, w_s, b_s):
    b, s, _ = cols.shape
    u, v = jnp.split(jax.nn.gelu(cols, approximate=False), 2, axis=-1)
    n = s // CHUNK
    v = rms_norm(v.reshape(b, n, CHUNK, GM_GROUPS, GM_GROUP_DIM),
                 v_norm_g.reshape(GM_GROUPS, GM_GROUP_DIM))
    causal = jnp.tril(jnp.ones((CHUNK, CHUNK), dtype=w_s.dtype))
    mixed = jnp.einsum('gts,bnsgc->bntgc', w_s * causal, v) + b_s.T[:, :, None]
    return u * mixed.reshape(b, s, GM_WIDTH)

def mla_mixer(cols, positions, q_norm_g, w_uq, kv_norm_g, w_ukv):
    b, s, _ = cols.shape
    c_q = cols[..., :MLA_Q_LORA]
    c_kv = cols[..., MLA_Q_LORA:MLA_Q_LORA + MLA_KV_LORA]
    k_rope = cols[..., MLA_Q_LORA + MLA_KV_LORA:]
    q = (rms_norm(c_q, q_norm_g) @ w_uq).reshape(b, s, MLA_HEADS, MLA_NOPE + MLA_ROPE)
    kv = (rms_norm(c_kv, kv_norm_g) @ w_ukv).reshape(b, s, MLA_HEADS, MLA_NOPE + MLA_V)
    q_nope, q_rope = q[..., :MLA_NOPE], q[..., MLA_NOPE:]
    k_nope, v = kv[..., :MLA_NOPE], kv[..., MLA_NOPE:]
    cos, sin = rope_angles(positions, MLA_ROPE)
    q_rope = apply_rope(q_rope, cos, sin)
    k_rope = apply_rope(k_rope[:, :, None, :], cos, sin)[:, :, 0, :]
    scale = (MLA_NOPE + MLA_ROPE) ** -0.5
    nb = s // Q_BLOCK

    def to_blocks(t):
        return jnp.moveaxis(t.reshape(b, nb, Q_BLOCK, *t.shape[2:]), 1, 0)

    key_pos = jnp.arange(s)

    def attend_block(args):
        qn, qr, blk = args
        scores = (jnp.einsum('bqhd,bkhd->bhqk', qn, k_nope)
                  + jnp.einsum('bqhr,bkr->bhqk', qr, k_rope)).astype(jnp.float32) * scale
        query_pos = blk * Q_BLOCK + jnp.arange(Q_BLOCK)
        scores = jnp.where(key_pos[None, :] <= query_pos[:, None], scores, -jnp.inf)
        p = jax.nn.softmax(scores, axis=-1).astype(v.dtype)
        return jnp.einsum('bhqk,bkhd->bqhd', p, v)

    out = lax.map(attend_block, (to_blocks(q_nope), to_blocks(q_rope), jnp.arange(nb)))
    return jnp.moveaxis(out, 0, 1).reshape(b, s, MLA_HEADS * MLA_V)

def causal_depthwise_conv(x, w, bias):
    y = lax.conv_general_dilated(
        x, w[:, None, :].astype(x.dtype), window_strides=(1,), padding=[(CONV_K - 1, 0)],
        dimension_numbers=('NWC', 'WIO', 'NWC'), feature_group_count=x.shape[-1])
    return y + bias.astype(x.dtype)

def mlstm_chunkwise(q, k, v, i_pre, f_pre):
    b, s, nh, dk = q.shape
    dv = v.shape[-1]
    n = s // CHUNK
    f32 = jnp.float32

    def chunks(t):
        return t.astype(f32).reshape(b, n, CHUNK, nh, -1).transpose(0, 3, 1, 2, 4)

    def gate_chunks(t):
        return t.astype(f32).reshape(b, n, CHUNK, nh).transpose(0, 3, 1, 2)

    q, k, v = chunks(q), chunks(k), chunks(v)
    log_i = gate_chunks(i_pre)
    log_f = jax.nn.log_sigmoid(gate_chunks(f_pre))
    cum_f = jnp.cumsum(log_f, axis=-1)
    causal = jnp.tril(jnp.ones((CHUNK, CHUNK), dtype=bool))
    log_d = jnp.where(causal, cum_f[..., :, None] - cum_f[..., None, :] + log_i[..., None, :], -jnp.inf)
    m_intra = jnp.max(log_d, axis=-1)
    f_total = cum_f[..., -1]
    log_w = f_total[..., None] - cum_f + log_i
    m_local = jnp.max(log_w, axis=-1)
    w_local = jnp.exp(log_w - m_local[..., None])
    c_local = jnp.einsum('bhnlk,bhnlv->bhnkv', k * w_local[..., None], v)
    n_local = jnp.einsum('bhnl,bhnlk->bhnk', w_local, k)

    def step(carry, inp):
        c_prev, n_prev, m_prev = carry
        c_loc, n_loc, m_loc, f_tot = inp
        m_new = jnp.maximum(f_tot + m_prev, m_loc)
        decay = jnp.exp(f_tot + m_prev - m_new)
        scale = jnp.exp(m_loc - m_new)
        c_new = decay[..., None, None] * c_prev + scale[..., None, None] * c_loc
        n_new = decay[..., None] * n_prev + scale[..., None] * n_loc
        return (c_new, n_new, m_new), (c_prev, n_prev, m_prev)

    init = (jnp.zeros((b, nh, dk, dv), f32), jnp.zeros((b, nh, dk), f32), jnp.zeros((b, nh), f32))
    xs = (jnp.moveaxis(c_local, 2, 0), jnp.moveaxis(n_local, 2, 0),
          jnp.moveaxis(m_local, 2, 0), jnp.moveaxis(f_total, 2, 0))
    _, (c_in, n_in, m_in) = lax.scan(step, init, xs)
    c_in = jnp.moveaxis(c_in, 0, 2)
    n_in = jnp.moveaxis(n_in, 0, 2)
    m_in = jnp.moveaxis(m_in, 0, 2)
    log_inter = cum_f + m_in[..., None]
    m_t = jnp.maximum(log_inter, m_intra)
    inter = jnp.exp(log_inter - m_t)
    p = jnp.einsum('bhnlk,bhnsk->bhnls', q, k) * jnp.exp(log_d - m_t[..., None])
    num = inter[..., None] * jnp.einsum('bhnlk,bhnkv->bhnlv', q, c_in) + jnp.einsum('bhnls,bhnsv->bhnlv', p, v)
    den = inter * jnp.einsum('bhnlk,bhnk->bhnl', q, n_in) + jnp.sum(p, axis=-1)
    h = num / jnp.maximum(jnp.abs(den), jnp.exp(-m_t))[..., None]
    return h.transpose(0, 2, 3, 1, 4).reshape(b, s, nh, dv)

def mlstm_mixer(cols, conv_w, conv_b, gate_b, h_norm_g):
    b, s, _ = cols.shape
    qk_w = 2 * ML_HEADS * ML_DK
    hv = ML_HEADS * ML_DV
    qk = jax.nn.silu(causal_depthwise_conv(cols[..., :qk_w], conv_w, conv_b))
    q, k = jnp.split(qk, 2, axis=-1)
    v = cols[..., qk_w:qk_w + hv]
    o = cols[..., qk_w + hv:qk_w + 2 * hv]
    gates = cols[..., qk_w + 2 * hv:].astype(jnp.float32) + gate_b.astype(jnp.float32)
    i_pre, f_pre = gates[..., :ML_HEADS], gates[..., ML_HEADS:]
    h = mlstm_chunkwise(q.reshape(b, s, ML_HEADS, ML_DK),
                        k.reshape(b, s, ML_HEADS, ML_DK) * ML_DK ** -0.5,
                        v.reshape(b, s, ML_HEADS, ML_DV), i_pre, f_pre)
    h = rms_norm(h, h_norm_g.reshape(ML_HEADS, ML_DV)).astype(cols.dtype)
    return h.reshape(b, s, hv) * jax.nn.sigmoid(o)

def moe_ffn(x, w_router, b_router, w_gate, w_up, w_down):
    logits = (x @ w_router).astype(jnp.float32) + b_router.astype(jnp.float32)
    top_vals, top_idx = lax.top_k(logits, TOP_K)
    weights = jax.nn.softmax(top_vals, axis=-1)
    gates = jnp.sum(jax.nn.one_hot(top_idx, N_EXPERTS, dtype=jnp.float32) * weights[..., None], axis=-2)
    out = jnp.zeros_like(x)
    for e in range(N_EXPERTS):
        out = out + gates[..., e:e + 1].astype(x.dtype) * swiglu(x, w_gate[e], w_up[e], w_down[e])
    return out

def _n_layers_of(start, period):
    return len(range(start, DEPTH, period))

def setup_inputs(seed: int = 0) -> dict:
    key = jax.random.key(seed)
    keys = list(jax.random.split(key, 40))
    f32 = jnp.float32

    def nk():
        return keys.pop()

    def w(shape, fan_in):
        return jax.random.normal(nk(), shape, f32) * fan_in ** -0.5

    def gain(shape):
        return 1.0 + 0.02 * jax.random.normal(nk(), shape, f32)

    na, nb, nc = (_n_layers_of(m, N_MIXERS) for m in range(N_MIXERS))
    nd, ne = _n_layers_of(0, 2), _n_layers_of(1, 2)
    gm_in = 2 * GM_WIDTH + MEM_WIDTH
    mla_in = MLA_Q_LORA + MLA_KV_LORA + MLA_ROPE + MEM_WIDTH
    ml_qk = 2 * ML_HEADS * ML_DK
    ml_in = ml_qk + 2 * ML_HEADS * ML_DV + 2 * ML_HEADS + MEM_WIDTH

    x = jax.random.normal(nk(), (BATCH, SEQ, D_MODEL), f32)
    mem = jax.random.normal(nk(), (BATCH, MEM_TOKENS, D_MODEL), f32)
    positions = (jnp.arange(SEQ, dtype=jnp.int32)[None, :]
                 + jax.random.randint(nk(), (BATCH, 1), 0, 1024, dtype=jnp.int32))
    i_bias = -1.0 + 0.1 * jax.random.normal(nk(), (nc, ML_HEADS), f32)
    f_bias = 3.0 + 3.0 * jax.random.uniform(nk(), (nc, ML_HEADS), f32)
    return {
        'x': x,
        'mem': mem,
        'positions': positions,
        'attn_norm': gain((DEPTH, D_MODEL)),
        'mem_norm': gain((DEPTH, D_MODEL)),
        'w_mem_kv': w((DEPTH, D_MODEL, 2 * MEM_WIDTH), D_MODEL),
        'ffn_norm': gain((DEPTH, D_MODEL)),
        'final_norm': gain((D_MODEL,)),
        'gm_w_in': w((na, D_MODEL, gm_in), D_MODEL),
        'gm_v_norm': gain((na, GM_WIDTH)),
        'gm_w_s': w((na, GM_GROUPS, CHUNK, CHUNK), CHUNK),
        'gm_b_s': 1.0 + 0.1 * jax.random.normal(nk(), (na, GM_GROUPS, CHUNK), f32),
        'gm_w_out': w((na, GM_WIDTH + MEM_WIDTH, D_MODEL), GM_WIDTH + MEM_WIDTH),
        'mla_w_in': w((nb, D_MODEL, mla_in), D_MODEL),
        'mla_q_norm': gain((nb, MLA_Q_LORA)),
        'mla_w_uq': w((nb, MLA_Q_LORA, MLA_HEADS * (MLA_NOPE + MLA_ROPE)), MLA_Q_LORA),
        'mla_kv_norm': gain((nb, MLA_KV_LORA)),
        'mla_w_ukv': w((nb, MLA_KV_LORA, MLA_HEADS * (MLA_NOPE + MLA_V)), MLA_KV_LORA),
        'mla_w_out': w((nb, MLA_HEADS * MLA_V + MEM_WIDTH, D_MODEL), MLA_HEADS * MLA_V + MEM_WIDTH),
        'ml_w_in': w((nc, D_MODEL, ml_in), D_MODEL),
        'ml_conv_w': w((nc, CONV_K, ml_qk), CONV_K),
        'ml_conv_b': 0.02 * jax.random.normal(nk(), (nc, ml_qk), f32),
        'ml_gate_b': jnp.concatenate([i_bias, f_bias], axis=-1),
        'ml_h_norm': gain((nc, ML_HEADS * ML_DV)),
        'ml_w_out': w((nc, ML_HEADS * ML_DV + MEM_WIDTH, D_MODEL), ML_HEADS * ML_DV + MEM_WIDTH),
        'ff_w_gate': w((nd, D_MODEL, FF_DENSE), D_MODEL),
        'ff_w_up': w((nd, D_MODEL, FF_DENSE), D_MODEL),
        'ff_w_down': w((nd, FF_DENSE, D_MODEL), FF_DENSE),
        'moe_w_router': w((ne, D_MODEL, N_EXPERTS), D_MODEL),
        'moe_b_router': 0.01 * jax.random.normal(nk(), (ne, N_EXPERTS), f32),
        'moe_w_gate': w((ne, N_EXPERTS, D_MODEL, FF_EXPERT), D_MODEL),
        'moe_w_up': w((ne, N_EXPERTS, D_MODEL, FF_EXPERT), D_MODEL),
        'moe_w_down': w((ne, N_EXPERTS, FF_EXPERT, D_MODEL), FF_EXPERT),
    }

def reference(x, mem, positions, attn_norm, mem_norm, w_mem_kv, ffn_norm, final_norm,
              gm_w_in, gm_v_norm, gm_w_s, gm_b_s, gm_w_out,
              mla_w_in, mla_q_norm, mla_w_uq, mla_kv_norm, mla_w_ukv, mla_w_out,
              ml_w_in, ml_conv_w, ml_conv_b, ml_gate_b, ml_h_norm, ml_w_out,
              ff_w_gate, ff_w_up, ff_w_down,
              moe_w_router, moe_b_router, moe_w_gate, moe_w_up, moe_w_down):
    h = x
    for layer in range(DEPTH):
        kind, j = layer % N_MIXERS, layer // N_MIXERS
        xn = rms_norm(h, attn_norm[layer])
        if kind == 0:
            proj = xn @ gm_w_in[j]
            mix = gmlp_mixer(proj[..., :-MEM_WIDTH], gm_v_norm[j], gm_w_s[j], gm_b_s[j])
            w_out = gm_w_out[j]
        elif kind == 1:
            proj = xn @ mla_w_in[j]
            mix = mla_mixer(proj[..., :-MEM_WIDTH], positions, mla_q_norm[j], mla_w_uq[j],
                            mla_kv_norm[j], mla_w_ukv[j])
            w_out = mla_w_out[j]
        else:
            proj = xn @ ml_w_in[j]
            mix = mlstm_mixer(proj[..., :-MEM_WIDTH], ml_conv_w[j], ml_conv_b[j], ml_gate_b[j], ml_h_norm[j])
            w_out = ml_w_out[j]
        mem_out = memory_cross_attention(proj[..., -MEM_WIDTH:], mem, mem_norm[layer], w_mem_kv[layer])
        h = h + jnp.concatenate([mix, mem_out], axis=-1) @ w_out
        xn = rms_norm(h, ffn_norm[layer])
        c = layer // 2
        if layer % 2 == 0:
            h = h + swiglu(xn, ff_w_gate[c], ff_w_up[c], ff_w_down[c])
        else:
            h = h + moe_ffn(xn, moe_w_router[c], moe_b_router[c], moe_w_gate[c], moe_w_up[c], moe_w_down[c])
    return rms_norm(h, final_norm)


_drawn_inputs = setup_inputs


def setup_inputs(seed=0):
    import zlib

    import numpy as np

    out = dict(_drawn_inputs(seed))
    spreads = {}
    factors = {'mem_norm': 4.129,
     'final_norm': 7.682,
     'gm_v_norm': 3.61,
     'mla_q_norm': 4.051,
     'mla_kv_norm': 3.107,
     'moe_b_router': 7.257}
    for name, (base, spread) in spreads.items():
        noise = np.random.default_rng([zlib.crc32(name.encode()), seed]).standard_normal(out[name].shape)
        drawn = base * np.exp(spread * noise) if base else spread * noise
        out[name] = jnp.asarray(drawn.astype(out[name].dtype))
    for name, factor in factors.items():
        out[name] = (out[name] * factor).astype(out[name].dtype)
    return out
```

```python
import numpy as np

import concourse.bass as bass
from concourse import mybir
from contextlib import ExitStack

F32 = mybir.dt.float32
F32R = mybir.dt.float32r
I32 = mybir.dt.int32
ALU = mybir.AluOpType
ACT = mybir.ActivationFunctionType
AX = mybir.AxisListType

P = 128
D = 1024
SEQ = 256
NT = SEQ // P
KD = D // P
MH = 4
MEMW = MH * P
GM = 1024
NG = GM // P
HEADS = 8
NOPE, ROPE = 128, 64
QK = NOPE + ROPE
QL, KVL = 768, 256
FF = 2816
FHALF = FF // 2
FB = FHALF // P
FCH = FHALF // 4
E = 8
FE = 1792
EB = FE // P
ECH = FE // 2
EN = ECH // 2
EPS = 1e-6
MEM_SCALE = float(P) ** -0.5
MLA_SCALE = float(QK) ** -0.5
NEG = -1e30
MAGIC = 12582912.0
TWO_PI = 2 * np.pi
CAT = KD + MH

UNIT = 3584
RAW, SPLIT = 3, 2


def two_pi_parts():
    parts, rest = [], TWO_PI
    for _ in range(3):
        m, e = np.frexp(rest)
        part = float(np.floor(m * 512) / 512 * 2.0 ** int(e))
        parts.append(part)
        rest -= part
    return parts + [float(np.float32(rest))]


def build(nc, x, mem, positions, attn_norm, mem_norm, w_mem_kv, ffn_norm, final_norm,
          gm_w_in, gm_v_norm, gm_w_s, gm_b_s, gm_w_out,
          mla_w_in, mla_q_norm, mla_w_uq, mla_kv_norm, mla_w_ukv, mla_w_out,
          ff_w_gate, ff_w_up, ff_w_down,
          moe_w_router, moe_b_router, moe_w_gate, moe_w_up, moe_w_down, rope_freq, out):
    def rows(w, k0, k, c0, n):
        return w[k0 * P:(k0 + k) * P, c0:c0 + n].rearrange("(k p) n -> p k n", p=P)

    units = []

    def add(w, k0, k, c0, n):
        units.append((rows(w, k0, k, c0, n), k, n))
        return len(units) - 1

    def add_wide(w, c0):
        return [add(w, 0, 4, c0, 512), add(w, 4, 4, c0, 512)]

    def add_kv(layer):
        w = w_mem_kv[layer]
        return [add(w, 0, KD, 0, 256), add(w, 0, KD, 256, 256)], add_wide(w, MEMW)

    def add_out(w):
        return [[add(w, 0, 6, c, 512), add(w, 6, 6, c, 512)] for c in (0, 512)]

    U_K0, U_V0 = add_kv(0)
    w = gm_w_in[0]
    U_Q0 = [add(w, 0, KD, 2 * GM + c, 256) for c in (0, 256)]
    U_GV = [add_wide(w, GM + c) for c in (0, 512)]
    U_GU = [add_wide(w, c) for c in (0, 512)]
    U_O0 = add_out(gm_w_out[0])
    U_FF = []
    for h in range(2):
        gu = [(add(ff_w_gate[0], 0, KD, h * FHALF + c * FCH, FCH),
               add(ff_w_up[0], 0, KD, h * FHALF + c * FCH, FCH)) for c in range(4)]
        U_FF.append((gu, [add(ff_w_down[0], h * FB, FB, c * 256, 256) for c in range(4)]))
    U_K1, U_V1 = add_kv(1)
    w = mla_w_in[0]
    U_Q1 = [add(w, 0, KD, QL + KVL + ROPE + c, 256) for c in (0, 256)]
    U_C = [add_wide(w, c) for c in (0, 512)]
    U_KR = add(w, 0, KD, QL + KVL, ROPE)
    U_UQ = [add(mla_w_uq[0], 0, QL // P, c * 2 * QK, 2 * QK) for c in range(4)]
    U_UKV = [add(mla_w_ukv[0], 0, KVL // P, c * 1024, 1024) for c in range(2)]
    U_O1 = add_out(mla_w_out[0])
    U_MOE = len(units)
    MU = 12
    moe_shape = [(4, ECH)] * 8 + [(7, 512)] * 4

    def shape_of(u):
        return units[u][1:] if u < U_MOE else moe_shape[(u - U_MOE) % MU]

    A_K = [(0, 1), (41, 42)]
    A_V = [2, 43]
    A_Q = [(3, 4), (44, 45)]
    A_MO = [5, 46]
    A_GV, A_GU = (9, 10), (11, 12)
    A_MIX = (13, 14)
    A_OUT = [(15, 16), (67, 68)]
    A_FF = [17, 29]
    A_C, A_KR = (50, 51), 52
    A_UQ = 53
    A_UKV = 57
    A_LO = 61
    A_RT = 69
    A_MOE = 71
    T_WS = 0
    T_MEM = [2, 34]
    T_X = [6, 38]
    T_PM = [10, 42]
    T_U = 14
    T_FN = [18, 59]
    T_FH = [22, 28]
    T_C = 46
    T_ROPE = 50
    T_PL = 53
    T_MOE = 63
    S_MEM = [0, 4]
    S_LAT = 8
    S_MOE = 14

    MEM_GROUPS = [(t, (2 * i, 2 * i + 1), SEQ) for t in range(NT) for i in range(2)]
    LAT_GROUPS = ([(0, tuple(range(4 * i, 4 * i + 4)), P) for i in range(2)]
                  + [(1, (2 * i, 2 * i + 1), SEQ) for i in range(4)])

    ctx = ExitStack()
    with ctx:
        def sb(name, shape, dt=F32):
            return ctx.enter_context(nc.sbuf_tensor(name, shape, dt))

        def sem(name):
            return ctx.enter_context(nc.semaphore(name))

        raw = sb("raw", [P, RAW * UNIT])
        hi = sb("hi", [P, SPLIT * UNIT], F32R)
        lo = sb("lo", [P, SPLIT * UNIT], F32R)
        xT = [sb(f"xT_{s}", [P, CAT * SEQ], F32R) for s in ("hi", "lo")]
        wk = [sb(f"wk_{s}", [P, 3072], F32R) for s in ("hi", "lo")]
        sel = sb("sel", [P, NT * P], F32R)
        selT = sb("selT", [P, NT * P], F32R)
        h = sb("h", [P, NT, D])
        R1 = sb("R1", [P, 2048])
        R2 = sb("R2", [P, 2048])
        R3 = sb("R3", [P, 4096])
        GB1 = sb("GB1", [P, D])
        GB2 = sb("GB2", [P, D])
        krT = sb("krT", [P, 2, SEQ])
        kr = sb("kr", [P, 2, NT, P])
        kraw = sb("kraw", [P, NT, ROPE])
        ident = sb("ident", [P, P])
        ones = sb("ones", [P, P])
        tri = sb("tri", [P, P])
        tris = sb("tris", [P, P])
        cmask = sb("cmask", [P, P])
        freq = sb("freq", [P, 32])
        posi = sb("posi", [P, NT], I32)
        posf = sb("posf", [P, NT])
        cs = sb("cs", [P, 2, NT, 32])
        ssum = sb("ssum", [P, 9, 2])
        rstd = sb("rstd", [P, 9, 2])
        vss = sb("vss", [P, NT, NG])
        vrs = sb("vrs", [P, NT, NG])
        mhalf = sb("mhalf", [P, NT * NG])
        gbs = sb("gbs", [P, NG])
        mx = sb("mx", [P, 14, 4])
        nb = sb("nb", [P, 14, 4])
        den = sb("den", [P, 14, 4])
        rden = sb("rden", [P, 14, 4])
        wr = sb("wr", [P, KD, E])
        br = sb("br", [P, E])
        prio = sb("prio", [P, E])
        rt = sb("rt", [P, 12, NT, E])
        r1 = sb("r1", [P, 10, NT])
        rsm = sb("rsm", [P, NT * 32])
        nround = sb("nround", [P, 1], I32)
        slot_of = sb("slot_of", [P, NT, 2 * E + 1])
        gate_of = sb("gate_of", [P, NT, 2 * E + 1])

        A = [[ctx.enter_context(nc.psum_tensor(f"A{p}{t}", [P, 512], F32)) for t in range(2)]
             for p in range(2)]
        T = [ctx.enter_context(nc.psum_tensor(f"T{b}", [P, 512], F32)) for b in range(2)]
        S = [ctx.enter_context(nc.psum_tensor(f"S{b}", [P, 512], F32)) for b in range(2)]

        raw_full = [sem(f"raw_full{i}") for i in range(RAW)]
        hi_done = sem("hi_done")
        lo_done = sem("lo_done")
        used = sem("used")
        t_done, s_done = sem("t_done"), sem("s_done")
        o_done = sem("o_done")
        mixed_done, route_mm, scat_done = sem("mixed_done"), sem("route_mm"), sem("scat_done")
        a_free = [sem(f"a_free{i}") for i in range(2)]
        t_free = [sem(f"t_free{i}") for i in range(2)]
        s_free = [sem(f"s_free{i}") for i in range(2)]
        x_in, mem_in, ws_in = sem("x_in"), sem("mem_in"), sem("ws_in")
        gb1_in, gb2_in = sem("gb1_in"), sem("gb2_in")
        gbs_in, rope_in, rout_in, mem2_in = sem("gbs_in"), sem("rope_in"), sem("rout_in"), sem("mem2_in")
        consts = sem("consts")
        ssum_done = sem("ssum_done")
        rstd_done = sem("rstd_done")
        pool_step = sem("pool_step")
        xn_done = sem("xn_done")
        vss_done, vrs_done, vn_done = sem("vss_done"), sem("vrs_done"), sem("vn_done")
        max_done = sem("max_done")
        exp_done = sem("exp_done")
        prob_done = sem("prob_done")
        rope_ang, rope_cs, rope_done = sem("rope_ang"), sem("rope_cs"), sem("rope_done")
        kr_copied = sem("kr_copied")
        c_ready = sem("c_ready")
        rt_exp_in, rt_exp = sem("rt_exp_in"), sem("rt_exp")
        mask_done, route_done, moe_const = sem("mask_done"), sem("route_done"), sem("moe_const")
        sel_done = sem("sel_done")
        y_hi = sem("y_hi")
        xs_hi, xs_done = sem("xs_hi"), sem("xs_done")
        act_step = sem("act_step")
        dve_step = sem("dve_step")
        out_done = sem("out_done")
        block = ctx.enter_context(nc.Block())

        xTv = [a[:, :].rearrange("p (k s) -> p k s", s=SEQ) for a in xT]
        wkv = [a[:, 0:FB * SEQ].rearrange("p (k s) -> p k s", s=SEQ) for a in wk]
        xg = [a[:, 0:KD * P] for a in xT]
        hT = [a[:, KD * P:KD * P + EB * P] for a in xT]
        xs = [a[:, 0:NT * D].rearrange("p (t d) -> p t d", t=NT) for a in wk]
        ys = [a[:, NT * D:NT * D + D] for a in wk]
        xn = R1[:, :].rearrange("p (t d) -> p t d", t=NT)
        gu = xn
        lat = xn
        memt = R2[:, :].rearrange("p (t d) -> p t d", t=NT)
        gv = memt
        qn = R2[:, :].rearrange("p (h s) -> p h s", h=HEADS)
        xnT = R2[:, :].rearrange("p (k s) -> p k s", k=KD)
        fsilu = R2[:, 0:NT * FCH].rearrange("p (t n) -> p t n", t=NT)
        mk = R3[:, 0:1024].rearrange("p (h s) -> p h s", h=MH)
        mv = R3[:, 1024:2048].rearrange("p (t n) -> p t n", t=NT)
        mq = R3[:, 2048:3072].rearrange("p (h s) -> p h s", h=MH)
        wsT = R3[:, 3072:4096].rearrange("p (g s) -> p g s", g=NG)
        kn = R3[:, 0:2048].rearrange("p (h s) -> p h s", h=HEADS)
        lv = R3[:, 2048:4096].rearrange("p (t n) -> p t n", t=NT)
        fhid = R3[:, 0:NT * FHALF].rearrange("p (t n) -> p t n", t=NT)
        esilu = R3[:, 0:ECH]
        ehid = R3[:, ECH:2 * ECH]
        wsr = R3[:, 0:1024].rearrange("p (g s) -> p g s", g=NG)
        PP = R1[:, 0:1024].rearrange("p (a b) -> p a b", a=2)
        PPT = R1[:, 1024:2048].rearrange("p (a b) -> p a b", a=2)
        iota = R3[:, 3072:3072 + P]
        qr = GB1[:, :].rearrange("p (t h r) -> p t h r", t=NT, h=HEADS)
        qrT = GB2[:, :].rearrange("p (i s) -> p i s", i=4)
        tmp = R1[:, :].rearrange("p (i t h r) -> p i t h r", i=4, t=NT, h=HEADS)
        junk, junk3 = R1[:, 0:D], R3[:, 2048:2048 + D]

        def piece(ring, slots, u, i):
            k, n = shape_of(u)
            at, half = (u % slots) * UNIT, k * n // 2
            return ring[:, at + i * half:at + (i + 1) * half]

        def part(ring, u, kk, c0, n):
            at = (u % SPLIT) * UNIT + kk * shape_of(u)[1] + c0
            return ring[:, at:at + n]

        @block.sync
        def _(sp):
            def load(u, src):
                k, n = shape_of(u)
                at = (u % RAW) * UNIT
                if u >= RAW:
                    sp.wait_ge(lo_done, 2 * (u - RAW) + 2)
                sp.dma_start(raw[:, at:at + k * n].rearrange("p (k n) -> p k n", n=n),
                             src).then_inc(raw_full[u % RAW], 16)

            sp.dma_start(memt, mem[0].rearrange("(t p) d -> p t d", p=P)).then_inc(mem_in, 16)
            sp.dma_start(h[:, :, :], x[0].rearrange("(t p) d -> p t d", p=P)).then_inc(x_in, 16)
            for u in range(U_MOE):
                load(u, units[u][0])

            def expert_loads(e, ve):
                for j in range(MU):
                    u = U_MOE + j
                    k, n = moe_shape[j]
                    if j < 8:
                        w = (moe_w_gate, moe_w_up)[j // 2 % 2]
                        k0, c0 = 4 * (j % 2), ECH * (j // 4)
                    else:
                        w, k0, c0 = moe_w_down, 7 * ((j - 8) // 2), 512 * (j % 2)
                    src = w[0, bass.ds(e, 1), k0 * P:(k0 + k) * P, c0:c0 + n]
                    at = (u % RAW) * UNIT
                    sp.wait_ge(lo_done, ve * (2 * MU) + 2 * (u - RAW) + 2)
                    sp.dma_start(raw[:, at:at + k * n].rearrange("p (k n) -> p k n", n=n),
                                 src.rearrange("e (k p) n -> p (e k) n", p=P)
                                 ).then_inc(raw_full[u % RAW], 16)

            with sp.Fori(0, E) as e:
                expert_loads(e, e)
            sp.wait_ge(route_done, 1)
            rounds = sp.value_load(nround[0:1, 0:1], min_val=E, max_val=2 * E)
            with sp.If(rounds > E):
                with sp.Fori(0, E) as e:
                    expert_loads(e, e + E)
            sp.wait_ge(xn_done, 2 * 7)
            for t in range(NT):
                sp.dma_start(out[0, t * P:(t + 1) * P, :], xn[:, t]).then_inc(out_done, 16)
            sp.wait_ge(out_done, 16 * NT)

        @block.tensor
        def _(pe):
            def a_job(j):
                if j >= 2:
                    pe.wait_ge(a_free[j % 2], 2 * (j // 2))
                return A[j % 2]

            def t_job(j):
                if j >= 2:
                    pe.wait_ge(t_free[j % 2], 2 * (j // 2))
                return T[j % 2]

            def s_job(j):
                if j >= 2:
                    pe.wait_ge(s_free[j % 2], j // 2)
                return S[j % 2]

            def split_ready(u, kk, it=0):
                k, n = shape_of(u)
                half = k * n // 2
                if kk == 0:
                    pe.wait_ge(lo_done, it * (2 * MU) + 2 * u + 1)
                if kk * n <= half < (kk + 1) * n:
                    pe.wait_ge(lo_done, it * (2 * MU) + 2 * u + 2)

            def three(out, stat, mov, start, stop):
                nc.tensor.matmul(out, stat[0], mov[1], start=start, stop=False)
                nc.tensor.matmul(out, stat[1], mov[0], start=False, stop=False)
                return nc.tensor.matmul(out, stat[0], mov[0], start=False, stop=stop)

            def project(us, banks, acts, tiles=NT, it=0, k_of=None, c_out=0):
                blocks = [(u, kk) for u in us for kk in range(shape_of(u)[0])]
                for i, (u, kk) in enumerate(blocks):
                    n = shape_of(u)[1]
                    split_ready(u, kk, it)
                    for t in range(tiles):
                        stat = [a[:, i, t * P:(t + 1) * P] for a in acts]
                        last = three(banks[t][:, 0:n], stat, (part(hi, u, kk, 0, n), part(lo, u, kk, 0, n)),
                                     i == 0, i == len(blocks) - 1)
                    if kk == shape_of(u)[0] - 1:
                        last.then_inc(used, 1)

            def project_T(u, out, acts, c0, first=True):
                k = shape_of(u)[0]
                for kk in range(k):
                    if first:
                        split_ready(u, kk)
                    last = three(out, (part(hi, u, kk, c0, P), part(lo, u, kk, c0, P)),
                                 [a[:, kk, :] for a in acts], kk == 0, kk == k - 1)
                return last

            def heads_T(u, j, acts):
                bank = a_job(j)[0]
                for i in range(2):
                    last = project_T(u, bank[:, i * SEQ:(i + 1) * SEQ], acts, i * P, i == 0)
                last.then_inc(used, 1)

            def transposes(j, blocks):
                bank = t_job(j)
                for i, b in enumerate(blocks):
                    last = nc.tensor.transpose(bank[:, i * P:(i + 1) * P], b, ident[:, :])
                last.then_inc(t_done, 1)

            def transposed(*jobs):
                for j in jobs:
                    pe.wait_ge(t_free[j % 2], 2 * (j // 2 + 1))

            def tile_transposes(src, n_norm, j0):
                for t in range(NT):
                    pe.wait_ge(xn_done, 2 * n_norm + t + 1)
                    for b in range(2):
                        transposes(j0 + 2 * t + b, [src[:, t, (4 * b + i) * P:(4 * b + i + 1) * P]
                                                    for i in range(4)])

            def attention(groups, first, scores, values, t0, a0):
                def score(g):
                    t, hs, n = groups[g]
                    bank = s_job(first + g)
                    for i, hd in enumerate(hs):
                        last = scores(bank[:, i * n:(i + 1) * n], hd, t, n)
                    last.then_inc(s_done, 1)

                def output(g):
                    t, hs, n = groups[g]
                    transposed(t0 + g)
                    bank = a_job(a0 + g)[0]
                    nk = n // P
                    for i, hd in enumerate(hs):
                        for b in range(nk):
                            at = (i * nk + b) * P
                            last = nc.tensor.matmul(bank[:, i * P:(i + 1) * P],
                                                    values[:, b, hd * P:(hd + 1) * P],
                                                    PPT[:, g % 2, at:at + P],
                                                    start=b == 0, stop=b == nk - 1)
                    last.then_inc(o_done, 1)

                score(0)
                for g in range(len(groups)):
                    if g + 1 < len(groups):
                        score(g + 1)
                    pe.wait_ge(prob_done, first + g + 1)
                    transposes(t0 + g, [PP[:, g % 2, i * P:(i + 1) * P] for i in range(4)])
                    if g:
                        output(g - 1)
                output(len(groups) - 1)

            def mem_scores(out, hd, t, n):
                return nc.tensor.matmul(out, mq[:, hd, t * P:(t + 1) * P], mk[:, hd, :],
                                        start=True, stop=True)

            def lat_scores(out, hd, t, n):
                nc.tensor.matmul(out, qn[:, hd, t * P:(t + 1) * P], kn[:, hd, 0:n],
                                 start=True, stop=False)
                return nc.tensor.matmul(out, qrT[:, hd // 2, t * P:(t + 1) * P],
                                        krT[:, hd % 2, 0:n], start=False, stop=True)

            def memory_heads(layer, norm_mem, norm_x, ku, vu, qu, xsrc):
                tile_transposes(memt, norm_mem, T_MEM[layer])
                transposed(*range(T_MEM[layer] + 2, T_MEM[layer] + 4))
                for i in range(2):
                    heads_T(ku[i], A_K[layer][i], wkv)
                project(vu, a_job(A_V[layer]), wkv)
                tile_transposes(xsrc, norm_x, T_X[layer])
                transposed(*range(T_X[layer] + 2, T_X[layer] + 4))
                for i in range(2):
                    heads_T(qu[i], A_Q[layer][i], xTv)
                pe.wait_ge(a_free[A_V[layer] % 2], 2 * (A_V[layer] // 2 + 1))
                for j in A_Q[layer]:
                    pe.wait_ge(a_free[j % 2], 2 * (j // 2 + 1))
                attention(MEM_GROUPS, S_MEM[layer], mem_scores, mv, T_PM[layer], A_MO[layer])

            pe.wait_ge(consts, 1)
            pe.wait_ge(ws_in, 16)
            for i in range(2):
                transposes(T_WS + i, [wsr[:, 4 * i + g, :] for g in range(4)])
            memory_heads(0, 0, 1, U_K0, U_V0, U_Q0, xn)
            for i in range(2):
                project(U_GV[i], a_job(A_GV[i]), xTv)
            for i in range(2):
                project(U_GU[i], a_job(A_GU[i]), xTv)
            pe.wait_ge(vn_done, NT)
            for j in range(2):
                pair = a_job(A_MIX[j])
                for i in range(4):
                    g = 4 * j + i
                    last = nc.tensor.matmul(pair[i // 2][:, (i % 2) * SEQ:(i % 2 + 1) * SEQ], wsT[:, g, :],
                                            gv[:, :, g * P:(g + 1) * P], start=True, stop=True)
                last.then_inc(mixed_done, 1)
            for b in range(2):
                j = A_MIX[b]
                pe.wait_ge(a_free[j % 2], 2 * (j // 2 + 1))
                for t in range(NT):
                    transposes(T_U + 2 * b + t, [gu[:, t, (4 * b + i) * P:(4 * b + i + 1) * P]
                                                 for i in range(4)])

            def out_projection(layer, us, t_last):
                transposed(*t_last)
                j = A_OUT[layer][0] - 1
                pe.wait_ge(a_free[j % 2], 2 * (j // 2 + 1))
                for c in range(2):
                    project(us[c], a_job(A_OUT[layer][c]), xTv)

            out_projection(0, U_O0, (T_U + 2, T_U + 3))
            tile_transposes(xn, 2, T_FN[0])
            transposed(T_FN[0] + 2, T_FN[0] + 3)
            for hf in range(2):
                gu_units, down_units = U_FF[hf]
                j0, tj = A_FF[hf], T_FH[hf]

                def hidden_T(i, b0, nb, chunks, t0=0):
                    j = j0 + 2 * chunks - 1
                    pe.wait_ge(a_free[j % 2], 2 * (j // 2 + 1))
                    for t in range(NT):
                        transposes(tj + 2 * i + t, [fhid[:, t, (b0 + b) * P:(b0 + b + 1) * P]
                                                    for b in range(nb)])

                for c in range(4):
                    project([gu_units[c][0]], a_job(j0 + 2 * c), xTv)
                    if c == 2:
                        hidden_T(0, 0, 4, 2)
                    if c == 3:
                        hidden_T(1, 4, 4, 3)
                    project([gu_units[c][1]], a_job(j0 + 2 * c + 1), xTv)
                for c in range(4):
                    u, pair = down_units[c], a_job(j0 + 8 + c)
                    if c == 0:
                        transposed(tj, tj + 1, tj + 2, tj + 3)
                    for kk in range(FB):
                        if c == 0 and kk == 8:
                            hidden_T(2, 8, 3, 4)
                            transposed(tj + 4, tj + 5)
                        split_ready(u, kk)
                        for t in range(NT):
                            last = three(pair[t][:, 0:256], [a[:, kk, t * P:(t + 1) * P] for a in wkv],
                                         (part(hi, u, kk, 0, 256), part(lo, u, kk, 0, 256)),
                                         kk == 0, kk == FB - 1)
                    last.then_inc(used, 1)

            memory_heads(1, 3, 4, U_K1, U_V1, U_Q1, xn)
            for i in range(2):
                project(U_C[i], a_job(A_C[i]), xTv)
            project([U_KR], a_job(A_KR), xTv)
            for t in range(NT):
                pe.wait_ge(c_ready, t + 1)
                for b in range(2):
                    transposes(T_C + 2 * t + b, [lat[:, t, (4 * b + i) * P:(4 * b + i + 1) * P]
                                                 for i in range(4)])
            transposed(T_C + 2, T_C + 3)
            for i in range(4):
                u, pair = U_UQ[i], a_job(A_UQ + i)
                for hh in range(2):
                    project_T(u, pair[0][:, hh * SEQ:(hh + 1) * SEQ], wkv, hh * QK, hh == 0)
                for t in range(NT):
                    for kk in range(QL // P):
                        at = (u % SPLIT) * UNIT + kk * 2 * QK
                        mov = [r[:, at:at + 2 * QK].rearrange("p (h c) -> p h c", h=2)[:, :, NOPE:QK]
                               for r in (hi, lo)]
                        last = three(pair[1][:, t * P:(t + 1) * P],
                                     [a[:, kk, t * P:(t + 1) * P] for a in wkv], mov,
                                     kk == 0, kk == QL // P - 1)
                last.then_inc(used, 1)
            kvT = [a[:, QL // P:, :] for a in wkv]
            for i in range(2):
                u, pair = U_UKV[i], a_job(A_UKV + 2 * i)
                for hh in range(4):
                    project_T(u, pair[hh // 2][:, (hh % 2) * SEQ:(hh % 2 + 1) * SEQ], kvT, hh * 256, hh == 0)
                pair = a_job(A_UKV + 2 * i + 1)
                for t in range(NT):
                    for kk in range(2):
                        at = (u % SPLIT) * UNIT + kk * 1024
                        mov = [r[:, at:at + 1024].rearrange("p (h c) -> p h c", h=4)[:, :, P:256]
                               for r in (hi, lo)]
                        last = three(pair[t][:, :], [a[:, kk, t * P:(t + 1) * P] for a in kvT], mov,
                                     kk == 0, kk == 1)
                last.then_inc(used, 1)
            pe.wait_ge(rope_done, 1)
            for t in range(NT):
                transposes(T_ROPE + t, [qr[:, t, 2 * i:2 * i + 2, :] for i in range(4)])
            transposes(T_ROPE + 2, [kr[:, b, t, :] for b in range(2) for t in range(NT)])
            transposed(T_ROPE + 1, T_ROPE + 2)
            for j in (A_UKV + 2, A_UKV + 3):
                pe.wait_ge(a_free[j % 2], 2 * (j // 2 + 1))
            attention(LAT_GROUPS, S_LAT, lat_scores, lv, T_PL, A_LO)
            out_projection(1, U_O1, ())
            tile_transposes(xn, 5, T_FN[1])
            transposed(T_FN[1] + 2, T_FN[1] + 3)
            pair = a_job(A_RT)
            pe.wait_ge(rout_in, 32)
            for t in range(NT):
                for kk in range(KD):
                    last = nc.tensor.matmul(pair[t][:, 0:E], xnT[:, kk, t * P:(t + 1) * P], wr[:, kk, :],
                                            start=kk == 0, stop=kk == KD - 1)
            last.then_inc(route_mm, 1)
            pair = a_job(A_RT + 1)
            pe.wait_ge(mask_done, 1)
            mask = rt[:, 0]
            nc.tensor.matmul(pair[0][:, 0:E], tris[:, :], mask[:, 0, :], start=True, stop=True)
            nc.tensor.matmul(pair[1][:, 0:E], ones[:, :], mask[:, 0, :], start=True, stop=False)
            nc.tensor.matmul(pair[1][:, 0:E], tris[:, :], mask[:, 1, :], start=False, stop=True)
            nc.tensor.matmul(pair[0][:, E:2 * E], ones[:, :], mask[:, 0, :], start=True, stop=False)
            nc.tensor.matmul(pair[0][:, E:2 * E], ones[:, :], mask[:, 1, :], start=False,
                             stop=True).then_inc(route_mm, 1)

            def gather(tj, it):
                for b in range(2):
                    pe.wait_ge(t_free[(tj + b) % 2], it * 8 + 2 * ((tj + b) // 2))
                    bank = T[(tj + b) % 2]
                    for i in range(4):
                        d = 4 * b + i
                        n = 0
                        for src in (xs[1], xs[0]):
                            for t in range(NT):
                                last = nc.tensor.matmul(bank[:, i * P:(i + 1) * P],
                                                        src[:, t, d * P:(d + 1) * P],
                                                        sel[:, t * P:(t + 1) * P], start=n == 0, stop=n == 3)
                                n += 1
                    last.then_inc(t_done, 1)

            pe.wait_ge(xs_done, NT)
            pe.wait_ge(sel_done, 1)
            gather(T_MOE, 0)
            pe.wait_ge(moe_const, 1)
            for c in range(2):
                pe.wait_ge(s_free[(S_MOE + c) % 2], (S_MOE + c) // 2)
                last = nc.tensor.matmul(S[(S_MOE + c) % 2][:, :], selT[:, 0:P], ys[0][:, c * 512:(c + 1) * 512],
                                        start=True, stop=True)
            last.then_inc(scat_done, 1)

            def scatter(t, ve):
                for c in range(2):
                    s = S_MOE + 2 + 2 * t + c
                    pe.wait_ge(s_free[s % 2], ve * 3 + s // 2)
                    for n in range(2):
                        last = nc.tensor.matmul(S[s % 2][:, :], selT[:, t * P:(t + 1) * P],
                                                ys[1 - n][:, c * 512:(c + 1) * 512],
                                                start=n == 0, stop=n == 1)
                    last.then_inc(scat_done, 1)

            def hidden_expert(ve, units4, j, before_second):
                pe.wait_ge(a_free[j % 2], ve * 4 + 2 * (j // 2))
                for n, u in enumerate(units4):
                    if n:
                        before_second()
                    for kk in range(4):
                        split_ready(u, kk, ve)
                        k = 4 * n + kk
                        stat = [a[:, k * P:(k + 1) * P] for a in xg]
                        for b in range(2):
                            mov = (part(hi, u, kk, b * EN, EN), part(lo, u, kk, b * EN, EN))
                            last = three(A[j % 2][b][:, 0:EN], stat, mov, k == 0, k == 7)
                    last.then_inc(used, 1)

            def hidden_T_expert(ve, c, tj):
                j = A_MOE + 2 * c + 1
                pe.wait_ge(a_free[j % 2], ve * 4 + 2 * (j // 2 + 1))
                for n, nb_ in enumerate((4, 3)):
                    j = tj + n
                    pe.wait_ge(t_free[j % 2], ve * 8 + 2 * (j // 2))
                    for b in range(nb_):
                        at = (4 * n + b) * P
                        last = nc.tensor.transpose(T[j % 2][:, b * P:(b + 1) * P], ehid[:, at:at + P],
                                                   ident[:, :])
                    last.then_inc(t_done, 1)

            def down(ve, u, c, half):
                bank = S[(S_MOE + 6 + c) % 2]
                if half == 0:
                    s = S_MOE + 6 + c
                    pe.wait_ge(s_free[s % 2], ve * 3 + s // 2)
                for kk in range(7):
                    split_ready(u, kk, ve)
                    k = 7 * half + kk
                    last = three(bank[:, :], [a[:, k * P:(k + 1) * P] for a in hT],
                                 (part(hi, u, kk, 0, 512), part(lo, u, kk, 0, 512)), k == 0, k == EB - 1)
                last.then_inc(used, 1)

            def nothing():
                pass

            pe.wait_ge(route_done, 1)
            rounds = pe.value_load(nround[0:1, 0:1], min_val=E, max_val=2 * E)
            t1 = T_MOE + 2
            with pe.Fori(0, rounds) as ve:
                U = U_MOE
                for b in range(2):
                    pe.wait_ge(t_free[(T_MOE + b) % 2], ve * 8 + 2 * ((T_MOE + b) // 2 + 1))
                hidden_expert(ve, (U, U + 1), A_MOE, nothing)
                scatter(0, ve)

                def second_scatter():
                    scatter(1, ve)
                    for t in range(NT):
                        j = t1 + t
                        pe.wait_ge(t_free[j % 2], ve * 8 + 2 * (j // 2))
                        nc.tensor.transpose(T[j % 2][:, 0:P], sel[:, t * P:(t + 1) * P].bitcast(F32),
                                            ident[:, :]).then_inc(t_done, 1)

                hidden_expert(ve, (U + 2, U + 3), A_MOE + 1, second_scatter)
                hidden_expert(ve, (U + 4, U + 5), A_MOE + 2, nothing)
                hidden_T_expert(ve, 0, t1 + 2)
                hidden_expert(ve, (U + 6, U + 7), A_MOE + 3, nothing)
                for j in (t1 + 2, t1 + 3):
                    pe.wait_ge(t_free[j % 2], ve * 8 + 2 * (j // 2 + 1))
                down(ve, U + 8, 0, 0)
                hidden_T_expert(ve, 1, t1 + 4)
                down(ve, U + 9, 1, 0)
                for j in (t1 + 4, t1 + 5):
                    pe.wait_ge(t_free[j % 2], ve * 8 + 2 * (j // 2 + 1))
                down(ve, U + 10, 0, 1)
                pe.wait_ge(sel_done, ve + 2)
                gather(t1 + 6, ve)
                down(ve, U + 11, 1, 1)
            scatter(0, rounds)
            scatter(1, rounds)

        @block.scalar
        def _(act):
            def act_copy(out, in_):
                return nc.scalar.activation(out, in_, ACT.Copy)

            def split(u, it=0):
                act.wait_ge(raw_full[u % RAW], it * (16 * MU // RAW) + 16 * (u // RAW + 1))
                if u >= SPLIT:
                    act.wait_ge(used, it * MU + u - SPLIT + 1)
                for i in range(2):
                    act_copy(piece(hi, SPLIT, u, i), piece(raw, RAW, u, i)).then_inc(hi_done, 1)

            def square_sums(n, src, n_cols=D, c0=0, scratch=junk):
                for t in range(NT):
                    if n or t:
                        act.wait_ge(ssum_done, 2 * n + t)
                    nc.scalar.activation(scratch[:, 0:n_cols], src[:, t, c0:c0 + n_cols], ACT.Square,
                                         accum_out=ssum[:, n, t:t + 1]).then_inc(ssum_done, 1)

            def t_bank(j, n=4):
                act.wait_ge(t_done, j + 1)
                return T[j % 2][:, 0:n * P].rearrange("p (k s) -> p k s", k=n)

            def t_hi(j, out, n=4):
                act_copy(out, t_bank(j, n)).then_inc(t_free[j % 2], 1)

            def tiles_hi(j0, acts):
                for t in range(NT):
                    for b in range(2):
                        t_hi(j0 + 2 * t + b, acts[0][:, 4 * b:4 * b + 4, t * P:(t + 1) * P])

            def two_heads(u, j, out):
                act.wait_ge(used, u + 1)
                act_copy(out, A[j % 2][0][:, :].rearrange("p (h s) -> p h s", h=2)
                         ).then_inc(a_free[j % 2], 2)

            def attention(groups, first, scale, t0, a0, cat0):
                def exps(g):
                    t, hs, n = groups[g]
                    gg = first + g
                    act.wait_ge(max_done, gg + 1)
                    if g >= 2:
                        act.wait_ge(t_done, t0 + g - 1)
                    for i in range(len(hs)):
                        last = nc.scalar.activation(PP[:, g % 2, i * n:(i + 1) * n],
                                                    S[gg % 2][:, i * n:(i + 1) * n], ACT.Exp,
                                                    bias=nb[:, gg, i:i + 1], scale=scale,
                                                    accum_out=den[:, gg, i:i + 1])
                    last.then_inc(s_free[gg % 2], 1)

                def out_hi(g):
                    t, hs, _ = groups[g]
                    j = a0 + g
                    act.wait_ge(o_done, first + g + 1)
                    act_copy(xTv[0][:, cat0 + hs[0]:cat0 + hs[0] + len(hs), t * P:(t + 1) * P],
                             A[j % 2][0][:, 0:len(hs) * P].rearrange("p (h s) -> p h s", h=len(hs))
                             ).then_inc(a_free[j % 2], 1)

                exps(0)
                for g in range(len(groups)):
                    if g + 1 < len(groups):
                        exps(g + 1)
                    bank = t_bank(t0 + g)
                    if g >= 2:
                        act.wait_ge(o_done, first + g - 1)
                    act_copy(PPT[:, g % 2, :].rearrange("p (k s) -> p k s", k=4), bank
                             ).then_inc(t_free[(t0 + g) % 2], 2)
                    if g:
                        out_hi(g - 1)
                out_hi(len(groups) - 1)

            def memory_heads(layer, ku, vu, qu):
                tiles_hi(T_MEM[layer], wkv)
                for i in range(2):
                    two_heads(ku[i], A_K[layer][i], mk[:, 2 * i:2 * i + 2, :])
                    split(ku[i] + 2)
                split(vu[0] + 2)
                split(vu[1] + 2)
                j = A_V[layer]
                act.wait_ge(used, vu[1] + 1)
                act_copy(mv[:, 0, :], A[j % 2][0][:, :]).then_inc(a_free[j % 2], 1)
                tiles_hi(T_X[layer], xTv)
                for i in range(2):
                    two_heads(qu[i], A_Q[layer][i], mq[:, 2 * i:2 * i + 2, :])
                    split(qu[i] + 2)
                attention(MEM_GROUPS, S_MEM[layer], MEM_SCALE, T_PM[layer], A_MO[layer], KD)

            act.dma_start(wsr, gm_w_s[0].rearrange("g t s -> t g s")).then_inc(ws_in, 16)
            act.dma_start(gbs[:, :], gm_b_s[0].rearrange("g t -> t g"),
                          allow_slow_non_contiguous=True).then_inc(gbs_in, 16)
            act.dma_start(posi[:, :], positions.rearrange("a (t p) -> p (a t)", p=P),
                          allow_slow_non_contiguous=True).then_inc(rope_in, 16)
            act.dma_start(freq[:, :], rope_freq.partition_broadcast(P)).then_inc(rope_in, 16)
            act.dma_start(wr[:, :, :], moe_w_router[0].rearrange("(k p) e -> p k e", p=P)).then_inc(rout_in, 16)
            act.dma_start(br[:, :], moe_b_router[0].partition_broadcast(P)).then_inc(rout_in, 16)
            act.wait_ge(mem_in, 16)
            square_sums(0, memt)
            act.wait_ge(x_in, 16)
            square_sums(1, h)
            split(0)
            split(1)
            memory_heads(0, U_K0, U_V0, U_Q0)
            for us, jobs, dst in ((U_GV, A_GV, gv), (U_GU, A_GU, gu)):
                for i in range(2):
                    split(us[i][0] + 2)
                    act.wait_ge(used, us[i][1] + 1)
                    j = jobs[i]
                    for t in range(NT):
                        nc.scalar.activation(dst[:, t, i * 512:(i + 1) * 512], A[j % 2][t][:, :],
                                             ACT.Gelu).then_inc(a_free[j % 2], 1)
                    split(us[i][1] + 2)
            for b in range(2):
                for t in range(NT):
                    t_hi(T_U + 2 * b + t, xTv[0][:, 4 * b:4 * b + 4, t * P:(t + 1) * P])
            act.wait_ge(rope_ang, 1)
            nc.scalar.activation(cs[:, :, :, :], cs[:, :, :, :], ACT.Sin).then_inc(rope_cs, 1)

            def residual_in(j0):
                for j in (j0, j0 + 1):
                    act.wait_ge(a_free[j % 2], 2 * (j // 2 + 1))

            for c in range(2):
                for u in U_O0[c]:
                    split(u + 2)
            residual_in(A_OUT[0][0])
            square_sums(2, h)
            tiles_hi(T_FN[0], xTv)
            for hf in range(2):
                gu_units, down_units = U_FF[hf]
                j0, tj = A_FF[hf], T_FH[hf]

                def hidden_hi(i, b0, n):
                    for t in range(NT):
                        t_hi(tj + 2 * i + t, wkv[0][:, b0:b0 + n, t * P:(t + 1) * P], n)

                for c in range(4):
                    g, u = gu_units[c]
                    act.wait_ge(used, g + 1)
                    if c or hf:
                        j = j0 + 2 * c - 1 if c else A_FF[0] + 7
                        act.wait_ge(a_free[j % 2], 2 * (j // 2 + 1))
                    j = j0 + 2 * c
                    for t in range(NT):
                        nc.scalar.activation(fsilu[:, t, :], A[j % 2][t][:, 0:FCH], ACT.Silu
                                             ).then_inc(a_free[j % 2], 1)
                    if c >= 2:
                        hidden_hi(c - 2, 4 * (c - 2), 4)
                    split(g + 2)
                    split(u + 2)
                hidden_hi(2, 8, 3)
                for c in range(4):
                    split(down_units[c] + 2)
                    if hf == 1 and c == 0:
                        act.wait_ge(mem2_in, 16)
                        square_sums(3, memt)
            residual_in(A_FF[1] + 10)
            for j in (A_FF[1] + 8, A_FF[1] + 9):
                act.wait_ge(a_free[j % 2], 2 * (j // 2 + 1))
            square_sums(4, h)
            memory_heads(1, U_K1, U_V1, U_Q1)
            for i in range(2):
                split(U_C[i][0] + 2)
                act.wait_ge(used, U_C[i][1] + 1)
                j = A_C[i]
                act_copy(lat[:, 0, i * 512:(i + 1) * 512], A[j % 2][0][:, :]).then_inc(a_free[j % 2], 1)
                split(U_C[i][1] + 2)
            for j in A_C:
                act.wait_ge(a_free[j % 2], 2 * (j // 2 + 1))
            square_sums(5, lat, QL, 0, junk3)
            square_sums(6, lat, KVL, QL, junk3)
            split(U_KR + 2)
            tiles_hi(T_C, wkv)
            for i in range(4):
                u, j = U_UQ[i], A_UQ + i
                act.wait_ge(used, u + 1)
                act_copy(qn[:, 2 * i:2 * i + 2, :], A[j % 2][0][:, :].rearrange("p (h s) -> p h s", h=2)
                         ).then_inc(a_free[j % 2], 1)
                split(u + 2)
            act.wait_ge(o_done, 8)
            for i in range(2):
                u, j = U_UKV[i], A_UKV + 2 * i
                act.wait_ge(used, u + 1)
                act_copy(kn[:, 4 * i:4 * i + 2, :], A[j % 2][0][:, :].rearrange("p (h s) -> p h s", h=2)
                         ).then_inc(a_free[j % 2], 1)
                j += 1
                act_copy(lv[:, 0, i * 512:(i + 1) * 512], A[j % 2][0][:, :]).then_inc(a_free[j % 2], 1)
                split(u + 2)
            for t in range(NT):
                act_copy(qrT[:, :, t * P:(t + 1) * P], t_bank(T_ROPE + t)
                         ).then_inc(t_free[(T_ROPE + t) % 2], 2)
            j = T_ROPE + 2
            act.wait_ge(t_done, j + 1)
            act_copy(krT[:, :, :].rearrange("p b s -> p (b s)"), T[j % 2][:, :]).then_inc(t_free[j % 2], 2)
            attention(LAT_GROUPS, S_LAT, MLA_SCALE, T_PL, A_LO, 0)
            for c in range(2):
                for u in U_O1[c]:
                    if u + 2 < U_MOE:
                        split(u + 2)
            residual_in(A_OUT[1][0])
            square_sums(7, h)
            for t in range(NT):
                for b in range(2):
                    j = T_FN[1] + 2 * t + b
                    act_copy(xnT[:, 4 * b:4 * b + 4, t * P:(t + 1) * P], t_bank(j)
                             ).then_inc(t_free[j % 2], 2)
            for t in range(NT):
                act_copy(xs[0][:, t, :], xn[:, t, :]).then_inc(xs_hi, 1)
            act.wait_ge(rt_exp_in, 1)
            nc.scalar.activation(r1[:, 3, :], r1[:, 2, :], ACT.Exp).then_inc(rt_exp, 1)

            def gathered_hi(tj, it):
                for b in range(2):
                    j = tj + b
                    act.wait_ge(t_done, it * 8 + j + 1)
                    act_copy(xg[0][:, b * 512:(b + 1) * 512], T[j % 2][:, :]).then_inc(t_free[j % 2], 1)

            def output_hi(c, it):
                act.wait_ge(used, it * MU + U_MOE - 1 + c)
                act.wait_ge(scat_done, 1)
                act_copy(ys[0][:, c * 512:(c + 1) * 512], S[(S_MOE + c) % 2][:, :]).then_inc(y_hi, 1)

            def silu(c, ve):
                act.wait_ge(used, ve * MU + U_MOE + 4 * c + 2)
                j = A_MOE + 2 * c - 1
                act.wait_ge(a_free[j % 2], ve * 4 + 2 * (j // 2 + 1))
                j = A_MOE + 2 * c
                for b in range(2):
                    nc.scalar.activation(esilu[:, b * EN:(b + 1) * EN], A[j % 2][b][:, 0:EN], ACT.Silu
                                         ).then_inc(a_free[j % 2], 1)

            def hidden_hi(c, tj, ve):
                for n, blocks in enumerate((4, 3)):
                    j, at = tj + n, (7 * c + 4 * n) * P
                    act.wait_ge(t_done, ve * 8 + j + 1)
                    act_copy(hT[0][:, at:at + blocks * P], T[j % 2][:, 0:blocks * P]
                             ).then_inc(t_free[j % 2], 1)

            gathered_hi(T_MOE, 0)
            act.wait_ge(route_done, 1)
            rounds = act.value_load(nround[0:1, 0:1], min_val=E, max_val=2 * E)
            U, t1 = U_MOE, T_MOE + 2
            with act.Fori(0, rounds) as ve:
                split(U, ve)
                output_hi(0, ve)
                split(U + 1, ve)
                output_hi(1, ve)
                split(U + 2, ve)
                split(U + 3, ve)
                silu(0, ve)
                split(U + 4, ve)
                for t in range(NT):
                    j = t1 + t
                    act.wait_ge(t_done, ve * 8 + j + 1)
                    act_copy(selT[:, t * P:(t + 1) * P], T[j % 2][:, 0:P]).then_inc(t_free[j % 2], 2)
                split(U + 5, ve)
                split(U + 6, ve)
                split(U + 7, ve)
                silu(1, ve)
                hidden_hi(0, t1 + 2, ve)
                split(U + 8, ve)
                split(U + 9, ve)
                hidden_hi(1, t1 + 4, ve)
                split(U + 10, ve)
                split(U + 11, ve)
                gathered_hi(t1 + 6, ve)
            output_hi(0, rounds)
            output_hi(1, rounds)
            for c in range(2):
                act.wait_ge(s_free[(S_MOE + 4 + c) % 2], rounds * 3 + (S_MOE + 4 + c) // 2 + 1)
            square_sums(8, h)

        @block.vector
        def _(dve):
            steps = [0]

            def step(ins):
                steps[0] += 1
                ins.then_inc(dve_step, 1)
                dve.wait_ge(dve_step, steps[0])

            def split(u, it=0):
                for i in range(2):
                    dve.wait_ge(hi_done, it * (2 * MU) + 2 * u + i + 1)
                    nc.vector.tensor_tensor(piece(lo, SPLIT, u, i), piece(raw, RAW, u, i),
                                            piece(hi, SPLIT, u, i).bitcast(F32), ALU.subtract
                                            ).then_inc(lo_done, 1)

            def normalise(n, src, dst, gain):
                dve.wait_ge(rstd_done, n + 1)
                for t in range(NT):
                    nc.vector.scalar_tensor_tensor(dst[:, t, :], src[:, t, :], rstd[:, n, t:t + 1],
                                                   gain[:, :], ALU.mult, ALU.mult).then_inc(xn_done, 1)

            def t_lo(j, out, hi_part, n=4):
                dve.wait_ge(t_free[j % 2], 2 * (j // 2) + 1)
                nc.vector.tensor_tensor(out, T[j % 2][:, 0:n * P].rearrange("p (k s) -> p k s", k=n),
                                        hi_part.bitcast(F32), ALU.subtract).then_inc(t_free[j % 2], 1)

            def tiles_lo(j0, acts):
                for t in range(NT):
                    for b in range(2):
                        hi_part, lo_part = [a[:, 4 * b:4 * b + 4, t * P:(t + 1) * P] for a in acts]
                        t_lo(j0 + 2 * t + b, lo_part, hi_part)

            def attention(groups, first, scale, t0, a0, cat0, causal):
                def maxima(g):
                    t, hs, n = groups[g]
                    gg = first + g
                    bank = S[gg % 2][:, :].rearrange("p (h s) -> p h s", h=len(hs))
                    dve.wait_ge(s_done, gg + 1)
                    if causal:
                        own = bank[:, :, n - P:n]
                        step(nc.vector.tensor_tensor(own, own, cmask[:, :].unsqueeze(1).to_broadcast(
                            [P, len(hs), P]), ALU.add))
                    step(nc.vector.tensor_reduce(mx[:, gg, 0:len(hs)], bank, AX.X, ALU.max, negate=True))
                    nc.vector.tensor_scalar(nb[:, gg, 0:len(hs)], mx[:, gg, 0:len(hs)], scale, None,
                                            ALU.mult).then_inc(max_done, 1)

                def probabilities(g):
                    t, hs, n = groups[g]
                    gg = first + g
                    dve.wait_ge(s_free[gg % 2], gg // 2 + 1)
                    step(nc.vector.reciprocal(rden[:, gg, 0:len(hs)], den[:, gg, 0:len(hs)]))
                    p = PP[:, g % 2, :].rearrange("p (h s) -> p h s", h=len(hs))
                    nc.vector.tensor_tensor(p, p, rden[:, gg, 0:len(hs)].unsqueeze(2).to_broadcast(
                        [P, len(hs), n]), ALU.mult).then_inc(prob_done, 1)

                def out_lo(g):
                    t, hs, _ = groups[g]
                    j = a0 + g
                    blocks = slice(cat0 + hs[0], cat0 + hs[0] + len(hs))
                    dve.wait_ge(a_free[j % 2], 2 * (j // 2) + 1)
                    nc.vector.tensor_tensor(xTv[1][:, blocks, t * P:(t + 1) * P],
                                            A[j % 2][0][:, 0:len(hs) * P].rearrange(
                                                "p (h s) -> p h s", h=len(hs)),
                                            xTv[0][:, blocks, t * P:(t + 1) * P].bitcast(F32),
                                            ALU.subtract).then_inc(a_free[j % 2], 1)

                maxima(0)
                for g in range(len(groups)):
                    if g + 1 < len(groups):
                        maxima(g + 1)
                    probabilities(g)
                    if g:
                        out_lo(g - 1)
                out_lo(len(groups) - 1)

            def memory_heads(layer, ku, vu, qu, before_x):
                tiles_lo(T_MEM[layer], wkv)
                before_x()
                for u in ku + vu:
                    split(u + 2)
                j = A_V[layer]
                dve.wait_ge(used, vu[1] + 1)
                nc.vector.tensor_copy(mv[:, 1, :], A[j % 2][1][:, :]).then_inc(a_free[j % 2], 1)
                tiles_lo(T_X[layer], xTv)
                for u in qu:
                    split(u + 2)
                attention(MEM_GROUPS, S_MEM[layer], MEM_SCALE, T_PM[layer], A_MO[layer], KD, False)

            def add_residual(j, c0, n, u):
                dve.wait_ge(used, u + 1)
                for t in range(NT):
                    nc.vector.tensor_tensor(h[:, t, c0:c0 + n], A[j % 2][t][:, 0:n], h[:, t, c0:c0 + n],
                                            ALU.add).then_inc(a_free[j % 2], 1)

            dve.wait_ge(gb1_in, 16)
            dve.wait_ge(mem_in, 16)
            normalise(0, memt, memt, GB1)
            split(0)
            dve.wait_ge(consts, 1)
            for i in range(2):
                j = T_WS + i
                dve.wait_ge(t_done, j + 1)
                nc.vector.tensor_tensor(wsT[:, 4 * i:4 * i + 4, :],
                                        T[j % 2][:, :].rearrange("p (k s) -> p k s", k=4),
                                        tri[:, :].unsqueeze(1).to_broadcast([P, 4, P]), ALU.mult
                                        ).then_inc(t_free[j % 2], 2)
            split(1)

            def x_norm():
                dve.wait_ge(gb2_in, 16)
                dve.wait_ge(x_in, 16)
                normalise(1, h, xn, GB2)

            memory_heads(0, U_K0, U_V0, U_Q0, x_norm)
            for i in range(2):
                split(U_GV[i][0] + 2)
                split(U_GV[i][1] + 2)
            for j in A_GV:
                dve.wait_ge(a_free[j % 2], 2 * (j // 2 + 1))
            for t in range(NT):
                step(nc.vector.tensor_tensor(junk3, gv[:, t, :], gv[:, t, :], ALU.mult))
                red = nc.vector.tensor_reduce(vss[:, t, :], junk3.rearrange("p (g c) -> p g c", g=NG),
                                              AX.X, ALU.add)
                if t == 0:
                    step(red)
                else:
                    red.then_inc(vss_done, 1)
            split(U_GU[0][0] + 2)
            split(U_GU[0][1] + 2)
            dve.wait_ge(vrs_done, 1)
            dve.wait_ge(gb1_in, 32)
            for t in range(NT):
                v = gv[:, t, :].rearrange("p (g c) -> p g c", g=NG)
                step(nc.vector.tensor_tensor(v, v, vrs[:, t, :].unsqueeze(2).to_broadcast([P, NG, P]),
                                             ALU.mult))
                nc.vector.tensor_tensor(gv[:, t, :], gv[:, t, :], GB1[:, :], ALU.mult).then_inc(vn_done, 1)
            split(U_GU[1][0] + 2)
            split(U_GU[1][1] + 2)
            dve.wait_ge(gbs_in, 16)
            for j in A_GU:
                dve.wait_ge(a_free[j % 2], 2 * (j // 2 + 1))
            for jj in range(2):
                j = A_MIX[jj]
                dve.wait_ge(mixed_done, jj + 1)
                for i in range(4):
                    g = 4 * jj + i
                    u_g = gu[:, :, g * P:(g + 1) * P]
                    mixed = A[j % 2][i // 2][:, (i % 2) * SEQ:(i % 2 + 1) * SEQ]
                    last = nc.vector.scalar_tensor_tensor(u_g, mixed.rearrange("p (t c) -> p t c", t=NT),
                                                          gbs[:, g:g + 1], u_g, ALU.add, ALU.mult)
                last.then_inc(a_free[j % 2], 2)
            for b in range(2):
                for t in range(NT):
                    hi_part, lo_part = [a[:, 4 * b:4 * b + 4, t * P:(t + 1) * P] for a in xTv]
                    t_lo(T_U + 2 * b + t, lo_part, hi_part)
            dve.wait_ge(rope_in, 32)
            step(nc.vector.tensor_copy(posf[:, :], posi[:, :]))
            ang, turns = rt[:, 0:4].rearrange("p i t e -> p (i t e)"), rt[:, 4:8].rearrange(
                "p i t e -> p (i t e)")
            for t in range(NT):
                step(nc.vector.tensor_scalar(ang[:, t * 32:(t + 1) * 32], freq[:, :], posf[:, t:t + 1],
                                             None, ALU.mult))
            for i, quarter in enumerate((np.pi / 2, 0.0)):
                step(nc.vector.tensor_scalar(turns, ang, float(quarter), float(1 / TWO_PI), ALU.add, ALU.mult))
                step(nc.vector.tensor_scalar(turns, turns, MAGIC, None, ALU.add))
                step(nc.vector.tensor_scalar(turns, turns, -MAGIC, None, ALU.add))
                csv = cs[:, i].rearrange("p t r -> p (t r)")
                src = ang
                for c in two_pi_parts():
                    step(nc.vector.scalar_tensor_tensor(csv, turns, -c, src, ALU.mult, ALU.add))
                    src = csv
                step(nc.vector.tensor_scalar(csv, csv, float(quarter), 3.1415925, ALU.add, ALU.min))
                last = nc.vector.tensor_scalar(csv, csv, -3.1415925, None, ALU.max)
                if i == 0:
                    step(last)
            last.then_inc(rope_ang, 1)
            for c in range(2):
                split(U_O0[c][0] + 2)
                add_residual(A_OUT[0][c], c * 512, 512, U_O0[c][1])
                split(U_O0[c][1] + 2)
            dve.wait_ge(gb2_in, 32)
            normalise(2, h, xn, GB2)
            tiles_lo(T_FN[0], xTv)
            for hf in range(2):
                gu_units, down_units = U_FF[hf]
                j0, tj = A_FF[hf], T_FH[hf]

                def hidden_lo(i, b0, n):
                    for t in range(NT):
                        hi_part, lo_part = [a[:, b0:b0 + n, t * P:(t + 1) * P] for a in wkv]
                        t_lo(tj + 2 * i + t, lo_part, hi_part, n)

                for c in range(4):
                    g, u = gu_units[c]
                    if c >= 2:
                        hidden_lo(c - 2, 4 * (c - 2), 4)
                    split(g + 2)
                    dve.wait_ge(used, u + 1)
                    jg, ju = j0 + 2 * c, j0 + 2 * c + 1
                    dve.wait_ge(a_free[jg % 2], 2 * (jg // 2 + 1))
                    for t in range(NT):
                        nc.vector.tensor_tensor(fhid[:, t, c * FCH:(c + 1) * FCH], A[ju % 2][t][:, 0:FCH],
                                                fsilu[:, t, :], ALU.mult).then_inc(a_free[ju % 2], 1)
                    split(u + 2)
                hidden_lo(2, 8, 3)
                for c in range(4):
                    add_residual(j0 + 8 + c, c * 256, 256, down_units[c])
                    split(down_units[c] + 2)
                    if hf == 1 and c == 1:
                        dve.wait_ge(gb1_in, 48)
                        dve.wait_ge(mem2_in, 16)
                        normalise(3, memt, memt, GB1)

            def h_norm():
                dve.wait_ge(gb2_in, 48)
                normalise(4, h, xn, GB2)

            memory_heads(1, U_K1, U_V1, U_Q1, h_norm)
            for i in range(2):
                split(U_C[i][0] + 2)
                dve.wait_ge(used, U_C[i][1] + 1)
                j = A_C[i]
                nc.vector.tensor_copy(lat[:, 1, i * 512:(i + 1) * 512], A[j % 2][1][:, :]
                                      ).then_inc(a_free[j % 2], 1)
                split(U_C[i][1] + 2)
            dve.wait_ge(used, U_KR + 1)
            for t in range(NT):
                nc.vector.tensor_copy(kraw[:, t, :], A[A_KR % 2][t][:, 0:ROPE]
                                      ).then_inc(a_free[A_KR % 2], 1)
            dve.wait_ge(rstd_done, 7)
            dve.wait_ge(gb1_in, 80)
            for t in range(NT):
                for n, c0, c1 in ((5, 0, QL), (6, QL, D)):
                    last = nc.vector.scalar_tensor_tensor(lat[:, t, c0:c1], lat[:, t, c0:c1],
                                                          rstd[:, n, t:t + 1], GB1[:, c0:c1],
                                                          ALU.mult, ALU.mult)
                last.then_inc(c_ready, 1)
            split(U_KR + 2)
            tiles_lo(T_C, wkv)
            for i in range(4):
                u, j = U_UQ[i], A_UQ + i
                dve.wait_ge(used, u + 1)
                nc.vector.tensor_copy(qr[:, :, 2 * i:2 * i + 2, :],
                                      A[j % 2][1][:, 0:2 * P].rearrange("p (t h r) -> p t h r", t=NT, h=2)
                                      ).then_inc(a_free[j % 2], 1)
                split(u + 2)
            dve.wait_ge(o_done, 8)
            for i in range(2):
                u, j = U_UKV[i], A_UKV + 2 * i
                dve.wait_ge(used, u + 1)
                nc.vector.tensor_copy(kn[:, 4 * i + 2:4 * i + 4, :],
                                      A[j % 2][1][:, :].rearrange("p (h s) -> p h s", h=2)
                                      ).then_inc(a_free[j % 2], 1)
                j += 1
                nc.vector.tensor_copy(lv[:, 1, i * 512:(i + 1) * 512], A[j % 2][1][:, :]
                                      ).then_inc(a_free[j % 2], 1)
                split(u + 2)
            dve.wait_ge(rope_cs, 1)
            for j in (A_UQ + 2, A_UQ + 3):
                dve.wait_ge(a_free[j % 2], 2 * (j // 2 + 1))

            def rotate(src, dst, scratch, heads):
                c, s_ = [cs[:, i].unsqueeze(2).to_broadcast([P, NT, heads, 32]) for i in range(2)]
                x1, x2 = src[:, :, :, 0:32], src[:, :, :, 32:64]
                for i, (a, b) in enumerate(((x1, c), (x2, s_), (x2, c), (x1, s_))):
                    step(nc.vector.tensor_tensor(scratch[i], a, b, ALU.mult))
                step(nc.vector.tensor_tensor(dst[:, :, :, 0:32], scratch[0], scratch[1], ALU.subtract))
                return nc.vector.tensor_tensor(dst[:, :, :, 32:64], scratch[2], scratch[3], ALU.add)

            step(rotate(qr, qr, [tmp[:, i] for i in range(4)], HEADS))
            small = rt[:, 0:8].rearrange("p i t e -> p (i t e)").rearrange("p (a t o r) -> p a t o r", a=2, t=NT, o=1)
            small2 = rt[:, 8:12].rearrange("p i t e -> p (i t e)").rearrange("p (t o r) -> p t o r", t=NT, o=1)
            small3 = rsm[:, :].rearrange("p (t o r) -> p t o r", t=NT, o=1)
            step(nc.vector.memset(kr[:, :, :, :], 0.0))
            for b in range(2):
                last = rotate(kraw[:, :, :].unsqueeze(2), kr[:, b, :, b * 64:(b + 1) * 64].unsqueeze(2),
                              [small[:, 0], small[:, 1], small2, small3], 1)
                if b == 0:
                    step(last)
            last.then_inc(rope_done, 1)
            attention(LAT_GROUPS, S_LAT, MLA_SCALE, T_PL, A_LO, 0, True)
            for c in range(2):
                if U_O1[c][0] + 2 < U_MOE:
                    split(U_O1[c][0] + 2)
                    split(U_O1[c][1] + 2)
                add_residual(A_OUT[1][c], c * 512, 512, U_O1[c][1])
            dve.wait_ge(gb1_in, 96)
            normalise(7, h, xn, GB1)
            for t in range(NT):
                dve.wait_ge(xs_hi, t + 1)
                nc.vector.tensor_tensor(xs[1][:, t, :], xn[:, t, :], xs[0][:, t, :].bitcast(F32),
                                        ALU.subtract).then_inc(xs_done, 1)

            def bc(a):
                return a.unsqueeze(2).to_broadcast([P, NT, E])

            mask, lg, eq, oh1, oh2, g = (rt[:, i] for i in range(6))
            j = A_RT
            dve.wait_ge(rout_in, 32)
            dve.wait_ge(route_mm, 1)
            for t in range(NT):
                last = nc.vector.tensor_tensor(lg[:, t, :], A[j % 2][t][:, 0:E], br[:, :], ALU.add)
            last.then_inc(a_free[j % 2], 2)
            dve.wait_ge(a_free[j % 2], 2 * (j // 2 + 1))
            pr = prio[:, :].unsqueeze(1).to_broadcast([P, NT, E])
            for i, oh in enumerate((oh1, oh2)):
                step(nc.vector.tensor_reduce(r1[:, i, :], lg, AX.X, ALU.max))
                step(nc.vector.tensor_tensor(eq, lg, bc(r1[:, i, :]), ALU.is_equal))
                step(nc.vector.tensor_tensor(eq, eq, pr, ALU.mult))
                step(nc.vector.tensor_reduce(r1[:, 9, :], eq, AX.X, ALU.max))
                step(nc.vector.tensor_tensor(oh, eq, bc(r1[:, 9, :]), ALU.is_equal))
                if i == 0:
                    step(nc.vector.scalar_tensor_tensor(lg, oh, NEG, lg, ALU.mult, ALU.add))
            nc.vector.tensor_tensor(r1[:, 2, :], r1[:, 1, :], r1[:, 0, :], ALU.subtract).then_inc(rt_exp_in, 1)
            nc.vector.tensor_tensor(mask, oh1, oh2, ALU.add).then_inc(mask_done, 1)
            dve.wait_ge(rt_exp, 1)
            step(nc.vector.tensor_scalar(r1[:, 4, :], r1[:, 3, :], 1.0, None, ALU.add))
            step(nc.vector.reciprocal(r1[:, 5, :], r1[:, 4, :]))
            step(nc.vector.tensor_tensor(r1[:, 6, :], r1[:, 3, :], r1[:, 5, :], ALU.mult))
            step(nc.vector.tensor_tensor(oh1, oh1, bc(r1[:, 5, :]), ALU.mult))
            step(nc.vector.tensor_tensor(oh2, oh2, bc(r1[:, 6, :]), ALU.mult))
            step(nc.vector.memset(gate_of[:, :, :], 0.0))
            step(nc.vector.memset(slot_of[:, :, :], -1.0))
            for r in range(2):
                step(nc.vector.tensor_tensor(gate_of[:, :, 1 + r * E:1 + (r + 1) * E], oh1, oh2, ALU.add))
            for a in (selT[:, :], ys[0], ys[1]):
                last = nc.vector.memset(a.bitcast(F32), 0.0)
            last.then_inc(moe_const, 1)
            j = A_RT + 1
            dve.wait_ge(route_mm, 2)
            step(nc.vector.tensor_reduce(r1[:, 7, 0:1], A[j % 2][0][:, E:2 * E], AX.X, ALU.max))
            step(nc.vector.tensor_scalar(r1[:, 7, 1:2], r1[:, 7, 0:1], P + 0.5, float(E), ALU.is_gt, ALU.mult))
            nc.vector.tensor_scalar(nround[:, :], r1[:, 7, 1:2], float(E), None, ALU.add).then_inc(route_done, 1)
            for t in range(NT):
                step(nc.vector.scalar_tensor_tensor(slot_of[:, t, 0:E], A[j % 2][t][:, 0:E], 1e4,
                                                    mask[:, t, :], ALU.add, ALU.mult))
            step(nc.vector.tensor_scalar(slot_of[:, :, E:2 * E], slot_of[:, :, 0:E], -1e4 - P, None, ALU.add))
            last = nc.vector.tensor_scalar(slot_of[:, :, 0:E], slot_of[:, :, 0:E], -1e4, None, ALU.add)
            last.then_inc(a_free[j % 2], 2)
            dve.wait_ge(a_free[j % 2], 2 * (j // 2 + 1))

            def one_hot(ve):
                for t in range(NT):
                    last = nc.vector.tensor_scalar(sel[:, t * P:(t + 1) * P], iota,
                                                   slot_of[:, t, bass.ds(ve, 1)], None, ALU.is_equal)
                last.then_inc(sel_done, 1)

            def gathered_lo(tj, it):
                for b in range(2):
                    j, cols = tj + b, slice(b * 512, (b + 1) * 512)
                    dve.wait_ge(t_free[j % 2], it * 8 + 2 * (j // 2) + 1)
                    nc.vector.tensor_tensor(xg[1][:, cols], T[j % 2][:, :], xg[0][:, cols].bitcast(F32),
                                            ALU.subtract).then_inc(t_free[j % 2], 1)

            def output_lo(c, it):
                dve.wait_ge(y_hi, it * 2 + c + 1)
                cols = slice(c * 512, (c + 1) * 512)
                nc.vector.tensor_tensor(ys[1][:, cols], S[(S_MOE + c) % 2][:, :], ys[0][:, cols].bitcast(F32),
                                        ALU.subtract).then_inc(s_free[(S_MOE + c) % 2], 1)

            def add_outputs(t, ve):
                for c in range(2):
                    s = S_MOE + 2 + 2 * t + c
                    dve.wait_ge(scat_done, ve * 4 + 2 * t + c + 2)
                    cols = slice(c * 512, (c + 1) * 512)
                    nc.vector.scalar_tensor_tensor(h[:, t, cols], S[s % 2][:, :],
                                                   gate_of[:, t, bass.ds(ve, 1)], h[:, t, cols],
                                                   ALU.mult, ALU.add).then_inc(s_free[s % 2], 1)

            def multiply(c, ve, t_before):
                jg, ju = A_MOE + 2 * c, A_MOE + 2 * c + 1
                dve.wait_ge(used, ve * MU + U_MOE + 4 * c + 4)
                dve.wait_ge(a_free[jg % 2], ve * 4 + 2 * (jg // 2 + 1))
                dve.wait_ge(t_done, ve * 8 + t_before)
                for b in range(2):
                    cols = slice(b * EN, (b + 1) * EN)
                    nc.vector.tensor_tensor(ehid[:, cols], A[ju % 2][b][:, 0:EN], esilu[:, cols],
                                            ALU.mult).then_inc(a_free[ju % 2], 1)

            def hidden_lo(c, tj, ve):
                for n, blocks in enumerate((4, 3)):
                    j, at = tj + n, (7 * c + 4 * n) * P
                    dve.wait_ge(t_free[j % 2], ve * 8 + 2 * (j // 2) + 1)
                    nc.vector.tensor_tensor(hT[1][:, at:at + blocks * P], T[j % 2][:, 0:blocks * P],
                                            hT[0][:, at:at + blocks * P].bitcast(F32), ALU.subtract
                                            ).then_inc(t_free[j % 2], 1)

            dve.wait_ge(consts, 2)
            one_hot(0)
            gathered_lo(T_MOE, 0)
            rounds = dve.value_load(nround[0:1, 0:1], min_val=E, max_val=2 * E)
            U, t1 = U_MOE, T_MOE + 2
            with dve.Fori(0, rounds) as ve:
                split(U, ve)
                output_lo(0, ve)
                split(U + 1, ve)
                output_lo(1, ve)
                split(U + 2, ve)
                add_outputs(0, ve)
                split(U + 3, ve)
                add_outputs(1, ve)
                split(U + 4, ve)
                multiply(0, ve, t1)
                split(U + 5, ve)
                dve.wait_ge(t_done, ve * 8 + t1 + 2)
                one_hot(ve + 1)
                split(U + 6, ve)
                split(U + 7, ve)
                hidden_lo(0, t1 + 2, ve)
                split(U + 8, ve)
                multiply(1, ve, t1 + 4)
                split(U + 9, ve)
                hidden_lo(1, t1 + 4, ve)
                split(U + 10, ve)
                split(U + 11, ve)
                gathered_lo(t1 + 6, ve)
            output_lo(0, rounds)
            output_lo(1, rounds)
            add_outputs(0, rounds)
            add_outputs(1, rounds)
            dve.wait_ge(gb2_in, 64)
            normalise(8, h, xn, GB2)

        @block.gpsimd
        def _(pool):
            steps = [0]

            def step(ins):
                steps[0] += 1
                ins.then_inc(pool_step, 1)
                pool.wait_ge(pool_step, steps[0])

            def gain(dst, vector, done, n=D):
                pool.dma_start(dst, vector.partition_broadcast(P)).then_inc(done, 16)

            def inverse_rms(out, sums, n_values, done, cols):
                step(nc.gpsimd.tensor_scalar(out, sums, 1.0 / n_values, EPS, ALU.mult, ALU.add))
                nc.gpsimd.tensor_tensor(out, out, mhalf[:, 0:cols], ALU.pow).then_inc(done, 1)

            def norm(n, n_values=D):
                pool.wait_ge(ssum_done, 2 * n + 2)
                inverse_rms(rstd[:, n, :], ssum[:, n, :], n_values, rstd_done, NT)

            gain(GB1[:, :], mem_norm[0], gb1_in)
            gain(GB2[:, :], attn_norm[0], gb2_in)
            step(nc.gpsimd.memset(mhalf[:, :], -0.5))
            for a, v in ((ident, 0.0), (ones, 1.0), (tri, 1.0), (tris, 1.0), (cmask, 0.0)):
                step(nc.gpsimd.memset(a[:, :], v))
            step(nc.gpsimd.affine_select(out=ident[:, :], in_=ident[:, :], pattern=[[-1, P]],
                                         compare_op=ALU.not_equal, fill=1.0, base=0, channel_multiplier=1))
            step(nc.gpsimd.affine_select(out=tri[:, :], in_=tri[:, :], pattern=[[1, P]],
                                         compare_op=ALU.is_ge, fill=0.0, base=0, channel_multiplier=-1))
            step(nc.gpsimd.affine_select(out=tris[:, :], in_=tris[:, :], pattern=[[1, P]],
                                         compare_op=ALU.is_gt, fill=0.0, base=0, channel_multiplier=-1))
            step(nc.gpsimd.affine_select(out=cmask[:, :], in_=cmask[:, :], pattern=[[-1, P]],
                                         compare_op=ALU.is_ge, fill=NEG, base=0, channel_multiplier=1))
            nc.gpsimd.iota(prio[:, :], pattern=[[-1, E]], base=E, channel_multiplier=0,
                           allow_small_or_imprecise_dtypes=True).then_inc(consts, 1)
            norm(0)
            norm(1)
            pool.wait_ge(xn_done, 2)
            gain(GB1[:, :], gm_v_norm[0], gb1_in)
            pool.wait_ge(xn_done, 4)
            gain(GB2[:, :], ffn_norm[0], gb2_in)
            pool.wait_ge(vss_done, 1)
            inverse_rms(vrs[:, :, :].rearrange("p t g -> p (t g)"), vss[:, :, :].rearrange("p t g -> p (t g)"),
                        P, vrs_done, NT * NG)
            pool.wait_ge(vn_done, NT)
            gain(GB1[:, :], mem_norm[1], gb1_in)
            norm(2)
            pool.wait_ge(xn_done, 6)
            gain(GB2[:, :], attn_norm[1], gb2_in)
            j = A_FF[1] + 7
            pool.wait_ge(a_free[j % 2], 2 * (j // 2 + 1))
            pool.dma_start(memt, mem[0].rearrange("(t p) d -> p t d", p=P)).then_inc(mem2_in, 16)
            norm(3)
            norm(4)
            pool.wait_ge(xn_done, 8)
            gain(GB1[:, 0:QL], mla_q_norm[0], gb1_in)
            gain(GB1[:, QL:D], mla_kv_norm[0], gb1_in)
            norm(5, QL)
            norm(6, KVL)
            pool.wait_ge(t_done, T_ROPE + 2)
            gain(GB1[:, :], ffn_norm[1], gb1_in)
            pool.wait_ge(o_done, 14)
            gain(GB2[:, :], final_norm, gb2_in)
            nc.gpsimd.iota(iota, pattern=[[1, P]], base=0, channel_multiplier=0,
                           allow_small_or_imprecise_dtypes=True).then_inc(consts, 1)
            norm(7)
            norm(8)


INPUTS = ["x", "mem", "positions", "attn_norm", "mem_norm", "w_mem_kv", "ffn_norm", "final_norm",
          "gm_w_in", "gm_v_norm", "gm_w_s", "gm_b_s", "gm_w_out",
          "mla_w_in", "mla_q_norm", "mla_w_uq", "mla_kv_norm", "mla_w_ukv", "mla_w_out",
          "ff_w_gate", "ff_w_up", "ff_w_down",
          "moe_w_router", "moe_b_router", "moe_w_gate", "moe_w_up", "moe_w_down"]


def kernel(**inputs):
    import concourse.bacc as bacc
    from concourse.bass_utils import run_bass_kernel_spmd

    nc = bacc.Bacc("TRN2", target_bir_lowering=False, num_devices=1)
    arrays = {f"in_{name}": np.ascontiguousarray(inputs[name]) for name in INPUTS}
    steps = np.arange(0, ROPE, 2, dtype=np.float32) / np.float32(ROPE)
    arrays["in_rope_freq"] = (1.0 / np.float32(10000.0) ** steps).astype(np.float32)
    args = [nc.dram_tensor(name, a.shape, mybir.dt.from_np(a.dtype), kind="ExternalInput").ap()
            for name, a in arrays.items()]
    out = nc.dram_tensor("out_0", (1, SEQ, D), F32, kind="ExternalOutput").ap()
    build(nc, *args, out)
    got = run_bass_kernel_spmd(nc, [arrays], core_ids=[0])
    return got.results[0]["out_0"]
```

```python
import numpy as np

import concourse.bass as bass
from concourse import mybir
from contextlib import ExitStack

F32 = mybir.dt.float32
F32R = mybir.dt.float32r
I32 = mybir.dt.int32
ALU = mybir.AluOpType
ACT = mybir.ActivationFunctionType
AX = mybir.AxisListType

P = 128
D = 1024
SEQ = 256
NT = SEQ // P
KD = D // P
MH = 4
MEMW = MH * P
GM = 1024
NG = GM // P
HEADS = 8
NOPE, ROPE = 128, 64
QK = NOPE + ROPE
QL, KVL = 768, 256
FF = 2816
FHALF = FF // 2
FB = FHALF // P
FCH = FHALF // 4
E = 8
FE = 1792
EB = FE // P
ECH = FE // 2
EN = ECH // 2
EPS = 1e-6
MEM_SCALE = float(P) ** -0.5
MLA_SCALE = float(QK) ** -0.5
NEG = -1e30
MAGIC = 12582912.0
TWO_PI = 2 * np.pi
CAT = KD + MH

OUT_ROWS = (KD, 0, 4)

UNIT = 3584
RAW, SPLIT = 3, 2


def two_pi_parts():
    parts, rest = [], TWO_PI
    for _ in range(3):
        m, e = np.frexp(rest)
        part = float(np.floor(m * 512) / 512 * 2.0 ** int(e))
        parts.append(part)
        rest -= part
    return parts + [float(np.float32(rest))]


def build(nc, x, mem, positions, attn_norm, mem_norm, w_mem_kv, ffn_norm, final_norm,
          gm_w_in, gm_v_norm, gm_w_s, gm_b_s, gm_w_out,
          mla_w_in, mla_q_norm, mla_w_uq, mla_kv_norm, mla_w_ukv, mla_w_out,
          ff_w_gate, ff_w_up, ff_w_down,
          moe_w_router, moe_b_router, moe_w_gate, moe_w_up, moe_w_down, rope_freq, out):
    def rows(w, k0, k, c0, n):
        return w[k0 * P:(k0 + k) * P, c0:c0 + n].rearrange("(k p) n -> p k n", p=P)

    units = []

    def add(w, k0, k, c0, n):
        units.append((rows(w, k0, k, c0, n), k, n))
        return len(units) - 1

    def add_wide(w, c0):
        return [add(w, 0, 4, c0, 512), add(w, 4, 4, c0, 512)]

    def add_kv(layer):
        w = w_mem_kv[layer]
        return [add(w, 0, KD, 0, 256), add(w, 0, KD, 256, 256)], add_wide(w, MEMW)

    def add_out(w):
        return [[add(w, k0, 4, c, 512) for c in (0, 512)] for k0 in OUT_ROWS]

    w = gm_w_in[0]
    U_Q0 = [add(w, 0, KD, 2 * GM + c, 256) for c in (0, 256)]
    U_K0, U_V0 = add_kv(0)
    U_GV = [add_wide(w, GM + c) for c in (0, 512)]
    U_GU = [add_wide(w, c) for c in (0, 512)]
    U_O0 = add_out(gm_w_out[0])
    U_FF = []
    for h in range(2):
        gu = [(add(ff_w_gate[0], 0, KD, h * FHALF + c * FCH, FCH),
               add(ff_w_up[0], 0, KD, h * FHALF + c * FCH, FCH)) for c in range(4)]
        U_FF.append((gu, [add(ff_w_down[0], h * FB, FB, c * 256, 256) for c in range(4)]))
    U_K1, U_V1 = add_kv(1)
    w = mla_w_in[0]
    U_C = [add_wide(w, c) for c in (0, 512)]
    U_Q1 = [add(w, 0, KD, QL + KVL + ROPE + c, 256) for c in (0, 256)]
    U_KR = add(w, 0, KD, QL + KVL, ROPE)
    U_UQ = [add(mla_w_uq[0], 0, QL // P, c * 2 * QK, 2 * QK) for c in range(4)]
    U_UKV = [add(mla_w_ukv[0], 0, KVL // P, c * 1024, 1024) for c in range(2)]
    U_O1 = add_out(mla_w_out[0])
    U_OUT = (U_O0, U_O1)
    U_MOE = len(units)
    MU = 12
    moe_shape = [(4, ECH)] * 8 + [(7, 512)] * 4

    def shape_of(u):
        return units[u][1:] if u < U_MOE else moe_shape[(u - U_MOE) % MU]

    def numbered(*jobs):
        first, n = {}, 0
        for name, count in jobs:
            first[name] = n
            n += count
        return first

    A_OF = numbered(("q0", 2), ("k0", 2), ("v0", 1), ("gv", 2), ("gu", 2), ("mix", 2), ("out0", 2),
                    ("ff0", 12), ("ff1", 12), ("k1", 2), ("v1", 1), ("c", 2), ("q1", 2), ("kr", 1),
                    ("uq", 4), ("ukv", 4), ("out1", 2), ("router", 2), ("experts", 0))
    A_Q = [A_OF["q0"], A_OF["q1"]]
    A_K = [A_OF["k0"], A_OF["k1"]]
    A_V = [A_OF["v0"], A_OF["v1"]]
    A_GV, A_GU = A_OF["gv"], A_OF["gu"]
    A_MIX = A_OF["mix"]
    A_OUT = [A_OF["out0"], A_OF["out1"]]
    A_FF = [A_OF["ff0"], A_OF["ff1"]]
    A_C, A_KR = A_OF["c"], A_OF["kr"]
    A_UQ = A_OF["uq"]
    A_UKV = A_OF["ukv"]
    A_RT = A_OF["router"]
    A_MOE = A_OF["experts"]
    T_OF = numbered(("x0", 4), ("mem0", 4), ("ws", 2), ("att0", 8), ("u", 4), ("fn0", 4),
                    ("fh0", 6), ("fh1", 6), ("mem1", 4), ("x1", 4), ("c", 4), ("att1", 7), ("rope", 3),
                    ("att1 last", 1), ("lat", 12), ("fn1", 4), ("experts", 0))
    T_X = [T_OF["x0"], T_OF["x1"]]
    T_MEM = [T_OF["mem0"], T_OF["mem1"]]
    T_WS, T_U = T_OF["ws"], T_OF["u"]
    T_FN = [T_OF["fn0"], T_OF["fn1"]]
    T_FH = [T_OF["fh0"], T_OF["fh1"]]
    T_C, T_ROPE = T_OF["c"], T_OF["rope"]
    T_MOE = T_OF["experts"]
    S_MEM = [0, 4]
    S_LAT = 8
    S_MOE = 14
    XN_OF = numbered(("x0", 4), ("mem0", 2), ("fn0", 4), ("mem1", 2), ("x1", 4), ("fn1", 4), ("final", NT))
    N_MEM, N_X, N_FN, N_CQ, N_CKV, N_FINAL = (0, 3), (1, 4), (2, 7), 5, 6, 8

    MEM_GROUPS = [(t, (2 * i, 2 * i + 1), SEQ) for t in range(NT) for i in range(2)]
    LAT_GROUPS = [(t, hs, n) for i in (0, 4)
                  for t, hs, n in ((1, (i, i + 1), SEQ), (1, (i + 2, i + 3), SEQ),
                                   (0, tuple(range(i, i + 4)), P))]

    class Heads:

        def __init__(self, groups, s0, t0, last_out, cat0, values):
            self.groups, self.n, self.s0, self.t0 = groups, len(groups), s0, t0
            self.last_out, self.cat0, self.values = last_out, cat0, values

        def t_prob(self, g):
            return self.t0 + max(0, 2 * g - 1)

        def t_out(self, g):
            return self.t0 + 2 * g + 2 if g < self.n - 1 else self.last_out

    ctx = ExitStack()
    with ctx:
        def sb(name, shape, dt=F32):
            return ctx.enter_context(nc.sbuf_tensor(name, shape, dt))

        def sem(name):
            return ctx.enter_context(nc.semaphore(name))

        raw = sb("raw", [P, RAW * UNIT])
        hi = sb("hi", [P, SPLIT * UNIT], F32R)
        lo = sb("lo", [P, SPLIT * UNIT], F32R)
        xT = [sb(f"xT_{s}", [P, CAT * SEQ], F32R) for s in ("hi", "lo")]
        wk = [sb(f"wk_{s}", [P, 3072], F32R) for s in ("hi", "lo")]
        sel = sb("sel", [P, NT * P], F32R)
        selT = sb("selT", [P, NT * P], F32R)
        h = sb("h", [P, NT, D])
        R1 = sb("R1", [P, 2048])
        R2 = sb("R2", [P, 2048])
        R3 = sb("R3", [P, 4096])
        GB1 = sb("GB1", [P, D])
        GB2 = sb("GB2", [P, D])
        krT = sb("krT", [P, 2, SEQ])
        kr = sb("kr", [P, 2, NT, P])
        kraw = sb("kraw", [P, NT, ROPE])
        ident = sb("ident", [P, P])
        ones = sb("ones", [P, P])
        tri = sb("tri", [P, P])
        tris = sb("tris", [P, P])
        cmask = sb("cmask", [P, P])
        freq = sb("freq", [P, 32])
        posi = sb("posi", [P, NT], I32)
        posf = sb("posf", [P, NT])
        cs = sb("cs", [P, 2, NT, 32])
        qscale = sb("qscale", [P, 2, NT])
        ssum = sb("ssum", [P, 9, 2])
        rstd = sb("rstd", [P, 9, 2])
        vss = sb("vss", [P, NT, NG])
        vrs = sb("vrs", [P, NT, NG])
        mhalf = sb("mhalf", [P, NT * NG])
        gbs = sb("gbs", [P, NG])
        mx = sb("mx", [P, 14, 4])
        nb = sb("nb", [P, 14, 4])
        den = sb("den", [P, 14, 4])
        rden = sb("rden", [P, 14, 4])
        wr = sb("wr", [P, KD, E])
        br = sb("br", [P, E])
        prio = sb("prio", [P, E])
        rt = sb("rt", [P, 12, NT, E])
        r1 = sb("r1", [P, 10, NT])
        rsm = sb("rsm", [P, NT * 32])
        nround = sb("nround", [P, 1], I32)
        slot_of = sb("slot_of", [P, NT, 2 * E + 1])
        gate_of = sb("gate_of", [P, NT, 2 * E + 1])

        A = [[ctx.enter_context(nc.psum_tensor(f"A{p}{t}", [P, 512], F32)) for t in range(2)]
             for p in range(2)]
        T = [ctx.enter_context(nc.psum_tensor(f"T{b}", [P, 512], F32)) for b in range(2)]
        S = [ctx.enter_context(nc.psum_tensor(f"S{b}", [P, 512], F32)) for b in range(2)]

        raw_full = [sem(f"raw_full{i}") for i in range(RAW)]
        hi_done = sem("hi_done")
        lo_done = sem("lo_done")
        used = sem("used")
        t_done, s_done = sem("t_done"), sem("s_done")
        mixed_done, route_mm, scat_done = sem("mixed_done"), sem("route_mm"), sem("scat_done")
        a_free = [sem(f"a_free{i}") for i in range(2)]
        t_free = [sem(f"t_free{i}") for i in range(2)]
        s_free = [sem(f"s_free{i}") for i in range(2)]
        x_in, mem_in, ws_in = sem("x_in"), sem("mem_in"), sem("ws_in")
        gb1_first, gb2_first = sem("gb1_first"), sem("gb2_first")
        gb1_in, gb2_in = sem("gb1_in"), sem("gb2_in")
        gbs_in, rope_in, rout_in, mem2_in = sem("gbs_in"), sem("rope_in"), sem("rout_in"), sem("mem2_in")
        consts = sem("consts")
        ssum_done = sem("ssum_done")
        rstd_done = sem("rstd_done")
        pool_step = sem("pool_step")
        xn_done = sem("xn_done")
        vss_done, vrs_done, vn_done = sem("vss_done"), sem("vrs_done"), sem("vn_done")
        max_done = sem("max_done")
        exp_done = sem("exp_done")
        prob_done = sem("prob_done")
        rope_ang, rope_cs, rope_done = sem("rope_ang"), sem("rope_cs"), sem("rope_done")
        kr_copied = sem("kr_copied")
        c_ready = sem("c_ready")
        rt_exp_in, rt_exp = sem("rt_exp_in"), sem("rt_exp")
        mask_done, route_done, moe_const = sem("mask_done"), sem("route_done"), sem("moe_const")
        sel_done = sem("sel_done")
        y_hi = sem("y_hi")
        xs_hi, xs_done = sem("xs_hi"), sem("xs_done")
        act_step = sem("act_step")
        dve_step = sem("dve_step")
        out_done = sem("out_done")
        block = ctx.enter_context(nc.Block())

        xTv = [a[:, :].rearrange("p (k s) -> p k s", s=SEQ) for a in xT]
        wkv = [a[:, 0:FB * SEQ].rearrange("p (k s) -> p k s", s=SEQ) for a in wk]
        xg = [a[:, 0:KD * P] for a in xT]
        hT = [a[:, KD * P:KD * P + EB * P] for a in xT]
        xs = [a[:, 0:NT * D].rearrange("p (t d) -> p t d", t=NT) for a in wk]
        ys = [a[:, NT * D:NT * D + D] for a in wk]
        xn = R1[:, :].rearrange("p (t d) -> p t d", t=NT)
        gu = xn
        lat = xn
        memt = R2[:, :].rearrange("p (t d) -> p t d", t=NT)
        gv = memt
        qn = R2[:, :].rearrange("p (h s) -> p h s", h=HEADS)
        xnT = R2[:, :].rearrange("p (k s) -> p k s", k=KD)
        fsilu = R2[:, 0:NT * FCH].rearrange("p (t n) -> p t n", t=NT)
        mk = R3[:, 0:1024].rearrange("p (h s) -> p h s", h=MH)
        mv = R3[:, 1024:2048].rearrange("p (t n) -> p t n", t=NT)
        mq = R3[:, 2048:3072].rearrange("p (h s) -> p h s", h=MH)
        wsT = R3[:, 3072:4096].rearrange("p (g s) -> p g s", g=NG)
        kn = R3[:, 0:2048].rearrange("p (h s) -> p h s", h=HEADS)
        lv = R3[:, 2048:4096].rearrange("p (t n) -> p t n", t=NT)
        fhid = R3[:, 0:NT * FHALF].rearrange("p (t n) -> p t n", t=NT)
        esilu = R3[:, 0:ECH]
        ehid = R3[:, ECH:2 * ECH]
        wsr = R3[:, 0:1024].rearrange("p (g s) -> p g s", g=NG)
        PP = R1[:, 0:1024].rearrange("p (a b) -> p a b", a=2)
        PPT = R1[:, 1024:2048].rearrange("p (a b) -> p a b", a=2)
        iota = R3[:, 3072:3072 + P]
        qr = GB1[:, :].rearrange("p (t h r) -> p t h r", t=NT, h=HEADS)
        qrT = GB2[:, :].rearrange("p (i s) -> p i s", i=4)
        tmp = R3[:, 3072:4096].rearrange("p (i t h r) -> p i t h r", i=4, t=NT, h=4)
        junk, junk_v, junk_end = R3[:, 3072:4096], R3[:, 2048:3072], R1[:, 0:D]
        mem_heads = [Heads(MEM_GROUPS, S_MEM[i], T_OF[f"att{i}"], last, KD, mv)
                     for i, last in enumerate((T_OF["att0"] + 7, T_OF["att1 last"]))]
        lat_heads = Heads(LAT_GROUPS, S_LAT, T_OF["lat"], T_OF["lat"] + 11, 0, lv)

        def piece(ring, slots, u, i):
            k, n = shape_of(u)
            at, half = (u % slots) * UNIT, k * n // 2
            return ring[:, at + i * half:at + (i + 1) * half]

        def part(ring, u, kk, c0, n):
            at = (u % SPLIT) * UNIT + kk * shape_of(u)[1] + c0
            return ring[:, at:at + n]

        @block.sync
        def _(sp):
            def load(u, src):
                k, n = shape_of(u)
                at = (u % RAW) * UNIT
                if u >= RAW:
                    sp.wait_ge(lo_done, 2 * (u - RAW) + 2)
                sp.dma_start(raw[:, at:at + k * n].rearrange("p (k n) -> p k n", n=n),
                             src).then_inc(raw_full[u % RAW], 16)

            sp.dma_start(GB2[:, :], attn_norm[0].partition_broadcast(P)).then_inc(gb2_first, 16)
            sp.dma_start(h[:, :, :], x[0].rearrange("(t p) d -> p t d", p=P)).then_inc(x_in, 16)
            load(0, units[0][0])
            sp.dma_start(memt, mem[0].rearrange("(t p) d -> p t d", p=P)).then_inc(mem_in, 16)
            sp.dma_start(GB1[:, :], mem_norm[0].partition_broadcast(P)).then_inc(gb1_first, 16)
            for u in range(1, U_MOE):
                load(u, units[u][0])

            def expert_loads(e, ve):
                for j in range(MU):
                    u = U_MOE + j
                    k, n = moe_shape[j]
                    if j < 8:
                        w = (moe_w_gate, moe_w_up)[j // 2 % 2]
                        k0, c0 = 4 * (j % 2), ECH * (j // 4)
                    else:
                        w, k0, c0 = moe_w_down, 7 * ((j - 8) // 2), 512 * (j % 2)
                    src = w[0, bass.ds(e, 1), k0 * P:(k0 + k) * P, c0:c0 + n]
                    at = (u % RAW) * UNIT
                    sp.wait_ge(lo_done, ve * (2 * MU) + 2 * (u - RAW) + 2)
                    sp.dma_start(raw[:, at:at + k * n].rearrange("p (k n) -> p k n", n=n),
                                 src.rearrange("e (k p) n -> p (e k) n", p=P)
                                 ).then_inc(raw_full[u % RAW], 16)

            with sp.Fori(0, E) as e:
                expert_loads(e, e)
            sp.wait_ge(route_done, 1)
            rounds = sp.value_load(nround[0:1, 0:1], min_val=E, max_val=2 * E)
            with sp.If(rounds > E):
                with sp.Fori(0, E) as e:
                    expert_loads(e, e + E)
            for t in range(NT):
                sp.wait_ge(xn_done, XN_OF["final"] + t + 1)
                sp.dma_start(out[0, t * P:(t + 1) * P, :], xn[:, t]).then_inc(out_done, 16)
            sp.wait_ge(out_done, 16 * NT)

        @block.tensor
        def _(pe):
            def a_job(j):
                if j >= 2:
                    pe.wait_ge(a_free[j % 2], 2 * (j // 2))
                return A[j % 2]

            def t_job(j):
                if j >= 2:
                    pe.wait_ge(t_free[j % 2], 2 * (j // 2))
                return T[j % 2]

            def s_job(j):
                if j >= 2:
                    pe.wait_ge(s_free[j % 2], j // 2)
                return S[j % 2]

            def split_ready(u, kk, it=0):
                k, n = shape_of(u)
                half = k * n // 2
                if kk == 0:
                    pe.wait_ge(lo_done, it * (2 * MU) + 2 * u + 1)
                if kk * n <= half < (kk + 1) * n:
                    pe.wait_ge(lo_done, it * (2 * MU) + 2 * u + 2)

            def three(out, stat, mov, start, stop):
                nc.tensor.matmul(out, stat[0], mov[1], start=start, stop=False)
                nc.tensor.matmul(out, stat[1], mov[0], start=False, stop=False)
                return nc.tensor.matmul(out, stat[0], mov[0], start=False, stop=stop)

            def project(u, pair, acts, k0=0, first=True, final=True, before=None):
                k, n = shape_of(u)
                for kk in range(k):
                    if before and kk in before:
                        before[kk]()
                    split_ready(u, kk)
                    for t in range(NT):
                        last = three(pair[t][:, 0:n], [a[:, k0 + kk, t * P:(t + 1) * P] for a in acts],
                                     (part(hi, u, kk, 0, n), part(lo, u, kk, 0, n)),
                                     first and kk == 0, final and kk == k - 1)
                last.then_inc(used, 1)

            def project_T(u, out, acts, c0, first=True, late=()):
                k = shape_of(u)[0]
                for kk in range(k):
                    if kk == 4:
                        transposed(*late)
                    if first:
                        split_ready(u, kk)
                    last = three(out, (part(hi, u, kk, c0, P), part(lo, u, kk, c0, P)),
                                 [a[:, kk, :] for a in acts], kk == 0, kk == k - 1)
                return last

            def heads_T(u, j, acts, late=()):
                bank = a_job(j)[0]
                for i in range(2):
                    last = project_T(u, bank[:, i * SEQ:(i + 1) * SEQ], acts, i * P, i == 0,
                                     () if i else late)
                last.then_inc(used, 1)

            def transposes(j, blocks):
                bank = t_job(j)
                for i, b in enumerate(blocks):
                    last = nc.tensor.transpose(bank[:, i * P:(i + 1) * P], b, ident[:, :])
                last.then_inc(t_done, 1)

            def transposed(*jobs):
                for j in jobs:
                    pe.wait_ge(t_free[j % 2], 2 * (j // 2 + 1))

            def half_T(src, name, j0, half, parts=2):
                for t in range(NT):
                    pe.wait_ge(xn_done, XN_OF[name] + (2 * half + t + 1 if parts == 2 else t + 1))
                    transposes(j0 + 2 * half + t, [src[:, t, (4 * half + i) * P:(4 * half + i + 1) * P]
                                                   for i in range(4)])

            def attend(a, g, scores):
                if g + 1 < a.n:
                    t, hs, n = a.groups[g + 1]
                    bank = s_job(a.s0 + g + 1)
                    for i, hd in enumerate(hs):
                        last = scores(bank[:, i * n:(i + 1) * n], hd, t, n)
                    last.then_inc(s_done, 1)
                if 0 <= g < a.n:
                    pe.wait_ge(prob_done, a.s0 + g + 1)
                    transposes(a.t_prob(g), [PP[:, g % 2, i * P:(i + 1) * P] for i in range(4)])
                if g >= 1:
                    t, hs, n = a.groups[g - 1]
                    transposed(a.t_prob(g - 1))
                    bank = t_job(a.t_out(g - 1))
                    nk = n // P
                    for i, hd in enumerate(hs):
                        for b in range(nk):
                            at = (i * nk + b) * P
                            last = nc.tensor.matmul(bank[:, i * P:(i + 1) * P],
                                                    a.values[:, b, hd * P:(hd + 1) * P],
                                                    PPT[:, (g - 1) % 2, at:at + P],
                                                    start=b == 0, stop=b == nk - 1)
                    last.then_inc(t_done, 1)

            def mem_scores(out, hd, t, n):
                return nc.tensor.matmul(out, mq[:, hd, t * P:(t + 1) * P], mk[:, hd, :],
                                        start=True, stop=True)

            def lat_scores(out, hd, t, n):
                nc.tensor.matmul(out, qn[:, hd, t * P:(t + 1) * P], kn[:, hd, 0:n],
                                 start=True, stop=False)
                return nc.tensor.matmul(out, qrT[:, hd // 2, t * P:(t + 1) * P],
                                        krT[:, hd % 2, 0:n], start=False, stop=True)

            def emptied(j):
                pe.wait_ge(a_free[j % 2], 2 * (j // 2 + 1))

            def out_projection(layer, stages, before_last):
                pair = [None, None]
                for i in range(6):
                    r, c = i // 2, i % 2
                    stages[i]()
                    if r == 0:
                        pair[c] = a_job(A_OUT[layer] + c)
                    project(U_OUT[layer][r][c], pair[c], xTv, OUT_ROWS[r], r == 0, r == 2,
                            before_last if i == 5 else None)

            def nothing():
                pass

            pe.wait_ge(consts, 1)
            half_T(xn, "x0", T_X[0], 0)
            half_T(xn, "x0", T_X[0], 1)
            transposed(T_X[0], T_X[0] + 1)
            for i in range(2):
                heads_T(U_Q0[i], A_Q[0] + i, xTv, (T_X[0] + 2, T_X[0] + 3))
            half_T(memt, "mem0", T_MEM[0], 0, 1)
            half_T(memt, "mem0", T_MEM[0], 1, 1)
            pe.wait_ge(ws_in, 16)
            for i in range(2):
                transposes(T_WS + i, [wsr[:, 4 * i + g, :] for g in range(4)])
            transposed(T_MEM[0], T_MEM[0] + 1)
            for i in range(2):
                heads_T(U_K0[i], A_K[0] + i, wkv, (T_MEM[0] + 2, T_MEM[0] + 3))
            pair = a_job(A_V[0])
            for n, u in enumerate(U_V0):
                project(u, pair, wkv, 4 * n, n == 0, n == 1)
            att = mem_heads[0]
            for i in range(2):
                pair = a_job(A_GV + i)
                project(U_GV[i][0], pair, xTv, 0, True, False)
                if i == 0:
                    for j in (A_Q[0], A_Q[0] + 1, A_K[0], A_K[0] + 1):
                        emptied(j)
                attend(att, 2 * i - 1, mem_scores)
                project(U_GV[i][1], pair, xTv, 4, False, True)
                if i == 0:
                    emptied(A_V[0])
                attend(att, 2 * i, mem_scores)
            pair = a_job(A_GU)
            project(U_GU[0][0], pair, xTv, 0, True, False)
            attend(att, 3, mem_scores)
            project(U_GU[0][1], pair, xTv, 4, False, True)
            attend(att, 4, mem_scores)
            pair = a_job(A_GU + 1)
            for n, u in enumerate(U_GU[1]):
                project(u, pair, xTv, 4 * n, n == 0, n == 1)
            pe.wait_ge(vn_done, NT)
            for j in range(2):
                pair = a_job(A_MIX + j)
                for i in range(4):
                    g = 4 * j + i
                    last = nc.tensor.matmul(pair[i // 2][:, (i % 2) * SEQ:(i % 2 + 1) * SEQ], wsT[:, g, :],
                                            gv[:, :, g * P:(g + 1) * P], start=True, stop=True)
                last.then_inc(mixed_done, 1)

            def gated_T(b):
                emptied(A_MIX + b)
                for t in range(NT):
                    transposes(T_U + 2 * b + t, [gu[:, t, (4 * b + i) * P:(4 * b + i + 1) * P]
                                                 for i in range(4)])

            out_projection(0, (lambda: transposed(att.t_out(2), att.t_out(3)), lambda: gated_T(0),
                               lambda: transposed(T_U, T_U + 1), lambda: gated_T(1),
                               lambda: transposed(T_U + 2, T_U + 3), nothing),
                           {3: lambda: half_T(xn, "fn0", T_FN[0], 0)})

            def second_half_T():
                half_T(xn, "fn0", T_FN[0], 1)
                transposed(T_FN[0] + 2, T_FN[0] + 3)

            transposed(T_FN[0], T_FN[0] + 1)
            for hf in range(2):
                gu_units, down_units = U_FF[hf]
                j0, tj = A_FF[hf], T_FH[hf]

                def hidden_T(i, b0, nb, chunks, t0=0):
                    j = j0 + 2 * chunks - 1
                    pe.wait_ge(a_free[j % 2], 2 * (j // 2 + 1))
                    for t in range(NT):
                        transposes(tj + 2 * i + t, [fhid[:, t, (b0 + b) * P:(b0 + b + 1) * P]
                                                    for b in range(nb)])

                for c in range(4):
                    project(gu_units[c][0], a_job(j0 + 2 * c), xTv,
                            before={4: second_half_T} if hf == 0 and c == 0 else None)
                    if c == 2:
                        hidden_T(0, 0, 4, 2)
                    if c == 3:
                        hidden_T(1, 4, 4, 3)
                    project(gu_units[c][1], a_job(j0 + 2 * c + 1), xTv)
                for c in range(4):
                    u, pair = down_units[c], a_job(j0 + 8 + c)
                    if c == 0:
                        transposed(tj, tj + 1, tj + 2, tj + 3)
                    def last_hidden_T():
                        hidden_T(2, 8, 3, 4)
                        transposed(tj + 4, tj + 5)

                    project(u, pair, wkv, before={8: last_hidden_T} if c == 0 else None)
                    if hf == 1 and c >= 2:
                        half_T(memt, "mem1", T_MEM[1], c - 2, 1)

            transposed(T_MEM[1], T_MEM[1] + 1)
            for i in range(2):
                heads_T(U_K1[i], A_K[1] + i, xTv, (T_MEM[1] + 2, T_MEM[1] + 3))
            pair = a_job(A_V[1])
            project(U_V1[0], pair, xTv, 0, True, False)
            half_T(xn, "x1", T_X[1], 0)
            project(U_V1[1], pair, xTv, 4, False, True)
            half_T(xn, "x1", T_X[1], 1)
            transposed(T_X[1], T_X[1] + 1)
            for i in range(2):
                pair = a_job(A_C + i)
                for n, u in enumerate(U_C[i]):
                    if n == 1 and i == 0:
                        transposed(T_X[1] + 2, T_X[1] + 3)
                    project(u, pair, wkv, 4 * n, n == 0, n == 1)
            for i in range(2):
                heads_T(U_Q1[i], A_Q[1] + i, wkv)
            pe.wait_ge(c_ready, NT)

            def latents_T(half):
                for t in range(NT):
                    transposes(T_C + 2 * half + t, [lat[:, t, (4 * half + i) * P:(4 * half + i + 1) * P]
                                                    for i in range(4)])

            latents_T(0)
            project(U_KR, a_job(A_KR), wkv)
            latents_T(1)
            transposed(T_C, T_C + 1)
            att = mem_heads[1]
            for i in range(4):
                u, pair = U_UQ[i], a_job(A_UQ + i)
                for hh in range(2):
                    project_T(u, pair[0][:, hh * SEQ:(hh + 1) * SEQ], xTv, hh * QK, hh == 0,
                              (T_C + 2, T_C + 3) if i == 0 and hh == 0 else ())
                for t in range(NT):
                    for kk in range(QL // P):
                        at = (u % SPLIT) * UNIT + kk * 2 * QK
                        mov = [r[:, at:at + 2 * QK].rearrange("p (h c) -> p h c", h=2)[:, :, NOPE:QK]
                               for r in (hi, lo)]
                        last = three(pair[1][:, t * P:(t + 1) * P],
                                     [a[:, kk, t * P:(t + 1) * P] for a in xTv], mov,
                                     kk == 0, kk == QL // P - 1)
                last.then_inc(used, 1)
                if i == 0:
                    for j in (A_K[1], A_K[1] + 1, A_V[1], A_Q[1], A_Q[1] + 1):
                        emptied(j)
                attend(att, i - 1, mem_scores)
            kvT = [a[:, QL // P:KD, :] for a in xTv]

            def keys_values(i):
                u, pair = U_UKV[i], a_job(A_UKV + 2 * i)
                for hh in range(4):
                    project_T(u, pair[hh // 2][:, (hh % 2) * SEQ:(hh % 2 + 1) * SEQ], kvT, hh * 256, hh == 0)
                pair = a_job(A_UKV + 2 * i + 1)
                for t in range(NT):
                    for kk in range(2):
                        at = (u % SPLIT) * UNIT + kk * 1024
                        mov = [r[:, at:at + 1024].rearrange("p (h c) -> p h c", h=4)[:, :, P:256]
                               for r in (hi, lo)]
                        last = three(pair[t][:, :], [a[:, kk, t * P:(t + 1) * P] for a in kvT], mov,
                                     kk == 0, kk == 1)
                last.then_inc(used, 1)

            keys_values(0)
            attend(att, 3, mem_scores)
            pe.wait_ge(rope_done, 3)
            for t in range(NT):
                transposes(T_ROPE + t, [qr[:, t, 2 * i:2 * i + 2, :] for i in range(4)])
            transposes(T_ROPE + 2, [kr[:, b, t, :] for b in range(2) for t in range(NT)])
            attend(att, 4, mem_scores)
            transposed(T_ROPE, T_ROPE + 1, T_ROPE + 2)
            for j in (A_UKV, A_UKV + 1):
                emptied(j)
            att = lat_heads
            attend(att, -1, lat_scores)
            keys_values(1)
            for j in (A_UKV + 2, A_UKV + 3):
                emptied(j)

            def rows_0():
                attend(att, 2, lat_scores)
                attend(att, 3, lat_scores)
                transposed(att.t_out(0), att.t_out(1), att.t_out(2))

            def rows_4():
                attend(att, 5, lat_scores)
                attend(att, 6, lat_scores)
                transposed(att.t_out(3), att.t_out(4), att.t_out(5))

            def rows_8():
                attend(att, 0, lat_scores)
                transposed(mem_heads[1].t_out(2), mem_heads[1].t_out(3))

            out_projection(1, (rows_8, lambda: attend(att, 1, lat_scores), rows_0,
                               lambda: attend(att, 4, lat_scores), rows_4, nothing),
                           {3: lambda: half_T(xn, "fn1", T_FN[1], 0)})
            half_T(xn, "fn1", T_FN[1], 1)
            transposed(*range(T_FN[1], T_FN[1] + 4))
            pair = a_job(A_RT)
            pe.wait_ge(rout_in, 32)
            for t in range(NT):
                for kk in range(KD):
                    last = nc.tensor.matmul(pair[t][:, 0:E], xnT[:, kk, t * P:(t + 1) * P], wr[:, kk, :],
                                            start=kk == 0, stop=kk == KD - 1)
            last.then_inc(route_mm, 1)
            pair = a_job(A_RT + 1)
            pe.wait_ge(mask_done, 1)
            mask = rt[:, 0]
            nc.tensor.matmul(pair[0][:, 0:E], tris[:, :], mask[:, 0, :], start=True, stop=True)
            nc.tensor.matmul(pair[1][:, 0:E], ones[:, :], mask[:, 0, :], start=True, stop=False)
            nc.tensor.matmul(pair[1][:, 0:E], tris[:, :], mask[:, 1, :], start=False, stop=True)
            nc.tensor.matmul(pair[0][:, E:2 * E], ones[:, :], mask[:, 0, :], start=True, stop=False)
            nc.tensor.matmul(pair[0][:, E:2 * E], ones[:, :], mask[:, 1, :], start=False,
                             stop=True).then_inc(route_mm, 1)

            def gather(tj, it):
                for b in range(2):
                    pe.wait_ge(t_free[(tj + b) % 2], it * 8 + 2 * ((tj + b) // 2))
                    bank = T[(tj + b) % 2]
                    for i in range(4):
                        d = 4 * b + i
                        n = 0
                        for src in (xs[1], xs[0]):
                            for t in range(NT):
                                last = nc.tensor.matmul(bank[:, i * P:(i + 1) * P],
                                                        src[:, t, d * P:(d + 1) * P],
                                                        sel[:, t * P:(t + 1) * P], start=n == 0, stop=n == 3)
                                n += 1
                    last.then_inc(t_done, 1)

            pe.wait_ge(xs_done, NT)
            pe.wait_ge(sel_done, 1)
            gather(T_MOE, 0)
            pe.wait_ge(moe_const, 1)
            for c in range(2):
                pe.wait_ge(s_free[(S_MOE + c) % 2], (S_MOE + c) // 2)
                last = nc.tensor.matmul(S[(S_MOE + c) % 2][:, :], selT[:, 0:P], ys[0][:, c * 512:(c + 1) * 512],
                                        start=True, stop=True)
            last.then_inc(scat_done, 1)

            def scatter(t, ve):
                for c in range(2):
                    s = S_MOE + 2 + 2 * t + c
                    pe.wait_ge(s_free[s % 2], ve * 3 + s // 2)
                    for n in range(2):
                        last = nc.tensor.matmul(S[s % 2][:, :], selT[:, t * P:(t + 1) * P],
                                                ys[1 - n][:, c * 512:(c + 1) * 512],
                                                start=n == 0, stop=n == 1)
                    last.then_inc(scat_done, 1)

            def hidden_expert(ve, units4, j, before_second):
                pe.wait_ge(a_free[j % 2], ve * 4 + 2 * (j // 2))
                for n, u in enumerate(units4):
                    if n:
                        before_second()
                    for kk in range(4):
                        split_ready(u, kk, ve)
                        k = 4 * n + kk
                        stat = [a[:, k * P:(k + 1) * P] for a in xg]
                        for b in range(2):
                            mov = (part(hi, u, kk, b * EN, EN), part(lo, u, kk, b * EN, EN))
                            last = three(A[j % 2][b][:, 0:EN], stat, mov, k == 0, k == 7)
                    last.then_inc(used, 1)

            def hidden_T_expert(ve, c, tj):
                j = A_MOE + 2 * c + 1
                pe.wait_ge(a_free[j % 2], ve * 4 + 2 * (j // 2 + 1))
                for n, nb_ in enumerate((4, 3)):
                    j = tj + n
                    pe.wait_ge(t_free[j % 2], ve * 8 + 2 * (j // 2))
                    for b in range(nb_):
                        at = (4 * n + b) * P
                        last = nc.tensor.transpose(T[j % 2][:, b * P:(b + 1) * P], ehid[:, at:at + P],
                                                   ident[:, :])
                    last.then_inc(t_done, 1)

            def down(ve, u, c, half):
                bank = S[(S_MOE + 6 + c) % 2]
                if half == 0:
                    s = S_MOE + 6 + c
                    pe.wait_ge(s_free[s % 2], ve * 3 + s // 2)
                for kk in range(7):
                    split_ready(u, kk, ve)
                    k = 7 * half + kk
                    last = three(bank[:, :], [a[:, k * P:(k + 1) * P] for a in hT],
                                 (part(hi, u, kk, 0, 512), part(lo, u, kk, 0, 512)), k == 0, k == EB - 1)
                last.then_inc(used, 1)

            pe.wait_ge(route_done, 1)
            rounds = pe.value_load(nround[0:1, 0:1], min_val=E, max_val=2 * E)
            t1 = T_MOE + 2
            with pe.Fori(0, rounds) as ve:
                U = U_MOE
                for b in range(2):
                    pe.wait_ge(t_free[(T_MOE + b) % 2], ve * 8 + 2 * ((T_MOE + b) // 2 + 1))
                hidden_expert(ve, (U, U + 1), A_MOE, nothing)
                scatter(0, ve)

                def second_scatter():
                    scatter(1, ve)
                    for t in range(NT):
                        j = t1 + t
                        pe.wait_ge(t_free[j % 2], ve * 8 + 2 * (j // 2))
                        nc.tensor.transpose(T[j % 2][:, 0:P], sel[:, t * P:(t + 1) * P].bitcast(F32),
                                            ident[:, :]).then_inc(t_done, 1)

                hidden_expert(ve, (U + 2, U + 3), A_MOE + 1, second_scatter)
                hidden_expert(ve, (U + 4, U + 5), A_MOE + 2, nothing)
                hidden_T_expert(ve, 0, t1 + 2)
                hidden_expert(ve, (U + 6, U + 7), A_MOE + 3, nothing)
                for j in (t1 + 2, t1 + 3):
                    pe.wait_ge(t_free[j % 2], ve * 8 + 2 * (j // 2 + 1))
                down(ve, U + 8, 0, 0)
                hidden_T_expert(ve, 1, t1 + 4)
                down(ve, U + 9, 1, 0)
                for j in (t1 + 4, t1 + 5):
                    pe.wait_ge(t_free[j % 2], ve * 8 + 2 * (j // 2 + 1))
                down(ve, U + 10, 0, 1)
                pe.wait_ge(sel_done, ve + 2)
                gather(t1 + 6, ve)
                down(ve, U + 11, 1, 1)
            scatter(0, rounds)
            scatter(1, rounds)

        @block.scalar
        def _(act):
            def act_copy(out, in_):
                return nc.scalar.activation(out, in_, ACT.Copy)

            def split(u, it=0):
                act.wait_ge(raw_full[u % RAW], it * (16 * MU // RAW) + 16 * (u // RAW + 1))
                if u >= SPLIT:
                    act.wait_ge(used, it * MU + u - SPLIT + 1)
                for i in range(2):
                    act_copy(piece(hi, SPLIT, u, i), piece(raw, RAW, u, i)).then_inc(hi_done, 1)

            def square_sums(n, src, n_cols=D, c0=0, scratch=junk):
                for t in range(NT):
                    if n or t:
                        act.wait_ge(ssum_done, 2 * n + t)
                    nc.scalar.activation(scratch[:, 0:n_cols], src[:, t, c0:c0 + n_cols], ACT.Square,
                                         accum_out=ssum[:, n, t:t + 1]).then_inc(ssum_done, 1)

            def t_bank(j, n=4):
                act.wait_ge(t_done, j + 1)
                return T[j % 2][:, 0:n * P].rearrange("p (k s) -> p k s", k=n)

            def t_hi(j, out, n=4):
                act_copy(out, t_bank(j, n)).then_inc(t_free[j % 2], 1)

            def half_hi(j0, acts, half):
                for t in range(NT):
                    t_hi(j0 + 2 * half + t, acts[0][:, 4 * half:4 * half + 4, t * P:(t + 1) * P])

            def two_heads(u, j, out):
                act.wait_ge(used, u + 1)
                act_copy(out, A[j % 2][0][:, :].rearrange("p (h s) -> p h s", h=2)
                         ).then_inc(a_free[j % 2], 2)

            def attend(a, g, scale_of):
                if g + 1 < a.n:
                    t, hs, n = a.groups[g + 1]
                    gg = a.s0 + g + 1
                    act.wait_ge(max_done, gg + 1)
                    if g >= 1:
                        act.wait_ge(t_done, a.t_prob(g - 1) + 1)
                    for i in range(len(hs)):
                        last = nc.scalar.activation(PP[:, (g + 1) % 2, i * n:(i + 1) * n],
                                                    S[gg % 2][:, i * n:(i + 1) * n], ACT.Exp,
                                                    bias=nb[:, gg, i:i + 1], scale=scale_of(t),
                                                    accum_out=den[:, gg, i:i + 1])
                    last.then_inc(s_free[gg % 2], 1)
                if 0 <= g < a.n:
                    j = a.t_prob(g)
                    if g >= 2:
                        act.wait_ge(t_done, a.t_out(g - 2) + 1)
                    act_copy(PPT[:, g % 2, :].rearrange("p (k s) -> p k s", k=4), t_bank(j)
                             ).then_inc(t_free[j % 2], 2)
                if g >= 1:
                    t, hs, _ = a.groups[g - 1]
                    t_hi(a.t_out(g - 1), xTv[0][:, a.cat0 + hs[0]:a.cat0 + hs[0] + len(hs),
                                                t * P:(t + 1) * P], len(hs))

            def mem_scale(layer):
                return lambda t: qscale[:, layer, t:t + 1]

            def lat_scale(t):
                return MLA_SCALE

            def scaled(n, t):
                return rstd[:, n, t:t + 1]

            act.dma_start(wsr, gm_w_s[0].rearrange("g t s -> t g s")).then_inc(ws_in, 16)
            act.dma_start(gbs[:, :], gm_b_s[0].rearrange("g t -> t g"),
                          allow_slow_non_contiguous=True).then_inc(gbs_in, 16)
            act.dma_start(posi[:, :], positions.rearrange("a (t p) -> p (a t)", p=P),
                          allow_slow_non_contiguous=True).then_inc(rope_in, 16)
            act.dma_start(freq[:, :], rope_freq.partition_broadcast(P)).then_inc(rope_in, 16)
            act.dma_start(wr[:, :, :], moe_w_router[0].rearrange("(k p) e -> p k e", p=P)).then_inc(rout_in, 16)
            act.dma_start(br[:, :], moe_b_router[0].partition_broadcast(P)).then_inc(rout_in, 16)
            half_hi(T_X[0], xTv, 0)
            split(0)
            half_hi(T_X[0], xTv, 1)
            act.wait_ge(mem_in, 16)
            square_sums(N_MEM[0], memt)
            split(1)
            square_sums(N_X[0], h)
            for i in range(2):
                two_heads(U_Q0[i], A_Q[0] + i, mq[:, 2 * i:2 * i + 2, :])
                split(U_Q0[i] + 2)
            half_hi(T_MEM[0], wkv, 0)
            half_hi(T_MEM[0], wkv, 1)
            for i in range(2):
                two_heads(U_K0[i], A_K[0] + i, mk[:, 2 * i:2 * i + 2, :])
                split(U_K0[i] + 2)

            def memory_values(layer, us):
                split(us[0] + 2)
                j = A_V[layer]
                act.wait_ge(used, us[1] + 1)
                act_copy(mv[:, 0, :], A[j % 2][0][:, :]).then_inc(a_free[j % 2], 1)

            memory_values(0, U_V0)
            split(U_V0[1] + 2)
            att = mem_heads[0]
            act.wait_ge(rstd_done, N_X[0] + 1)

            def gelu(u, j, dst, i):
                act.wait_ge(used, u + 1)
                for t in range(NT):
                    nc.scalar.activation(dst[:, t, i * 512:(i + 1) * 512], A[j % 2][t][:, :], ACT.Gelu,
                                         scale=scaled(N_X[0], t)).then_inc(a_free[j % 2], 1)

            for i in range(2):
                attend(att, 2 * i - 1, mem_scale(0))
                split(U_GV[i][0] + 2)
                gelu(U_GV[i][1], A_GV + i, gv, i)
                attend(att, 2 * i, mem_scale(0))
                split(U_GV[i][1] + 2)
            attend(att, 3, mem_scale(0))
            split(U_GU[0][0] + 2)
            attend(att, 4, mem_scale(0))
            gelu(U_GU[0][1], A_GU, gu, 0)
            split(U_GU[0][1] + 2)
            split(U_GU[1][0] + 2)
            gelu(U_GU[1][1], A_GU + 1, gu, 1)
            split(U_GU[1][1] + 2)

            def gated_hi(b):
                for t in range(NT):
                    t_hi(T_U + 2 * b + t, xTv[0][:, 4 * b:4 * b + 4, t * P:(t + 1) * P])

            def residual_in(j0):
                for j in (j0, j0 + 1):
                    act.wait_ge(a_free[j % 2], 2 * (j // 2 + 1))

            (a0, a1), (b0, b1), (c0, c1) = U_OUT[0]
            split(a0 + 2)
            gated_hi(0)
            split(a1 + 2)
            gated_hi(1)
            for u in (b0, b1, c0):
                split(u + 2)
            half_hi(T_FN[0], xTv, 0)
            residual_in(A_OUT[0])
            square_sums(N_FN[0], h)
            half_hi(T_FN[0], xTv, 1)
            split(c1 + 2)
            act.wait_ge(rstd_done, N_FN[0] + 1)
            for hf in range(2):
                gu_units, down_units = U_FF[hf]
                j0, tj = A_FF[hf], T_FH[hf]

                def hidden_hi(i, b0, n):
                    for t in range(NT):
                        t_hi(tj + 2 * i + t, wkv[0][:, b0:b0 + n, t * P:(t + 1) * P], n)

                for c in range(4):
                    g, u = gu_units[c]
                    act.wait_ge(used, g + 1)
                    if c or hf:
                        j = j0 + 2 * c - 1 if c else A_FF[0] + 7
                        act.wait_ge(a_free[j % 2], 2 * (j // 2 + 1))
                    j = j0 + 2 * c
                    for t in range(NT):
                        nc.scalar.activation(fsilu[:, t, :], A[j % 2][t][:, 0:FCH], ACT.Silu,
                                             scale=scaled(N_FN[0], t)).then_inc(a_free[j % 2], 1)
                    if c >= 2:
                        hidden_hi(c - 2, 4 * (c - 2), 4)
                    split(g + 2)
                    split(u + 2)
                hidden_hi(2, 8, 3)
                for c in range(4):
                    split(down_units[c] + 2)
                    if hf == 0 and c == 3:
                        act.wait_ge(rope_ang, 1)
                        nc.scalar.activation(cs[:, :, :, :], cs[:, :, :, :], ACT.Sin).then_inc(rope_cs, 1)
                    if hf == 1 and c == 0:
                        act.wait_ge(mem2_in, 16)
                        square_sums(N_MEM[1], memt)
                    if hf == 1 and c >= 2:
                        half_hi(T_MEM[1], xTv, c - 2)
            residual_in(A_FF[1] + 10)
            for j in (A_FF[1] + 8, A_FF[1] + 9):
                act.wait_ge(a_free[j % 2], 2 * (j // 2 + 1))
            square_sums(N_X[1], h)
            for i in range(2):
                two_heads(U_K1[i], A_K[1] + i, mk[:, 2 * i:2 * i + 2, :])
                split(U_K1[i] + 2)
            split(U_V1[0] + 2)
            half_hi(T_X[1], wkv, 0)
            act.wait_ge(used, U_V1[1] + 1)
            j = A_V[1]
            act_copy(mv[:, 0, :], A[j % 2][0][:, :]).then_inc(a_free[j % 2], 1)
            half_hi(T_X[1], wkv, 1)
            split(U_V1[1] + 2)
            act.wait_ge(rstd_done, N_X[1] + 1)
            for i in range(2):
                split(U_C[i][0] + 2)
                act.wait_ge(used, U_C[i][1] + 1)
                j = A_C + i
                nc.scalar.activation(lat[:, 0, i * 512:(i + 1) * 512], A[j % 2][0][:, :], ACT.Copy,
                                     scale=scaled(N_X[1], 0)).then_inc(a_free[j % 2], 1)
                split(U_C[i][1] + 2)
            for j in (A_C, A_C + 1):
                act.wait_ge(a_free[j % 2], 2 * (j // 2 + 1))
            square_sums(N_CQ, lat, QL)
            square_sums(N_CKV, lat, KVL, QL)
            for i in range(2):
                two_heads(U_Q1[i], A_Q[1] + i, mq[:, 2 * i:2 * i + 2, :])
                split(U_Q1[i] + 2)
            half_hi(T_C, xTv, 0)
            split(U_KR + 2)
            half_hi(T_C, xTv, 1)
            att = mem_heads[1]
            for i in range(4):
                u, j = U_UQ[i], A_UQ + i
                act.wait_ge(used, u + 1)
                act_copy(qn[:, 2 * i:2 * i + 2, :], A[j % 2][0][:, :].rearrange("p (h s) -> p h s", h=2)
                         ).then_inc(a_free[j % 2], 1)
                attend(att, i - 1, mem_scale(1))
                split(u + 2)

            def keys_values(i):
                u, j = U_UKV[i], A_UKV + 2 * i
                act.wait_ge(used, u + 1)
                act_copy(kn[:, 4 * i:4 * i + 2, :], A[j % 2][0][:, :].rearrange("p (h s) -> p h s", h=2)
                         ).then_inc(a_free[j % 2], 1)
                j += 1
                act_copy(lv[:, 0, i * 512:(i + 1) * 512], A[j % 2][0][:, :]).then_inc(a_free[j % 2], 1)

            act.wait_ge(s_done, S_MEM[1] + 4)
            keys_values(0)
            attend(att, 3, mem_scale(1))
            split(U_UKV[0] + 2)
            for t in range(NT):
                act_copy(qrT[:, :, t * P:(t + 1) * P], t_bank(T_ROPE + t)
                         ).then_inc(t_free[(T_ROPE + t) % 2], 2)
            j = T_ROPE + 2
            act.wait_ge(t_done, j + 1)
            act_copy(krT[:, :, :].rearrange("p b s -> p (b s)"), T[j % 2][:, :]).then_inc(t_free[j % 2], 2)
            attend(att, 4, mem_scale(1))
            att = lat_heads
            attend(att, -1, lat_scale)
            keys_values(1)
            split(U_UKV[1] + 2)
            attend(att, 0, lat_scale)
            (a0, a1), (b0, b1), (c0, c1) = U_OUT[1]
            for u, stages in ((a0, (1,)), (a1, (2, 3)), (b0, (4,)), (b1, (5, 6)), (c0, ())):
                act.wait_ge(used, u + 1)
                for g in stages:
                    attend(att, g, lat_scale)
                split(u + 2)

            def router_in(half):
                for t in range(NT):
                    j = T_FN[1] + 2 * half + t
                    act_copy(xnT[:, 4 * half:4 * half + 4, t * P:(t + 1) * P], t_bank(j)
                             ).then_inc(t_free[j % 2], 2)

            router_in(0)
            residual_in(A_OUT[1])
            square_sums(N_FN[1], h)
            router_in(1)
            split(c1 + 2)
            act.wait_ge(rstd_done, N_FN[1] + 1)
            for t in range(NT):
                nc.scalar.activation(xs[0][:, t, :], xn[:, t, :], ACT.Copy, scale=scaled(N_FN[1], t)
                                     ).then_inc(xs_hi, 1)
            act.wait_ge(rt_exp_in, 1)
            nc.scalar.activation(r1[:, 3, :], r1[:, 2, :], ACT.Exp).then_inc(rt_exp, 1)

            def gathered_hi(tj, it):
                for b in range(2):
                    j = tj + b
                    act.wait_ge(t_done, it * 8 + j + 1)
                    act_copy(xg[0][:, b * 512:(b + 1) * 512], T[j % 2][:, :]).then_inc(t_free[j % 2], 1)

            def output_hi(c, it):
                act.wait_ge(used, it * MU + U_MOE - 1 + c)
                act.wait_ge(scat_done, 1)
                act_copy(ys[0][:, c * 512:(c + 1) * 512], S[(S_MOE + c) % 2][:, :]).then_inc(y_hi, 1)

            def silu(c, ve):
                act.wait_ge(used, ve * MU + U_MOE + 4 * c + 2)
                j = A_MOE + 2 * c - 1
                act.wait_ge(a_free[j % 2], ve * 4 + 2 * (j // 2 + 1))
                j = A_MOE + 2 * c
                for b in range(2):
                    nc.scalar.activation(esilu[:, b * EN:(b + 1) * EN], A[j % 2][b][:, 0:EN], ACT.Silu
                                         ).then_inc(a_free[j % 2], 1)

            def hidden_hi(c, tj, ve):
                for n, blocks in enumerate((4, 3)):
                    j, at = tj + n, (7 * c + 4 * n) * P
                    act.wait_ge(t_done, ve * 8 + j + 1)
                    act_copy(hT[0][:, at:at + blocks * P], T[j % 2][:, 0:blocks * P]
                             ).then_inc(t_free[j % 2], 1)

            gathered_hi(T_MOE, 0)
            act.wait_ge(route_done, 1)
            rounds = act.value_load(nround[0:1, 0:1], min_val=E, max_val=2 * E)
            U, t1 = U_MOE, T_MOE + 2
            with act.Fori(0, rounds) as ve:
                output_hi(0, ve)
                output_hi(1, ve)
                split(U + 2, ve)
                split(U + 3, ve)
                silu(0, ve)
                split(U + 4, ve)
                for t in range(NT):
                    j = t1 + t
                    act.wait_ge(t_done, ve * 8 + j + 1)
                    act_copy(selT[:, t * P:(t + 1) * P], T[j % 2][:, 0:P]).then_inc(t_free[j % 2], 2)
                split(U + 5, ve)
                split(U + 6, ve)
                split(U + 7, ve)
                silu(1, ve)
                hidden_hi(0, t1 + 2, ve)
                split(U + 8, ve)
                split(U + 9, ve)
                hidden_hi(1, t1 + 4, ve)
                split(U + 10, ve)
                split(U + 11, ve)
                gathered_hi(t1 + 6, ve)
                with act.If(ve < rounds - 1):
                    split(U, ve + 1)
                    split(U + 1, ve + 1)
            output_hi(0, rounds)
            output_hi(1, rounds)
            for c in range(2):
                act.wait_ge(s_free[(S_MOE + 4 + c) % 2], rounds * 3 + (S_MOE + 4 + c) // 2 + 1)
            square_sums(N_FINAL, h, scratch=junk_end)

        @block.vector
        def _(dve):
            steps = [0]

            def step(ins):
                steps[0] += 1
                ins.then_inc(dve_step, 1)
                dve.wait_ge(dve_step, steps[0])

            def split(u, it=0):
                for i in range(2):
                    dve.wait_ge(hi_done, it * (2 * MU) + 2 * u + i + 1)
                    nc.vector.tensor_tensor(piece(lo, SPLIT, u, i), piece(raw, RAW, u, i),
                                            piece(hi, SPLIT, u, i).bitcast(F32), ALU.subtract
                                            ).then_inc(lo_done, 1)

            def normalise(n, src, dst, gain):
                dve.wait_ge(rstd_done, n + 1)
                for t in range(NT):
                    nc.vector.scalar_tensor_tensor(dst[:, t, :], src[:, t, :], rstd[:, n, t:t + 1],
                                                   gain[:, :], ALU.mult, ALU.mult).then_inc(xn_done, 1)

            def times_gain(half, gain):
                cols = slice(half * 512, (half + 1) * 512)
                for t in range(NT):
                    nc.vector.tensor_tensor(xn[:, t, cols], h[:, t, cols], gain[:, cols], ALU.mult
                                            ).then_inc(xn_done, 1)

            def memory_scale(layer):
                dve.wait_ge(rstd_done, N_X[layer] + 1)
                step(nc.vector.tensor_scalar(qscale[:, layer, :], rstd[:, N_X[layer], :], MEM_SCALE, None,
                                             ALU.mult))

            def t_lo(j, out, hi_part, n=4):
                dve.wait_ge(t_free[j % 2], 2 * (j // 2) + 1)
                nc.vector.tensor_tensor(out, T[j % 2][:, 0:n * P].rearrange("p (k s) -> p k s", k=n),
                                        hi_part.bitcast(F32), ALU.subtract).then_inc(t_free[j % 2], 1)

            def half_lo(j0, acts, half):
                for t in range(NT):
                    hi_part, lo_part = [a[:, 4 * half:4 * half + 4, t * P:(t + 1) * P] for a in acts]
                    t_lo(j0 + 2 * half + t, lo_part, hi_part)

            def maxima(a, g, scale_of, causal):
                if g + 1 < a.n:
                    t, hs, n = a.groups[g + 1]
                    gg = a.s0 + g + 1
                    bank = S[gg % 2][:, :].rearrange("p (h s) -> p h s", h=len(hs))
                    dve.wait_ge(s_done, gg + 1)
                    if causal:
                        own = bank[:, :, n - P:n]
                        step(nc.vector.tensor_tensor(own, own, cmask[:, :].unsqueeze(1).to_broadcast(
                            [P, len(hs), P]), ALU.add))
                    step(nc.vector.tensor_reduce(mx[:, gg, 0:len(hs)], bank, AX.X, ALU.max, negate=True))
                    nc.vector.tensor_scalar(nb[:, gg, 0:len(hs)], mx[:, gg, 0:len(hs)], scale_of(t), None,
                                            ALU.mult).then_inc(max_done, 1)
                if g >= 1:
                    t, hs, _ = a.groups[g - 1]
                    blocks = slice(a.cat0 + hs[0], a.cat0 + hs[0] + len(hs))
                    t_lo(a.t_out(g - 1), xTv[1][:, blocks, t * P:(t + 1) * P],
                         xTv[0][:, blocks, t * P:(t + 1) * P], len(hs))

            def probabilities(a, g):
                if g + 1 < a.n:
                    t, hs, n = a.groups[g + 1]
                    gg = a.s0 + g + 1
                    dve.wait_ge(s_free[gg % 2], gg // 2 + 1)
                    step(nc.vector.reciprocal(rden[:, gg, 0:len(hs)], den[:, gg, 0:len(hs)]))
                    p = PP[:, (g + 1) % 2, :].rearrange("p (h s) -> p h s", h=len(hs))
                    nc.vector.tensor_tensor(p, p, rden[:, gg, 0:len(hs)].unsqueeze(2).to_broadcast(
                        [P, len(hs), n]), ALU.mult).then_inc(prob_done, 1)

            def mem_stage(layer, g, u):
                maxima(mem_heads[layer], g, lambda t: qscale[:, layer, t:t + 1], False)
                if u:
                    split(u)
                probabilities(mem_heads[layer], g)

            def lat_stage(g):
                maxima(lat_heads, g, lambda t: MLA_SCALE, True)
                probabilities(lat_heads, g)

            def memory_values(layer, us):
                j = A_V[layer]
                dve.wait_ge(used, us[1] + 1)
                nc.vector.tensor_copy(mv[:, 1, :], A[j % 2][1][:, :]).then_inc(a_free[j % 2], 1)

            def add_residual(j, c0, n, u):
                dve.wait_ge(used, u + 1)
                for t in range(NT):
                    nc.vector.tensor_tensor(h[:, t, c0:c0 + n], A[j % 2][t][:, 0:n], h[:, t, c0:c0 + n],
                                            ALU.add).then_inc(a_free[j % 2], 1)

            def added(j):
                dve.wait_ge(a_free[j % 2], 2 * (j // 2 + 1))

            dve.wait_ge(gb2_first, 16)
            dve.wait_ge(x_in, 16)
            times_gain(0, GB2)
            times_gain(1, GB2)
            half_lo(T_X[0], xTv, 0)
            split(0)
            half_lo(T_X[0], xTv, 1)
            split(1)
            dve.wait_ge(gb1_first, 16)
            dve.wait_ge(mem_in, 16)
            normalise(N_MEM[0], memt, memt, GB1)
            split(U_Q0[0] + 2)
            split(U_Q0[1] + 2)
            half_lo(T_MEM[0], wkv, 0)
            half_lo(T_MEM[0], wkv, 1)
            dve.wait_ge(consts, 1)
            dve.wait_ge(ssum_done, 2 * N_X[0] + 2)
            for i in range(2):
                j = T_WS + i
                dve.wait_ge(t_done, j + 1)
                nc.vector.tensor_tensor(wsT[:, 4 * i:4 * i + 4, :],
                                        T[j % 2][:, :].rearrange("p (k s) -> p k s", k=4),
                                        tri[:, :].unsqueeze(1).to_broadcast([P, 4, P]), ALU.mult
                                        ).then_inc(t_free[j % 2], 2)
            split(U_K0[0] + 2)
            split(U_K0[1] + 2)
            split(U_V0[0] + 2)
            memory_values(0, U_V0)
            split(U_V0[1] + 2)
            memory_scale(0)
            mem_stage(0, -1, U_GV[0][0] + 2)
            mem_stage(0, 0, U_GV[0][1] + 2)
            mem_stage(0, 1, U_GV[1][0] + 2)
            mem_stage(0, 2, U_GV[1][1] + 2)
            for j in (A_GV, A_GV + 1):
                dve.wait_ge(a_free[j % 2], 2 * (j // 2 + 1))
            for t in range(NT):
                step(nc.vector.tensor_tensor(junk_v, gv[:, t, :], gv[:, t, :], ALU.mult))
                red = nc.vector.tensor_reduce(vss[:, t, :], junk_v.rearrange("p (g c) -> p g c", g=NG),
                                              AX.X, ALU.add)
                if t == 0:
                    step(red)
                else:
                    red.then_inc(vss_done, 1)
            mem_stage(0, 3, U_GU[0][0] + 2)
            dve.wait_ge(vrs_done, 1)
            dve.wait_ge(gb1_in, 16)
            for t in range(NT):
                v = gv[:, t, :].rearrange("p (g c) -> p g c", g=NG)
                step(nc.vector.tensor_tensor(v, v, vrs[:, t, :].unsqueeze(2).to_broadcast([P, NG, P]),
                                             ALU.mult))
                nc.vector.tensor_tensor(gv[:, t, :], gv[:, t, :], GB1[:, :], ALU.mult).then_inc(vn_done, 1)
            mem_stage(0, 4, U_GU[0][1] + 2)
            split(U_GU[1][0] + 2)
            split(U_GU[1][1] + 2)
            dve.wait_ge(gbs_in, 16)
            for j in (A_GU, A_GU + 1):
                dve.wait_ge(a_free[j % 2], 2 * (j // 2 + 1))
            for jj in range(2):
                j = A_MIX + jj
                dve.wait_ge(mixed_done, jj + 1)
                for i in range(4):
                    g = 4 * jj + i
                    u_g = gu[:, :, g * P:(g + 1) * P]
                    mixed = A[j % 2][i // 2][:, (i % 2) * SEQ:(i % 2 + 1) * SEQ]
                    last = nc.vector.scalar_tensor_tensor(u_g, mixed.rearrange("p (t c) -> p t c", t=NT),
                                                          gbs[:, g:g + 1], u_g, ALU.add, ALU.mult)
                last.then_inc(a_free[j % 2], 2)

            def gated_lo(b):
                for t in range(NT):
                    hi_part, lo_part = [a[:, 4 * b:4 * b + 4, t * P:(t + 1) * P] for a in xTv]
                    t_lo(T_U + 2 * b + t, lo_part, hi_part)

            (a0, a1), (b0, b1), (c0, c1) = U_OUT[0]
            split(a0 + 2)
            gated_lo(0)
            split(a1 + 2)
            gated_lo(1)
            split(b0 + 2)
            split(b1 + 2)
            dve.wait_ge(gb2_in, 16)
            add_residual(A_OUT[0], 0, 512, c0)
            added(A_OUT[0])
            times_gain(0, GB2)
            split(c0 + 2)
            half_lo(T_FN[0], xTv, 0)
            add_residual(A_OUT[0] + 1, 512, 512, c1)
            added(A_OUT[0] + 1)
            times_gain(1, GB2)
            half_lo(T_FN[0], xTv, 1)
            split(c1 + 2)
            dve.wait_ge(rstd_done, N_FN[0] + 1)

            def rotary_angles():
                dve.wait_ge(rope_in, 32)
                step(nc.vector.tensor_copy(posf[:, :], posi[:, :]))
                ang, turns = rt[:, 0:4].rearrange("p i t e -> p (i t e)"), rt[:, 4:8].rearrange(
                    "p i t e -> p (i t e)")
                for t in range(NT):
                    step(nc.vector.tensor_scalar(ang[:, t * 32:(t + 1) * 32], freq[:, :], posf[:, t:t + 1],
                                                 None, ALU.mult))
                for i, quarter in enumerate((np.pi / 2, 0.0)):
                    step(nc.vector.tensor_scalar(turns, ang, float(quarter), float(1 / TWO_PI), ALU.add,
                                                 ALU.mult))
                    step(nc.vector.tensor_scalar(turns, turns, MAGIC, None, ALU.add))
                    step(nc.vector.tensor_scalar(turns, turns, -MAGIC, None, ALU.add))
                    csv = cs[:, i].rearrange("p t r -> p (t r)")
                    src = ang
                    for c in two_pi_parts():
                        step(nc.vector.scalar_tensor_tensor(csv, turns, -c, src, ALU.mult, ALU.add))
                        src = csv
                    step(nc.vector.tensor_scalar(csv, csv, float(quarter), 3.1415925, ALU.add, ALU.min))
                    last = nc.vector.tensor_scalar(csv, csv, -3.1415925, None, ALU.max)
                    if i == 0:
                        step(last)
                last.then_inc(rope_ang, 1)

            for hf in range(2):
                gu_units, down_units = U_FF[hf]
                j0, tj = A_FF[hf], T_FH[hf]

                def hidden_lo(i, b0, n):
                    for t in range(NT):
                        hi_part, lo_part = [a[:, b0:b0 + n, t * P:(t + 1) * P] for a in wkv]
                        t_lo(tj + 2 * i + t, lo_part, hi_part, n)

                for c in range(4):
                    g, u = gu_units[c]
                    if c >= 2:
                        hidden_lo(c - 2, 4 * (c - 2), 4)
                    split(g + 2)
                    dve.wait_ge(used, u + 1)
                    jg, ju = j0 + 2 * c, j0 + 2 * c + 1
                    dve.wait_ge(a_free[jg % 2], 2 * (jg // 2 + 1))
                    for t in range(NT):
                        nc.vector.scalar_tensor_tensor(fhid[:, t, c * FCH:(c + 1) * FCH],
                                                       A[ju % 2][t][:, 0:FCH], rstd[:, N_FN[0], t:t + 1],
                                                       fsilu[:, t, :], ALU.mult, ALU.mult
                                                       ).then_inc(a_free[ju % 2], 1)
                    split(u + 2)
                hidden_lo(2, 8, 3)
                for c in range(4):
                    add_residual(j0 + 8 + c, c * 256, 256, down_units[c])
                    if hf == 1 and c == 1:
                        dve.wait_ge(gb1_in, 32)
                        dve.wait_ge(mem2_in, 16)
                        normalise(N_MEM[1], memt, memt, GB1)
                    split(down_units[c] + 2)
                    if hf == 0 and c == 1:
                        rotary_angles()
                    if hf == 1 and c >= 2:
                        half_lo(T_MEM[1], xTv, c - 2)

            dve.wait_ge(gb2_in, 32)
            for c in range(4):
                added(A_FF[1] + 8 + c)
            times_gain(0, GB2)
            times_gain(1, GB2)
            split(U_K1[0] + 2)
            split(U_K1[1] + 2)
            split(U_V1[0] + 2)
            half_lo(T_X[1], wkv, 0)
            memory_values(1, U_V1)
            half_lo(T_X[1], wkv, 1)
            split(U_V1[1] + 2)
            memory_scale(1)
            for i in range(2):
                split(U_C[i][0] + 2)
                dve.wait_ge(used, U_C[i][1] + 1)
                j = A_C + i
                nc.vector.tensor_scalar(lat[:, 1, i * 512:(i + 1) * 512], A[j % 2][1][:, :],
                                        rstd[:, N_X[1], 1:2], None, ALU.mult).then_inc(a_free[j % 2], 1)
                split(U_C[i][1] + 2)
            dve.wait_ge(rstd_done, N_CKV + 1)
            dve.wait_ge(gb1_in, 64)
            for t in range(NT):
                for n, c0, c1 in ((N_CQ, 0, QL), (N_CKV, QL, D)):
                    last = nc.vector.scalar_tensor_tensor(lat[:, t, c0:c1], lat[:, t, c0:c1],
                                                          rstd[:, n, t:t + 1], GB1[:, c0:c1],
                                                          ALU.mult, ALU.mult)
                last.then_inc(c_ready, 1)
            split(U_Q1[0] + 2)
            split(U_Q1[1] + 2)
            half_lo(T_C, xTv, 0)
            dve.wait_ge(used, U_KR + 1)
            for t in range(NT):
                nc.vector.tensor_scalar(kraw[:, t, :], A[A_KR % 2][t][:, 0:ROPE],
                                        rstd[:, N_X[1], t:t + 1], None, ALU.mult
                                        ).then_inc(a_free[A_KR % 2], 1)
            split(U_KR + 2)
            half_lo(T_C, xTv, 1)
            added(A_KR)

            def rotate(src, dst, scratch, heads):
                c, s_ = [cs[:, i].unsqueeze(2).to_broadcast([P, NT, heads, 32]) for i in range(2)]
                x1, x2 = src[:, :, :, 0:32], src[:, :, :, 32:64]
                for i, (a, b) in enumerate(((x1, c), (x2, s_), (x2, c), (x1, s_))):
                    step(nc.vector.tensor_tensor(scratch[i], a, b, ALU.mult))
                step(nc.vector.tensor_tensor(dst[:, :, :, 0:32], scratch[0], scratch[1], ALU.subtract))
                return nc.vector.tensor_tensor(dst[:, :, :, 32:64], scratch[2], scratch[3], ALU.add)

            small = rt[:, 0:8].rearrange("p i t e -> p (i t e)").rearrange("p (a t o r) -> p a t o r", a=2, t=NT, o=1)
            small2 = rt[:, 8:12].rearrange("p i t e -> p (i t e)").rearrange("p (t o r) -> p t o r", t=NT, o=1)
            small3 = rsm[:, :].rearrange("p (t o r) -> p t o r", t=NT, o=1)
            dve.wait_ge(rope_cs, 1)
            step(nc.vector.memset(kr[:, :, :, :], 0.0))
            for b in range(2):
                last = rotate(kraw[:, :, :].unsqueeze(2), kr[:, b, :, b * 64:(b + 1) * 64].unsqueeze(2),
                              [small[:, 0], small[:, 1], small2, small3], 1)
                if b == 0:
                    step(last)
            last.then_inc(rope_done, 1)
            for i in range(4):
                u, j = U_UQ[i], A_UQ + i
                dve.wait_ge(used, u + 1)
                nc.vector.tensor_copy(qr[:, :, 2 * i:2 * i + 2, :],
                                      A[j % 2][1][:, 0:2 * P].rearrange("p (t h r) -> p t h r", t=NT, h=2)
                                      ).then_inc(a_free[j % 2], 1)
                mem_stage(1, i - 1, u + 2)
                if i % 2:
                    added(j - 1)
                    added(j)
                    if i == 3:
                        dve.wait_ge(rope_done, 2)
                    heads4 = qr[:, :, 2 * i - 2:2 * i + 2, :]
                    rotate(heads4, heads4, [tmp[:, i_] for i_ in range(4)], 4).then_inc(rope_done, 1)

            def keys_values(i):
                u, j = U_UKV[i], A_UKV + 2 * i
                dve.wait_ge(used, u + 1)
                nc.vector.tensor_copy(kn[:, 4 * i + 2:4 * i + 4, :],
                                      A[j % 2][1][:, :].rearrange("p (h s) -> p h s", h=2)
                                      ).then_inc(a_free[j % 2], 1)
                j += 1
                nc.vector.tensor_copy(lv[:, 1, i * 512:(i + 1) * 512], A[j % 2][1][:, :]
                                      ).then_inc(a_free[j % 2], 1)

            dve.wait_ge(rope_done, 3)
            keys_values(0)
            mem_stage(1, 3, 0)
            mem_stage(1, 4, U_UKV[0] + 2)
            lat_stage(-1)
            keys_values(1)
            split(U_UKV[1] + 2)
            lat_stage(0)
            (a0, a1), (b0, b1), (c0, c1) = U_OUT[1]
            for u, stages in ((a0, (1,)), (a1, (2, 3)), (b0, (4,)), (b1, (5, 6))):
                for g in stages:
                    lat_stage(g)
                split(u + 2)
            dve.wait_ge(gb1_in, 80)
            add_residual(A_OUT[1], 0, 512, c0)
            added(A_OUT[1])
            times_gain(0, GB1)
            split(c0 + 2)
            add_residual(A_OUT[1] + 1, 512, 512, c1)
            added(A_OUT[1] + 1)
            times_gain(1, GB1)
            split(c1 + 2)
            for t in range(NT):
                dve.wait_ge(xs_hi, t + 1)
                nc.vector.scalar_tensor_tensor(xs[1][:, t, :], xn[:, t, :], rstd[:, N_FN[1], t:t + 1],
                                               xs[0][:, t, :].bitcast(F32), ALU.mult, ALU.subtract
                                               ).then_inc(xs_done, 1)

            def bc(a):
                return a.unsqueeze(2).to_broadcast([P, NT, E])

            mask, lg, eq, oh1, oh2, g = (rt[:, i] for i in range(6))
            j = A_RT
            dve.wait_ge(rout_in, 32)
            dve.wait_ge(route_mm, 1)
            for t in range(NT):
                last = nc.vector.scalar_tensor_tensor(lg[:, t, :], A[j % 2][t][:, 0:E],
                                                      rstd[:, N_FN[1], t:t + 1], br[:, :], ALU.mult, ALU.add)
            last.then_inc(a_free[j % 2], 2)
            dve.wait_ge(a_free[j % 2], 2 * (j // 2 + 1))
            pr = prio[:, :].unsqueeze(1).to_broadcast([P, NT, E])
            for i, oh in enumerate((oh1, oh2)):
                step(nc.vector.tensor_reduce(r1[:, i, :], lg, AX.X, ALU.max))
                step(nc.vector.tensor_tensor(eq, lg, bc(r1[:, i, :]), ALU.is_equal))
                step(nc.vector.tensor_tensor(eq, eq, pr, ALU.mult))
                step(nc.vector.tensor_reduce(r1[:, 9, :], eq, AX.X, ALU.max))
                step(nc.vector.tensor_tensor(oh, eq, bc(r1[:, 9, :]), ALU.is_equal))
                if i == 0:
                    step(nc.vector.scalar_tensor_tensor(lg, oh, NEG, lg, ALU.mult, ALU.add))
            nc.vector.tensor_tensor(r1[:, 2, :], r1[:, 1, :], r1[:, 0, :], ALU.subtract).then_inc(rt_exp_in, 1)
            nc.vector.tensor_tensor(mask, oh1, oh2, ALU.add).then_inc(mask_done, 1)
            dve.wait_ge(rt_exp, 1)
            step(nc.vector.tensor_scalar(r1[:, 4, :], r1[:, 3, :], 1.0, None, ALU.add))
            step(nc.vector.reciprocal(r1[:, 5, :], r1[:, 4, :]))
            step(nc.vector.tensor_tensor(r1[:, 6, :], r1[:, 3, :], r1[:, 5, :], ALU.mult))
            step(nc.vector.tensor_tensor(oh1, oh1, bc(r1[:, 5, :]), ALU.mult))
            step(nc.vector.tensor_tensor(oh2, oh2, bc(r1[:, 6, :]), ALU.mult))
            step(nc.vector.memset(gate_of[:, :, :], 0.0))
            step(nc.vector.memset(slot_of[:, :, :], -1.0))
            for r in range(2):
                step(nc.vector.tensor_tensor(gate_of[:, :, 1 + r * E:1 + (r + 1) * E], oh1, oh2, ALU.add))
            for a in (selT[:, :], ys[0], ys[1]):
                last = nc.vector.memset(a.bitcast(F32), 0.0)
            last.then_inc(moe_const, 1)
            j = A_RT + 1
            dve.wait_ge(route_mm, 2)
            step(nc.vector.tensor_reduce(r1[:, 7, 0:1], A[j % 2][0][:, E:2 * E], AX.X, ALU.max))
            step(nc.vector.tensor_scalar(r1[:, 7, 1:2], r1[:, 7, 0:1], P + 0.5, float(E), ALU.is_gt, ALU.mult))
            nc.vector.tensor_scalar(nround[:, :], r1[:, 7, 1:2], float(E), None, ALU.add).then_inc(route_done, 1)
            for t in range(NT):
                step(nc.vector.scalar_tensor_tensor(slot_of[:, t, 0:E], A[j % 2][t][:, 0:E], 1e4,
                                                    mask[:, t, :], ALU.add, ALU.mult))
            step(nc.vector.tensor_scalar(slot_of[:, :, E:2 * E], slot_of[:, :, 0:E], -1e4 - P, None, ALU.add))
            last = nc.vector.tensor_scalar(slot_of[:, :, 0:E], slot_of[:, :, 0:E], -1e4, None, ALU.add)
            last.then_inc(a_free[j % 2], 2)
            dve.wait_ge(a_free[j % 2], 2 * (j // 2 + 1))

            def one_hot(ve):
                for t in range(NT):
                    last = nc.vector.tensor_scalar(sel[:, t * P:(t + 1) * P], iota,
                                                   slot_of[:, t, bass.ds(ve, 1)], None, ALU.is_equal)
                last.then_inc(sel_done, 1)

            def gathered_lo(tj, it):
                for b in range(2):
                    j, cols = tj + b, slice(b * 512, (b + 1) * 512)
                    dve.wait_ge(t_free[j % 2], it * 8 + 2 * (j // 2) + 1)
                    nc.vector.tensor_tensor(xg[1][:, cols], T[j % 2][:, :], xg[0][:, cols].bitcast(F32),
                                            ALU.subtract).then_inc(t_free[j % 2], 1)

            def output_lo(c, it):
                dve.wait_ge(y_hi, it * 2 + c + 1)
                cols = slice(c * 512, (c + 1) * 512)
                nc.vector.tensor_tensor(ys[1][:, cols], S[(S_MOE + c) % 2][:, :], ys[0][:, cols].bitcast(F32),
                                        ALU.subtract).then_inc(s_free[(S_MOE + c) % 2], 1)

            def add_outputs(t, ve):
                for c in range(2):
                    s = S_MOE + 2 + 2 * t + c
                    dve.wait_ge(scat_done, ve * 4 + 2 * t + c + 2)
                    cols = slice(c * 512, (c + 1) * 512)
                    nc.vector.scalar_tensor_tensor(h[:, t, cols], S[s % 2][:, :],
                                                   gate_of[:, t, bass.ds(ve, 1)], h[:, t, cols],
                                                   ALU.mult, ALU.add).then_inc(s_free[s % 2], 1)

            def multiply(c, ve, t_before):
                jg, ju = A_MOE + 2 * c, A_MOE + 2 * c + 1
                dve.wait_ge(used, ve * MU + U_MOE + 4 * c + 4)
                dve.wait_ge(a_free[jg % 2], ve * 4 + 2 * (jg // 2 + 1))
                dve.wait_ge(t_done, ve * 8 + t_before)
                for b in range(2):
                    cols = slice(b * EN, (b + 1) * EN)
                    nc.vector.tensor_tensor(ehid[:, cols], A[ju % 2][b][:, 0:EN], esilu[:, cols],
                                            ALU.mult).then_inc(a_free[ju % 2], 1)

            def hidden_lo(c, tj, ve):
                for n, blocks in enumerate((4, 3)):
                    j, at = tj + n, (7 * c + 4 * n) * P
                    dve.wait_ge(t_free[j % 2], ve * 8 + 2 * (j // 2) + 1)
                    nc.vector.tensor_tensor(hT[1][:, at:at + blocks * P], T[j % 2][:, 0:blocks * P],
                                            hT[0][:, at:at + blocks * P].bitcast(F32), ALU.subtract
                                            ).then_inc(t_free[j % 2], 1)

            dve.wait_ge(consts, 2)
            one_hot(0)
            gathered_lo(T_MOE, 0)
            rounds = dve.value_load(nround[0:1, 0:1], min_val=E, max_val=2 * E)
            U, t1 = U_MOE, T_MOE + 2
            with dve.Fori(0, rounds) as ve:
                output_lo(0, ve)
                output_lo(1, ve)
                split(U + 2, ve)
                add_outputs(0, ve)
                split(U + 3, ve)
                add_outputs(1, ve)
                split(U + 4, ve)
                multiply(0, ve, t1)
                split(U + 5, ve)
                dve.wait_ge(t_done, ve * 8 + t1 + 2)
                one_hot(ve + 1)
                split(U + 6, ve)
                split(U + 7, ve)
                hidden_lo(0, t1 + 2, ve)
                split(U + 8, ve)
                multiply(1, ve, t1 + 4)
                split(U + 9, ve)
                hidden_lo(1, t1 + 4, ve)
                split(U + 10, ve)
                split(U + 11, ve)
                gathered_lo(t1 + 6, ve)
                with dve.If(ve < rounds - 1):
                    split(U, ve + 1)
                    split(U + 1, ve + 1)
            output_lo(0, rounds)
            output_lo(1, rounds)
            add_outputs(0, rounds)
            add_outputs(1, rounds)
            dve.wait_ge(gb2_in, 48)
            normalise(N_FINAL, h, xn, GB2)

        @block.gpsimd
        def _(pool):
            steps = [0]

            def step(ins):
                steps[0] += 1
                ins.then_inc(pool_step, 1)
                pool.wait_ge(pool_step, steps[0])

            def gain(dst, vector, done, n=D):
                pool.dma_start(dst, vector.partition_broadcast(P)).then_inc(done, 16)

            def inverse_rms(out, sums, n_values, done, cols):
                step(nc.gpsimd.tensor_scalar(out, sums, 1.0 / n_values, EPS, ALU.mult, ALU.add))
                nc.gpsimd.tensor_tensor(out, out, mhalf[:, 0:cols], ALU.pow).then_inc(done, 1)

            def norm(n, n_values=D):
                pool.wait_ge(ssum_done, 2 * n + 2)
                inverse_rms(rstd[:, n, :], ssum[:, n, :], n_values, rstd_done, NT)

            step(nc.gpsimd.memset(mhalf[:, :], -0.5))
            for a, v in ((ident, 0.0), (ones, 1.0), (tri, 1.0), (tris, 1.0), (cmask, 0.0)):
                step(nc.gpsimd.memset(a[:, :], v))
            step(nc.gpsimd.affine_select(out=ident[:, :], in_=ident[:, :], pattern=[[-1, P]],
                                         compare_op=ALU.not_equal, fill=1.0, base=0, channel_multiplier=1))
            step(nc.gpsimd.affine_select(out=tri[:, :], in_=tri[:, :], pattern=[[1, P]],
                                         compare_op=ALU.is_ge, fill=0.0, base=0, channel_multiplier=-1))
            step(nc.gpsimd.affine_select(out=tris[:, :], in_=tris[:, :], pattern=[[1, P]],
                                         compare_op=ALU.is_gt, fill=0.0, base=0, channel_multiplier=-1))
            step(nc.gpsimd.affine_select(out=cmask[:, :], in_=cmask[:, :], pattern=[[-1, P]],
                                         compare_op=ALU.is_ge, fill=NEG, base=0, channel_multiplier=1))
            nc.gpsimd.iota(prio[:, :], pattern=[[-1, E]], base=E, channel_multiplier=0,
                           allow_small_or_imprecise_dtypes=True).then_inc(consts, 1)
            norm(N_MEM[0])
            norm(N_X[0])
            pool.wait_ge(xn_done, XN_OF["mem0"])
            gain(GB2[:, :], ffn_norm[0], gb2_in)
            pool.wait_ge(xn_done, XN_OF["fn0"])
            gain(GB1[:, :], gm_v_norm[0], gb1_in)
            pool.wait_ge(vss_done, 1)
            inverse_rms(vrs[:, :, :].rearrange("p t g -> p (t g)"), vss[:, :, :].rearrange("p t g -> p (t g)"),
                        P, vrs_done, NT * NG)
            pool.wait_ge(vn_done, NT)
            gain(GB1[:, :], mem_norm[1], gb1_in)
            norm(N_FN[0])
            pool.wait_ge(xn_done, XN_OF["mem1"])
            gain(GB2[:, :], attn_norm[1], gb2_in)
            j = A_FF[1] + 7
            pool.wait_ge(a_free[j % 2], 2 * (j // 2 + 1))
            pool.dma_start(memt, mem[0].rearrange("(t p) d -> p t d", p=P)).then_inc(mem2_in, 16)
            norm(N_MEM[1])
            norm(N_X[1])
            pool.wait_ge(xn_done, XN_OF["x1"])
            gain(GB1[:, 0:QL], mla_q_norm[0], gb1_in)
            gain(GB1[:, QL:D], mla_kv_norm[0], gb1_in)
            norm(N_CQ, QL)
            norm(N_CKV, KVL)
            pool.wait_ge(t_done, T_ROPE + 2)
            gain(GB1[:, :], ffn_norm[1], gb1_in)
            pool.wait_ge(t_done, T_FN[1])
            gain(GB2[:, :], final_norm, gb2_in)
            norm(N_FN[1])
            nc.gpsimd.iota(iota, pattern=[[1, P]], base=0, channel_multiplier=0,
                           allow_small_or_imprecise_dtypes=True).then_inc(consts, 1)
            norm(N_FINAL)


INPUTS = ["x", "mem", "positions", "attn_norm", "mem_norm", "w_mem_kv", "ffn_norm", "final_norm",
          "gm_w_in", "gm_v_norm", "gm_w_s", "gm_b_s", "gm_w_out",
          "mla_w_in", "mla_q_norm", "mla_w_uq", "mla_kv_norm", "mla_w_ukv", "mla_w_out",
          "ff_w_gate", "ff_w_up", "ff_w_down",
          "moe_w_router", "moe_b_router", "moe_w_gate", "moe_w_up", "moe_w_down"]


def kernel(**inputs):
    import concourse.bacc as bacc
    from concourse.bass_utils import run_bass_kernel_spmd

    nc = bacc.Bacc("TRN2", target_bir_lowering=False, num_devices=1)
    arrays = {f"in_{name}": np.ascontiguousarray(inputs[name]) for name in INPUTS}
    steps = np.arange(0, ROPE, 2, dtype=np.float32) / np.float32(ROPE)
    arrays["in_rope_freq"] = (1.0 / np.float32(10000.0) ** steps).astype(np.float32)
    args = [nc.dram_tensor(name, a.shape, mybir.dt.from_np(a.dtype), kind="ExternalInput").ap()
            for name, a in arrays.items()]
    out = nc.dram_tensor("out_0", (1, SEQ, D), F32, kind="ExternalOutput").ap()
    build(nc, *args, out)
    got = run_bass_kernel_spmd(nc, [arrays], core_ids=[0])
    return got.results[0]["out_0"]
```

```python
import numpy as np

import concourse.bass as bass
from concourse import mybir
from contextlib import ExitStack

F32 = mybir.dt.float32
F32R = mybir.dt.float32r
I32 = mybir.dt.int32
ALU = mybir.AluOpType
ACT = mybir.ActivationFunctionType
AX = mybir.AxisListType

P = 128
D = 1024
SEQ = 256
NT = SEQ // P
KD = D // P
MH = 4
MEMW = MH * P
GM = 1024
NG = GM // P
HEADS = 8
NOPE, ROPE = 128, 64
QK = NOPE + ROPE
QL, KVL = 768, 256
FF = 2816
FHALF = FF // 2
FB = FHALF // P
FCH = FHALF // 4
E = 8
FE = 1792
EB = FE // P
ECH = FE // 2
EN = ECH // 2
EPS = 1e-6
MEM_SCALE = float(P) ** -0.5
MLA_SCALE = float(QK) ** -0.5
NEG = -1e30
MAGIC = 12582912.0
TWO_PI = 2 * np.pi
CAT = KD + MH

C_CHUNKS = ((0, 384), (384, 352), (736, 352))
OUT_ROWS = (KD, 0, 4)

UNIT = 3584
RAW, SPLIT = 3, 2


def two_pi_parts():
    parts, rest = [], TWO_PI
    for _ in range(3):
        m, e = np.frexp(rest)
        part = float(np.floor(m * 512) / 512 * 2.0 ** int(e))
        parts.append(part)
        rest -= part
    return parts + [float(np.float32(rest))]


def build(nc, x, mem, positions, attn_norm, mem_norm, w_mem_kv, ffn_norm, final_norm,
          gm_w_in, gm_v_norm, gm_w_s, gm_b_s, gm_w_out,
          mla_w_in, mla_q_norm, mla_w_uq, mla_kv_norm, mla_w_ukv, mla_w_out,
          ff_w_gate, ff_w_up, ff_w_down,
          moe_w_router, moe_b_router, moe_w_gate, moe_w_up, moe_w_down, rope_freq, out):
    def rows(w, k0, k, c0, n):
        return w[k0 * P:(k0 + k) * P, c0:c0 + n].rearrange("(k p) n -> p k n", p=P)

    units = []

    def add(w, k0, k, c0, n):
        units.append((rows(w, k0, k, c0, n), k, n))
        return len(units) - 1

    def add_wide(w, c0):
        return [add(w, 0, 4, c0, 512), add(w, 4, 4, c0, 512)]

    def add_kv(layer):
        w = w_mem_kv[layer]
        return [add(w, 0, KD, 0, 256), add(w, 0, KD, 256, 256)], add_wide(w, MEMW)

    def add_out(w):
        return [[add(w, k0, 4, c, 512) for c in (0, 512)] for k0 in OUT_ROWS]

    w = gm_w_in[0]
    U_Q0 = [add(w, 0, KD, 2 * GM + c, 256) for c in (0, 256)]
    U_GV = [add_wide(w, GM)]
    U_K0, U_V0 = add_kv(0)
    U_GV.append(add_wide(w, GM + 512))
    U_GU = [add_wide(w, c) for c in (0, 512)]
    U_O0 = add_out(gm_w_out[0])
    U_FF = []
    for h in range(2):
        gu = [(add(ff_w_gate[0], 0, KD, h * FHALF + c * FCH, FCH),
               add(ff_w_up[0], 0, KD, h * FHALF + c * FCH, FCH)) for c in range(4)]
        U_FF.append((gu, [add(ff_w_down[0], h * FB, FB, c * 256, 256) for c in range(4)]))
    U_K1, U_V1 = add_kv(1)
    w = mla_w_in[0]
    U_C = [add(w, 0, KD, c0, n) for c0, n in C_CHUNKS]
    U_Q1 = [add(w, 0, KD, QL + KVL + ROPE + c, 256) for c in (0, 256)]
    U_QR = len(units)
    by_head = mla_w_uq[0].rearrange("(k p) (h c) -> p k h c", p=P, h=HEADS)
    for h0, n_heads, c0, c1 in ((0, HEADS, NOPE, QK), (0, 4, 0, NOPE), (4, 4, 0, NOPE)):
        units.append((by_head[:, :, h0:h0 + n_heads, c0:c1], QL // P, n_heads * (c1 - c0)))
    U_UQ = [U_QR + 1, U_QR + 2]
    U_UKV = [add(mla_w_ukv[0], 0, KVL // P, c * 1024, 1024) for c in range(2)]
    U_O1 = add_out(mla_w_out[0])
    U_OUT = (U_O0, U_O1)
    U_MOE = len(units)
    MU = 12
    moe_shape = [(4, ECH)] * 8 + [(7, 512)] * 4

    def shape_of(u):
        return units[u][1:] if u < U_MOE else moe_shape[(u - U_MOE) % MU]

    def numbered(*jobs):
        first, n = {}, 0
        for name, count in jobs:
            first[name] = n
            n += count
        return first

    A_OF = numbered(("q0", 2), ("gv0", 1), ("k0", 2), ("v0", 1), ("gv1", 1), ("gu", 2), ("mix", 2),
                    ("out0", 2),
                    ("ff0", 12), ("ff1", 12), ("k1", 2), ("v1", 1), ("c", 3), ("q1", 2),
                    ("uq", 3), ("ukv", 4), ("out1", 2), ("router", 2), ("experts", 0))
    A_Q = [A_OF["q0"], A_OF["q1"]]
    A_K = [A_OF["k0"], A_OF["k1"]]
    A_V = [A_OF["v0"], A_OF["v1"]]
    A_GV, A_GU = (A_OF["gv0"], A_OF["gv1"]), A_OF["gu"]
    A_MIX = A_OF["mix"]
    A_OUT = [A_OF["out0"], A_OF["out1"]]
    A_FF = [A_OF["ff0"], A_OF["ff1"]]
    A_C = A_OF["c"]
    A_UQ = A_OF["uq"]
    A_UKV = A_OF["ukv"]
    A_RT = A_OF["router"]
    A_MOE = A_OF["experts"]
    T_OF = numbered(("x0", 4), ("mem0", 4), ("ws", 2), ("att0", 8), ("u", 4), ("fn0", 4),
                    ("fh0", 6), ("fh1", 6), ("mem1", 4), ("x1", 4), ("c", 4), ("att1", 7), ("rope", 3),
                    ("att1 last", 1), ("lat", 12), ("fn1", 4), ("experts", 0))
    T_X = [T_OF["x0"], T_OF["x1"]]
    T_MEM = [T_OF["mem0"], T_OF["mem1"]]
    T_WS, T_U = T_OF["ws"], T_OF["u"]
    T_FN = [T_OF["fn0"], T_OF["fn1"]]
    T_FH = [T_OF["fh0"], T_OF["fh1"]]
    T_C, T_ROPE = T_OF["c"], T_OF["rope"]
    T_MOE = T_OF["experts"]
    S_MEM = [0, 4]
    S_LAT = 8
    S_MOE = 14
    XN_OF = numbered(("x0", 4), ("mem0", 2), ("fn0", 4), ("mem1", 2), ("x1", 4), ("fn1", 4), ("final", NT))
    N_MEM, N_X, N_FN, N_CQ, N_CKV, N_FINAL = (0, 3), (1, 4), (2, 7), 5, 6, 8

    MEM_GROUPS = [(t, (2 * i, 2 * i + 1), SEQ) for t in range(NT) for i in range(2)]
    LAT_GROUPS = [(t, hs, n) for i in (0, 4)
                  for t, hs, n in ((0, tuple(range(i, i + 4)), P),
                                   (1, (i, i + 1), SEQ), (1, (i + 2, i + 3), SEQ))]

    class Heads:

        def __init__(self, groups, s0, t0, last_out, cat0, values):
            self.groups, self.n, self.s0, self.t0 = groups, len(groups), s0, t0
            self.last_out, self.cat0, self.values = last_out, cat0, values

        def t_prob(self, g):
            return self.t0 + max(0, 2 * g - 1)

        def t_out(self, g):
            return self.t0 + 2 * g + 2 if g < self.n - 1 else self.last_out

    ctx = ExitStack()
    with ctx:
        def sb(name, shape, dt=F32):
            return ctx.enter_context(nc.sbuf_tensor(name, shape, dt))

        def sem(name):
            return ctx.enter_context(nc.semaphore(name))

        raw = sb("raw", [P, RAW * UNIT])
        hi = sb("hi", [P, SPLIT * UNIT], F32R)
        lo = sb("lo", [P, SPLIT * UNIT], F32R)
        xT = [sb(f"xT_{s}", [P, CAT * SEQ], F32R) for s in ("hi", "lo")]
        wk = [sb(f"wk_{s}", [P, 3072], F32R) for s in ("hi", "lo")]
        sel = sb("sel", [P, NT * P], F32R)
        selT = sb("selT", [P, NT * P], F32R)
        h = sb("h", [P, NT, D])
        R1 = sb("R1", [P, 2048])
        R2 = sb("R2", [P, 2048])
        R3 = sb("R3", [P, 4096])
        GB1 = sb("GB1", [P, D])
        GB2 = sb("GB2", [P, D])
        krT = sb("krT", [P, 2, SEQ])
        kr = sb("kr", [P, 2, NT, P])
        kraw = sb("kraw", [P, NT, ROPE])
        ident = sb("ident", [P, P])
        ones = sb("ones", [P, P])
        tri = sb("tri", [P, P])
        tris = sb("tris", [P, P])
        cmask = sb("cmask", [P, P])
        freq = sb("freq", [P, 32])
        posi = sb("posi", [P, NT], I32)
        posf = sb("posf", [P, NT])
        cs = sb("cs", [P, 2, NT, 32])
        qscale = sb("qscale", [P, 2, NT])
        ssum = sb("ssum", [P, 9, 2])
        rstd = sb("rstd", [P, 9, 2])
        vss = sb("vss", [P, NT, NG])
        vrs = sb("vrs", [P, NT, NG])
        mhalf = sb("mhalf", [P, NT * NG])
        gbs = sb("gbs", [P, NG])
        mx = sb("mx", [P, 14, 4])
        nb = sb("nb", [P, 14, 4])
        den = sb("den", [P, 14, 4])
        rden = sb("rden", [P, 14, 4])
        wr = sb("wr", [P, KD, E])
        br = sb("br", [P, E])
        prio = sb("prio", [P, E])
        rt = sb("rt", [P, 12, NT, E])
        r1 = sb("r1", [P, 10, NT])
        rsm = sb("rsm", [P, NT * 32])
        nround = sb("nround", [P, 1], I32)
        slot_of = sb("slot_of", [P, NT, 2 * E + 1])
        gate_of = sb("gate_of", [P, NT, 2 * E + 1])

        A = [[ctx.enter_context(nc.psum_tensor(f"A{p}{t}", [P, 512], F32)) for t in range(2)]
             for p in range(2)]
        T = [ctx.enter_context(nc.psum_tensor(f"T{b}", [P, 512], F32)) for b in range(2)]
        S = [ctx.enter_context(nc.psum_tensor(f"S{b}", [P, 512], F32)) for b in range(2)]

        raw_full = [sem(f"raw_full{i}") for i in range(RAW)]
        blocks_in = [sem(f"blocks_in{i}") for i in range(RAW)]
        hi_done = sem("hi_done")
        lo_done = sem("lo_done")
        used = sem("used")
        t_done, s_done = sem("t_done"), sem("s_done")
        mixed_done, route_mm, scat_done = sem("mixed_done"), sem("route_mm"), sem("scat_done")
        a_free = [sem(f"a_free{i}") for i in range(2)]
        t_free = [sem(f"t_free{i}") for i in range(2)]
        s_free = [sem(f"s_free{i}") for i in range(2)]
        x_in = [sem(f"x_in{i}") for i in range(2)]
        mem_in, ws_in = sem("mem_in"), sem("ws_in")
        gb1_first, gb2_first = sem("gb1_first"), sem("gb2_first")
        gb1_in, gb2_in = sem("gb1_in"), sem("gb2_in")
        gbs_in, rope_in, rout_in, mem2_in = sem("gbs_in"), sem("rope_in"), sem("rout_in"), sem("mem2_in")
        consts = sem("consts")
        ssum_done = sem("ssum_done")
        rstd_done = sem("rstd_done")
        pool_step = sem("pool_step")
        xn_done = sem("xn_done")
        vss_done, vrs_done, vn_done = sem("vss_done"), sem("vrs_done"), sem("vn_done")
        max_done = sem("max_done")
        exp_done = sem("exp_done")
        prob_done = sem("prob_done")
        rope_ang, rope_cs, rope_done = sem("rope_ang"), sem("rope_cs"), sem("rope_done")
        kr_copied = sem("kr_copied")
        c_ready = sem("c_ready")
        rt_exp_in, rt_exp = sem("rt_exp_in"), sem("rt_exp")
        mask_done, route_done, moe_const = sem("mask_done"), sem("route_done"), sem("moe_const")
        sel_done = sem("sel_done")
        y_hi = sem("y_hi")
        xs_hi, xs_done = sem("xs_hi"), sem("xs_done")
        act_step = sem("act_step")
        dve_step = sem("dve_step")
        out_done = sem("out_done")
        block = ctx.enter_context(nc.Block())

        xTv = [a[:, :].rearrange("p (k s) -> p k s", s=SEQ) for a in xT]
        wkv = [a[:, 0:FB * SEQ].rearrange("p (k s) -> p k s", s=SEQ) for a in wk]
        xg = [a[:, 0:KD * P] for a in xT]
        hT = [a[:, KD * P:KD * P + EB * P] for a in xT]
        xs = [a[:, 0:NT * D].rearrange("p (t d) -> p t d", t=NT) for a in wk]
        ys = [a[:, NT * D:NT * D + D] for a in wk]
        xn = R1[:, :].rearrange("p (t d) -> p t d", t=NT)
        gu = xn
        lat = xn
        memt = R2[:, :].rearrange("p (t d) -> p t d", t=NT)
        gv = memt
        qn = R2[:, :].rearrange("p (h s) -> p h s", h=HEADS)
        xnT = R2[:, :].rearrange("p (k s) -> p k s", k=KD)
        fsilu = R2[:, 0:NT * FCH].rearrange("p (t n) -> p t n", t=NT)
        mk = R3[:, 0:1024].rearrange("p (h s) -> p h s", h=MH)
        mv = R3[:, 1024:2048].rearrange("p (t n) -> p t n", t=NT)
        mq = R3[:, 2048:3072].rearrange("p (h s) -> p h s", h=MH)
        wsT = R3[:, 3072:4096].rearrange("p (g s) -> p g s", g=NG)
        kn = R3[:, 0:2048].rearrange("p (h s) -> p h s", h=HEADS)
        lv = R3[:, 2048:4096].rearrange("p (t n) -> p t n", t=NT)
        fhid = R3[:, 0:NT * FHALF].rearrange("p (t n) -> p t n", t=NT)
        esilu = R3[:, 0:ECH]
        ehid = R3[:, ECH:2 * ECH]
        wsr = R3[:, 0:1024].rearrange("p (g s) -> p g s", g=NG)
        PP = R1[:, 0:1024].rearrange("p (a b) -> p a b", a=2)
        PPT = R1[:, 1024:2048].rearrange("p (a b) -> p a b", a=2)
        iota = R3[:, 3072:3072 + P]
        qr = GB1[:, :].rearrange("p (t h r) -> p t h r", t=NT, h=HEADS)
        qrT = GB2[:, :].rearrange("p (i s) -> p i s", i=4)
        tmp = R3[:, 3072:4096].rearrange("p (i t h r) -> p i t h r", i=4, t=NT, h=4)
        junk, junk_v, junk_end = R3[:, 3072:4096], R3[:, 2048:3072], R1[:, D:2 * D]
        mem_heads = [Heads(MEM_GROUPS, S_MEM[i], T_OF[f"att{i}"], last, KD, mv)
                     for i, last in enumerate((T_OF["att0"] + 7, T_OF["att1 last"]))]
        lat_heads = Heads(LAT_GROUPS, S_LAT, T_OF["lat"], T_OF["lat"] + 11, 0, lv)

        def piece(ring, slots, u, i):
            k, n = shape_of(u)
            at, half = (u % slots) * UNIT, k * n // 2
            return ring[:, at + i * half:at + (i + 1) * half]

        def part(ring, u, kk, c0, n):
            at = (u % SPLIT) * UNIT + kk * shape_of(u)[1] + c0
            return ring[:, at:at + n]

        @block.sync
        def _(sp):
            def load(u, src):
                k, n = shape_of(u)
                at = (u % RAW) * UNIT
                if u >= RAW:
                    sp.wait_ge(lo_done, 2 * (u - RAW) + 2)
                dst = raw[:, at:at + k * n]
                if u in (U_QR, *U_UQ):
                    dst = dst.rearrange("p (k h c) -> p k h c", k=k, h=src.shape[2])
                    for kk in range(k):
                        done = raw_full if kk == k - 1 else blocks_in
                        sp.dma_start(dst[:, kk], src[:, kk]).then_inc(done[u % RAW], 16)
                else:
                    sp.dma_start(dst.rearrange("p (k n) -> p k n", n=n), src
                                 ).then_inc(raw_full[u % RAW], 16)

            sp.dma_start(GB2[:, :], attn_norm[0].partition_broadcast(P)).then_inc(gb2_first, 16)
            for half in range(2):
                cols = slice(half * 512, (half + 1) * 512)
                sp.dma_start(h[:, :, cols], x[0][:, cols].rearrange("(t p) d -> p t d", p=P)
                             ).then_inc(x_in[half], 16)
            for u in range(3):
                load(u, units[u][0])
            sp.dma_start(memt, mem[0].rearrange("(t p) d -> p t d", p=P)).then_inc(mem_in, 16)
            sp.dma_start(GB1[:, :], mem_norm[0].partition_broadcast(P)).then_inc(gb1_first, 16)
            for u in range(3, U_MOE):
                load(u, units[u][0])

            def expert_loads(e, ve):
                for j in range(MU):
                    u = U_MOE + j
                    k, n = moe_shape[j]
                    if j < 8:
                        w = (moe_w_gate, moe_w_up)[j // 2 % 2]
                        k0, c0 = 4 * (j % 2), ECH * (j // 4)
                    else:
                        w, k0, c0 = moe_w_down, 7 * ((j - 8) // 2), 512 * (j % 2)
                    src = w[0, bass.ds(e, 1), k0 * P:(k0 + k) * P, c0:c0 + n]
                    at = (u % RAW) * UNIT
                    sp.wait_ge(lo_done, ve * (2 * MU) + 2 * (u - RAW) + 2)
                    sp.dma_start(raw[:, at:at + k * n].rearrange("p (k n) -> p k n", n=n),
                                 src.rearrange("e (k p) n -> p (e k) n", p=P)
                                 ).then_inc(raw_full[u % RAW], 16)

            with sp.Fori(0, E) as e:
                expert_loads(e, e)
            sp.wait_ge(route_done, 1)
            rounds = sp.value_load(nround[0:1, 0:1], min_val=E, max_val=2 * E)
            with sp.If(rounds > E):
                with sp.Fori(0, E) as e:
                    expert_loads(e, e + E)
            for t in range(NT):
                sp.wait_ge(xn_done, XN_OF["final"] + t + 1)
                sp.dma_start(out[0, t * P:(t + 1) * P, :], xn[:, t]).then_inc(out_done, 16)
            sp.wait_ge(out_done, 16 * NT)

        @block.tensor
        def _(pe):
            def a_job(j):
                if j >= 2:
                    pe.wait_ge(a_free[j % 2], 2 * (j // 2))
                return A[j % 2]

            def t_job(j):
                if j >= 2:
                    pe.wait_ge(t_free[j % 2], 2 * (j // 2))
                return T[j % 2]

            def s_job(j):
                if j >= 2:
                    pe.wait_ge(s_free[j % 2], j // 2)
                return S[j % 2]

            def split_ready(u, kk, it=0):
                k, n = shape_of(u)
                half = k * n // 2
                if kk == 0:
                    pe.wait_ge(lo_done, it * (2 * MU) + 2 * u + 1)
                if kk * n <= half < (kk + 1) * n:
                    pe.wait_ge(lo_done, it * (2 * MU) + 2 * u + 2)

            def three(out, stat, mov, start, stop):
                nc.tensor.matmul(out, stat[0], mov[1], start=start, stop=False)
                nc.tensor.matmul(out, stat[1], mov[0], start=False, stop=False)
                return nc.tensor.matmul(out, stat[0], mov[0], start=False, stop=stop)

            def project(u, pair, acts, k0=0, first=True, final=True, before=None):
                k, n = shape_of(u)
                for kk in range(k):
                    if before and kk in before:
                        before[kk]()
                    split_ready(u, kk)
                    for t in range(NT):
                        last = three(pair[t][:, 0:n], [a[:, k0 + kk, t * P:(t + 1) * P] for a in acts],
                                     (part(hi, u, kk, 0, n), part(lo, u, kk, 0, n)),
                                     first and kk == 0, final and kk == k - 1)
                last.then_inc(used, 1)

            def project_T(u, out, acts, c0, first=True, late=()):
                k = shape_of(u)[0]
                for kk in range(k):
                    if kk == 4:
                        transposed(*late)
                    if first:
                        split_ready(u, kk)
                    last = three(out, (part(hi, u, kk, c0, P), part(lo, u, kk, c0, P)),
                                 [a[:, kk, :] for a in acts], kk == 0, kk == k - 1)
                return last

            def heads_T(u, j, acts, late=(), between=None):
                bank = a_job(j)[0]
                for i in range(2):
                    if i and between:
                        between()
                    last = project_T(u, bank[:, i * SEQ:(i + 1) * SEQ], acts, i * P, i == 0,
                                     () if i else late)
                last.then_inc(used, 1)

            def transposes(j, blocks):
                bank = t_job(j)
                for i, b in enumerate(blocks):
                    last = nc.tensor.transpose(bank[:, i * P:(i + 1) * P], b, ident[:, :])
                last.then_inc(t_done, 1)

            def transposed(*jobs):
                for j in jobs:
                    pe.wait_ge(t_free[j % 2], 2 * (j // 2 + 1))

            def half_T(src, name, j0, half, parts=2):
                for t in range(NT):
                    pe.wait_ge(xn_done, XN_OF[name] + (2 * half + t + 1 if parts == 2 else t + 1))
                    transposes(j0 + 2 * half + t, [src[:, t, (4 * half + i) * P:(4 * half + i + 1) * P]
                                                   for i in range(4)])

            def attend(a, g, scores):
                if g + 1 < a.n:
                    t, hs, n = a.groups[g + 1]
                    bank = s_job(a.s0 + g + 1)
                    for i, hd in enumerate(hs):
                        last = scores(bank[:, i * n:(i + 1) * n], hd, t, n)
                    last.then_inc(s_done, 1)
                if 0 <= g < a.n:
                    pe.wait_ge(prob_done, a.s0 + g + 1)
                    transposes(a.t_prob(g), [PP[:, g % 2, i * P:(i + 1) * P] for i in range(4)])
                if g >= 1:
                    t, hs, n = a.groups[g - 1]
                    transposed(a.t_prob(g - 1))
                    bank = t_job(a.t_out(g - 1))
                    nk = n // P
                    for i, hd in enumerate(hs):
                        for b in range(nk):
                            at = (i * nk + b) * P
                            last = nc.tensor.matmul(bank[:, i * P:(i + 1) * P],
                                                    a.values[:, b, hd * P:(hd + 1) * P],
                                                    PPT[:, (g - 1) % 2, at:at + P],
                                                    start=b == 0, stop=b == nk - 1)
                    last.then_inc(t_done, 1)

            def mem_scores(out, hd, t, n):
                return nc.tensor.matmul(out, mq[:, hd, t * P:(t + 1) * P], mk[:, hd, :],
                                        start=True, stop=True)

            def lat_scores(out, hd, t, n):
                nc.tensor.matmul(out, qn[:, hd, t * P:(t + 1) * P], kn[:, hd, 0:n],
                                 start=True, stop=False)
                return nc.tensor.matmul(out, qrT[:, hd // 2, t * P:(t + 1) * P],
                                        krT[:, hd % 2, 0:n], start=False, stop=True)

            def emptied(j):
                pe.wait_ge(a_free[j % 2], 2 * (j // 2 + 1))

            def out_projection(layer, stages, inside):
                pair = [None, None]
                for i in range(6):
                    r, c = i // 2, i % 2
                    stages[i]()
                    if r == 0:
                        pair[c] = a_job(A_OUT[layer] + c)
                    project(U_OUT[layer][r][c], pair[c], xTv, OUT_ROWS[r], r == 0, r == 2,
                            inside.get(i))

            def nothing():
                pass

            pe.wait_ge(consts, 1)
            half_T(xn, "x0", T_X[0], 0)
            half_T(xn, "x0", T_X[0], 1)
            transposed(T_X[0], T_X[0] + 1)
            for i in range(2):
                heads_T(U_Q0[i], A_Q[0] + i, xTv, (T_X[0] + 2, T_X[0] + 3))
            pair = a_job(A_GV[0])
            project(U_GV[0][0], pair, xTv, 0, True, False)
            half_T(memt, "mem0", T_MEM[0], 0, 1)
            project(U_GV[0][1], pair, xTv, 4, False, True,
                    {3: lambda: half_T(memt, "mem0", T_MEM[0], 1, 1)})
            pe.wait_ge(ws_in, 16)
            for i in range(2):
                transposes(T_WS + i, [wsr[:, 4 * i + g, :] for g in range(4)])
            transposed(T_MEM[0], T_MEM[0] + 1)
            for i in range(2):
                heads_T(U_K0[i], A_K[0] + i, wkv, (T_MEM[0] + 2, T_MEM[0] + 3))
            att = mem_heads[0]
            pair = a_job(A_V[0])
            project(U_V0[0], pair, wkv, 0, True, False)
            for j in (A_Q[0], A_Q[0] + 1, A_K[0], A_K[0] + 1):
                emptied(j)
            attend(att, -1, mem_scores)
            project(U_V0[1], pair, wkv, 4, False, True)
            attend(att, 0, mem_scores)
            pair = a_job(A_GV[1])
            project(U_GV[1][0], pair, xTv, 0, True, False)
            emptied(A_V[0])
            attend(att, 1, mem_scores)
            project(U_GV[1][1], pair, xTv, 4, False, True)
            attend(att, 2, mem_scores)
            pair = a_job(A_GU)
            project(U_GU[0][0], pair, xTv, 0, True, False)
            attend(att, 3, mem_scores)
            project(U_GU[0][1], pair, xTv, 4, False, True)
            attend(att, 4, mem_scores)

            def mix(j):
                pair = a_job(A_MIX + j)
                for i in range(4):
                    g = 4 * j + i
                    last = nc.tensor.matmul(pair[i // 2][:, (i % 2) * SEQ:(i % 2 + 1) * SEQ], wsT[:, g, :],
                                            gv[:, :, g * P:(g + 1) * P], start=True, stop=True)
                last.then_inc(mixed_done, 1)

            pair = a_job(A_GU + 1)
            project(U_GU[1][0], pair, xTv, 0, True, False)
            pe.wait_ge(vn_done, NT)
            mix(0)
            project(U_GU[1][1], pair, xTv, 4, False, True)

            def gated_T(b):
                emptied(A_MIX + b)
                for t in range(NT):
                    transposes(T_U + 2 * b + t, [gu[:, t, (4 * b + i) * P:(4 * b + i + 1) * P]
                                                 for i in range(4)])

            gated_T(0)
            out_projection(0, (lambda: transposed(att.t_out(2), att.t_out(3)), lambda: gated_T(1),
                               lambda: transposed(T_U, T_U + 1), nothing,
                               lambda: transposed(T_U + 2, T_U + 3), nothing),
                           {0: {2: lambda: mix(1)}, 5: {3: lambda: half_T(xn, "fn0", T_FN[0], 0)}})

            def second_half_T():
                half_T(xn, "fn0", T_FN[0], 1)
                transposed(T_FN[0] + 2, T_FN[0] + 3)

            transposed(T_FN[0], T_FN[0] + 1)
            for hf in range(2):
                gu_units, down_units = U_FF[hf]
                j0, tj = A_FF[hf], T_FH[hf]

                def hidden_T(i, b0, nb, chunks, t0=0):
                    j = j0 + 2 * chunks - 1
                    pe.wait_ge(a_free[j % 2], 2 * (j // 2 + 1))
                    for t in range(NT):
                        transposes(tj + 2 * i + t, [fhid[:, t, (b0 + b) * P:(b0 + b + 1) * P]
                                                    for b in range(nb)])

                for c in range(4):
                    project(gu_units[c][0], a_job(j0 + 2 * c), xTv,
                            before={4: second_half_T} if hf == 0 and c == 0 else None)
                    if c == 2:
                        hidden_T(0, 0, 4, 2)
                    if c == 3:
                        hidden_T(1, 4, 4, 3)
                    project(gu_units[c][1], a_job(j0 + 2 * c + 1), xTv)
                for c in range(4):
                    u, pair = down_units[c], a_job(j0 + 8 + c)
                    if c == 0:
                        transposed(tj, tj + 1, tj + 2, tj + 3)
                    before = {}
                    if c == 0:
                        before = {5: lambda: hidden_T(2, 8, 3, 4), 8: lambda: transposed(tj + 4, tj + 5)}
                    if hf == 1 and c == 3:
                        before = {4: lambda: half_T(memt, "mem1", T_MEM[1], 1, 1)}
                    project(u, pair, wkv, before=before)
                    if hf == 1 and c == 2:
                        half_T(memt, "mem1", T_MEM[1], 0, 1)

            transposed(T_MEM[1], T_MEM[1] + 1)
            for i in range(2):
                heads_T(U_K1[i], A_K[1] + i, xTv, (T_MEM[1] + 2, T_MEM[1] + 3))
            pair = a_job(A_V[1])
            project(U_V1[0], pair, xTv, 0, True, False)
            half_T(xn, "x1", T_X[1], 0)
            project(U_V1[1], pair, xTv, 4, False, True)
            half_T(xn, "x1", T_X[1], 1)
            transposed(T_X[1], T_X[1] + 1)
            for i in range(3):
                project(U_C[i], a_job(A_C + i), wkv,
                        before=None if i else {4: lambda: transposed(T_X[1] + 2, T_X[1] + 3)})

            def latents_T(half):
                pe.wait_ge(c_ready, NT)
                for t in range(NT):
                    transposes(T_C + 2 * half + t, [lat[:, t, (4 * half + i) * P:(4 * half + i + 1) * P]
                                                    for i in range(4)])

            heads_T(U_Q1[0], A_Q[1], wkv)
            heads_T(U_Q1[1], A_Q[1] + 1, wkv, between=lambda: latents_T(0))
            latents_T(1)
            transposed(T_C, T_C + 1)
            att = mem_heads[1]
            project(U_QR, a_job(A_UQ), xTv, before={4: lambda: transposed(T_C + 2, T_C + 3)})
            for j in (A_K[1], A_K[1] + 1, A_V[1], A_Q[1], A_Q[1] + 1):
                emptied(j)
            attend(att, -1, mem_scores)
            for i in range(2):
                u, pair = U_UQ[i], a_job(A_UQ + 1 + i)
                for hh in range(4):
                    if hh == 2:
                        attend(att, 2 * i, mem_scores)
                    last = project_T(u, pair[hh // 2][:, (hh % 2) * SEQ:(hh % 2 + 1) * SEQ], xTv,
                                     hh * P, hh == 0)
                last.then_inc(used, 1)
                attend(att, 2 * i + 1, mem_scores)
            kvT = [a[:, QL // P:KD, :] for a in xTv]

            def keys_values(i):
                u, pair = U_UKV[i], a_job(A_UKV + 2 * i)
                for hh in range(4):
                    project_T(u, pair[hh // 2][:, (hh % 2) * SEQ:(hh % 2 + 1) * SEQ], kvT, hh * 256, hh == 0)
                pair = a_job(A_UKV + 2 * i + 1)
                for t in range(NT):
                    for kk in range(2):
                        at = (u % SPLIT) * UNIT + kk * 1024
                        mov = [r[:, at:at + 1024].rearrange("p (h c) -> p h c", h=4)[:, :, P:256]
                               for r in (hi, lo)]
                        last = three(pair[t][:, :], [a[:, kk, t * P:(t + 1) * P] for a in kvT], mov,
                                     kk == 0, kk == 1)
                last.then_inc(used, 1)

            keys_values(0)
            pe.wait_ge(rope_done, 3)
            for t in range(NT):
                transposes(T_ROPE + t, [qr[:, t, 2 * i:2 * i + 2, :] for i in range(4)])
            transposes(T_ROPE + 2, [kr[:, b, t, :] for b in range(2) for t in range(NT)])
            attend(att, 4, mem_scores)
            transposed(T_ROPE, T_ROPE + 1, T_ROPE + 2)
            for j in (A_UKV, A_UKV + 1):
                emptied(j)
            att = lat_heads
            attend(att, -1, lat_scores)
            keys_values(1)

            def stage_2():
                for j in (A_UKV + 2, A_UKV + 3):
                    emptied(j)
                attend(att, 2, lat_scores)

            def rows_8():
                attend(att, 0, lat_scores)
                transposed(mem_heads[1].t_out(2), mem_heads[1].t_out(3))

            def rows_0():
                attend(att, 3, lat_scores)
                transposed(att.t_out(0), att.t_out(1))

            def rows_4():
                attend(att, 6, lat_scores)
                transposed(att.t_out(3), att.t_out(4))

            out_projection(1, (rows_8, nothing, rows_0, nothing, rows_4, nothing),
                           {0: {3: lambda: attend(att, 1, lat_scores)}, 1: {2: stage_2},
                            2: {2: lambda: transposed(att.t_out(2)),
                                3: lambda: attend(att, 4, lat_scores)},
                            3: {2: lambda: attend(att, 5, lat_scores)},
                            4: {2: lambda: transposed(att.t_out(5))},
                            5: {3: lambda: half_T(xn, "fn1", T_FN[1], 0)}})
            pair = a_job(A_RT)
            pe.wait_ge(rout_in, 32)
            for half in range(2):
                if half:
                    half_T(xn, "fn1", T_FN[1], 1)
                transposed(T_FN[1] + 2 * half, T_FN[1] + 2 * half + 1)
                for t in range(NT):
                    for kk in range(4 * half, 4 * half + 4):
                        last = nc.tensor.matmul(pair[t][:, 0:E], xnT[:, kk, t * P:(t + 1) * P],
                                                wr[:, kk, :], start=kk == 0, stop=kk == KD - 1)
            last.then_inc(route_mm, 1)
            pair = a_job(A_RT + 1)
            pe.wait_ge(mask_done, 1)
            mask = rt[:, 0]
            nc.tensor.matmul(pair[0][:, 0:E], tris[:, :], mask[:, 0, :], start=True, stop=True)
            nc.tensor.matmul(pair[1][:, 0:E], ones[:, :], mask[:, 0, :], start=True, stop=False)
            nc.tensor.matmul(pair[1][:, 0:E], tris[:, :], mask[:, 1, :], start=False, stop=True)
            nc.tensor.matmul(pair[0][:, E:2 * E], ones[:, :], mask[:, 0, :], start=True, stop=False)
            nc.tensor.matmul(pair[0][:, E:2 * E], ones[:, :], mask[:, 1, :], start=False,
                             stop=True).then_inc(route_mm, 1)

            def gather(tj, it):
                for b in range(2):
                    pe.wait_ge(t_free[(tj + b) % 2], it * 8 + 2 * ((tj + b) // 2))
                    bank = T[(tj + b) % 2]
                    for i in range(4):
                        d = 4 * b + i
                        n = 0
                        for src in (xs[1], xs[0]):
                            for t in range(NT):
                                last = nc.tensor.matmul(bank[:, i * P:(i + 1) * P],
                                                        src[:, t, d * P:(d + 1) * P],
                                                        sel[:, t * P:(t + 1) * P], start=n == 0, stop=n == 3)
                                n += 1
                    last.then_inc(t_done, 1)

            pe.wait_ge(moe_const, 1)
            for c in range(2):
                pe.wait_ge(s_free[(S_MOE + c) % 2], (S_MOE + c) // 2)
                last = nc.tensor.matmul(S[(S_MOE + c) % 2][:, :], selT[:, 0:P], ys[0][:, c * 512:(c + 1) * 512],
                                        start=True, stop=True)
            last.then_inc(scat_done, 1)
            pe.wait_ge(xs_done, NT)
            pe.wait_ge(sel_done, 1)
            gather(T_MOE, 0)

            def scatter(t, ve):
                for c in range(2):
                    s = S_MOE + 2 + 2 * t + c
                    pe.wait_ge(s_free[s % 2], ve * 3 + s // 2)
                    for n in range(2):
                        last = nc.tensor.matmul(S[s % 2][:, :], selT[:, t * P:(t + 1) * P],
                                                ys[1 - n][:, c * 512:(c + 1) * 512],
                                                start=n == 0, stop=n == 1)
                    last.then_inc(scat_done, 1)

            def hidden_expert(ve, units4, j, before_second):
                pe.wait_ge(a_free[j % 2], ve * 4 + 2 * (j // 2))
                for n, u in enumerate(units4):
                    if n:
                        before_second()
                    for kk in range(4):
                        split_ready(u, kk, ve)
                        k = 4 * n + kk
                        stat = [a[:, k * P:(k + 1) * P] for a in xg]
                        for b in range(2):
                            mov = (part(hi, u, kk, b * EN, EN), part(lo, u, kk, b * EN, EN))
                            last = three(A[j % 2][b][:, 0:EN], stat, mov, k == 0, k == 7)
                    last.then_inc(used, 1)

            def hidden_T_expert(ve, c, tj):
                j = A_MOE + 2 * c + 1
                pe.wait_ge(a_free[j % 2], ve * 4 + 2 * (j // 2 + 1))
                for n, nb_ in enumerate((4, 3)):
                    j = tj + n
                    pe.wait_ge(t_free[j % 2], ve * 8 + 2 * (j // 2))
                    for b in range(nb_):
                        at = (4 * n + b) * P
                        last = nc.tensor.transpose(T[j % 2][:, b * P:(b + 1) * P], ehid[:, at:at + P],
                                                   ident[:, :])
                    last.then_inc(t_done, 1)

            def down(ve, u, c, half):
                bank = S[(S_MOE + 6 + c) % 2]
                if half == 0:
                    s = S_MOE + 6 + c
                    pe.wait_ge(s_free[s % 2], ve * 3 + s // 2)
                for kk in range(7):
                    split_ready(u, kk, ve)
                    k = 7 * half + kk
                    last = three(bank[:, :], [a[:, k * P:(k + 1) * P] for a in hT],
                                 (part(hi, u, kk, 0, 512), part(lo, u, kk, 0, 512)), k == 0, k == EB - 1)
                last.then_inc(used, 1)

            pe.wait_ge(route_done, 1)
            rounds = pe.value_load(nround[0:1, 0:1], min_val=E, max_val=2 * E)
            t1 = T_MOE + 2
            with pe.Fori(0, rounds) as ve:
                U = U_MOE

                def gathered(b):
                    pe.wait_ge(t_free[(T_MOE + b) % 2], ve * 8 + 2 * ((T_MOE + b) // 2 + 1))

                gathered(0)
                hidden_expert(ve, (U, U + 1), A_MOE, lambda: gathered(1))
                scatter(0, ve)

                def second_scatter():
                    scatter(1, ve)
                    for t in range(NT):
                        j = t1 + t
                        pe.wait_ge(t_free[j % 2], ve * 8 + 2 * (j // 2))
                        nc.tensor.transpose(T[j % 2][:, 0:P], sel[:, t * P:(t + 1) * P].bitcast(F32),
                                            ident[:, :]).then_inc(t_done, 1)

                hidden_expert(ve, (U + 2, U + 3), A_MOE + 1, second_scatter)
                hidden_expert(ve, (U + 4, U + 5), A_MOE + 2, nothing)
                hidden_T_expert(ve, 0, t1 + 2)
                hidden_expert(ve, (U + 6, U + 7), A_MOE + 3, nothing)
                for j in (t1 + 2, t1 + 3):
                    pe.wait_ge(t_free[j % 2], ve * 8 + 2 * (j // 2 + 1))
                down(ve, U + 8, 0, 0)
                hidden_T_expert(ve, 1, t1 + 4)
                down(ve, U + 9, 1, 0)
                for j in (t1 + 4, t1 + 5):
                    pe.wait_ge(t_free[j % 2], ve * 8 + 2 * (j // 2 + 1))
                down(ve, U + 10, 0, 1)
                pe.wait_ge(sel_done, ve + 2)
                with pe.If(ve < rounds - 1):
                    gather(t1 + 6, ve)
                down(ve, U + 11, 1, 1)
            scatter(0, rounds)
            scatter(1, rounds)

        @block.scalar
        def _(act):
            def act_copy(out, in_):
                return nc.scalar.activation(out, in_, ACT.Copy)

            def split(u, it=0):
                act.wait_ge(raw_full[u % RAW], it * (16 * MU // RAW) + 16 * (u // RAW + 1))
                if u in (U_QR, *U_UQ):
                    act.wait_ge(blocks_in[u % RAW], 16 * (QL // P - 1))
                if u >= SPLIT:
                    act.wait_ge(used, it * MU + u - SPLIT + 1)
                for i in range(2):
                    act_copy(piece(hi, SPLIT, u, i), piece(raw, RAW, u, i)).then_inc(hi_done, 1)

            def square_sums(n, src, n_cols=D, c0=0, scratch=junk):
                for t in range(NT):
                    if n or t:
                        act.wait_ge(ssum_done, 2 * n + t)
                    nc.scalar.activation(scratch[:, 0:n_cols], src[:, t, c0:c0 + n_cols], ACT.Square,
                                         accum_out=ssum[:, n, t:t + 1]).then_inc(ssum_done, 1)

            def t_bank(j, n=4):
                act.wait_ge(t_done, j + 1)
                return T[j % 2][:, 0:n * P].rearrange("p (k s) -> p k s", k=n)

            def t_hi(j, out, n=4):
                act_copy(out, t_bank(j, n)).then_inc(t_free[j % 2], 1)

            def half_hi(j0, acts, half):
                for t in range(NT):
                    t_hi(j0 + 2 * half + t, acts[0][:, 4 * half:4 * half + 4, t * P:(t + 1) * P])

            def two_heads(u, j, out):
                act.wait_ge(used, u + 1)
                act_copy(out, A[j % 2][0][:, :].rearrange("p (h s) -> p h s", h=2)
                         ).then_inc(a_free[j % 2], 2)

            def attend(a, g, scale_of):
                if g + 1 < a.n:
                    t, hs, n = a.groups[g + 1]
                    gg = a.s0 + g + 1
                    act.wait_ge(max_done, gg + 1)
                    if g >= 1:
                        act.wait_ge(t_done, a.t_prob(g - 1) + 1)
                    for i in range(len(hs)):
                        last = nc.scalar.activation(PP[:, (g + 1) % 2, i * n:(i + 1) * n],
                                                    S[gg % 2][:, i * n:(i + 1) * n], ACT.Exp,
                                                    bias=nb[:, gg, i:i + 1], scale=scale_of(t),
                                                    accum_out=den[:, gg, i:i + 1])
                    last.then_inc(s_free[gg % 2], 1)
                if 0 <= g < a.n:
                    j = a.t_prob(g)
                    if g >= 2:
                        act.wait_ge(t_done, a.t_out(g - 2) + 1)
                    act_copy(PPT[:, g % 2, :].rearrange("p (k s) -> p k s", k=4), t_bank(j)
                             ).then_inc(t_free[j % 2], 2)
                if g >= 1:
                    t, hs, _ = a.groups[g - 1]
                    t_hi(a.t_out(g - 1), xTv[0][:, a.cat0 + hs[0]:a.cat0 + hs[0] + len(hs),
                                                t * P:(t + 1) * P], len(hs))

            def mem_scale(layer):
                return lambda t: qscale[:, layer, t:t + 1]

            def lat_scale(t):
                return MLA_SCALE

            def scaled(n, t):
                return rstd[:, n, t:t + 1]

            half_hi(T_X[0], xTv, 0)
            split(0)
            half_hi(T_X[0], xTv, 1)
            act.dma_start(wsr, gm_w_s[0].rearrange("g t s -> t g s")).then_inc(ws_in, 16)
            act.dma_start(gbs[:, :], gm_b_s[0].rearrange("g t -> t g"),
                          allow_slow_non_contiguous=True).then_inc(gbs_in, 16)
            act.dma_start(posi[:, :], positions.rearrange("a (t p) -> p (a t)", p=P),
                          allow_slow_non_contiguous=True).then_inc(rope_in, 16)
            act.dma_start(freq[:, :], rope_freq.partition_broadcast(P)).then_inc(rope_in, 16)
            act.dma_start(wr[:, :, :], moe_w_router[0].rearrange("(k p) e -> p k e", p=P)).then_inc(rout_in, 16)
            act.dma_start(br[:, :], moe_b_router[0].partition_broadcast(P)).then_inc(rout_in, 16)
            split(1)
            two_heads(U_Q0[0], A_Q[0], mq[:, 0:2, :])
            split(U_Q0[0] + 2)
            act.wait_ge(mem_in, 16)
            square_sums(N_MEM[0], memt)
            for half in range(2):
                act.wait_ge(x_in[half], 16)
            square_sums(N_X[0], h)
            two_heads(U_Q0[1], A_Q[0] + 1, mq[:, 2:4, :])
            split(U_Q0[1] + 2)

            def gelu(u, j, dst, i):
                act.wait_ge(used, u + 1)
                for t in range(NT):
                    nc.scalar.activation(dst[:, t, i * 512:(i + 1) * 512], A[j % 2][t][:, :], ACT.Gelu,
                                         scale=scaled(N_X[0], t)).then_inc(a_free[j % 2], 1)

            split(U_GV[0][0] + 2)
            half_hi(T_MEM[0], wkv, 0)
            half_hi(T_MEM[0], wkv, 1)
            act.wait_ge(rstd_done, N_X[0] + 1)
            gelu(U_GV[0][1], A_GV[0], gv, 0)
            split(U_GV[0][1] + 2)
            for i in range(2):
                two_heads(U_K0[i], A_K[0] + i, mk[:, 2 * i:2 * i + 2, :])
                split(U_K0[i] + 2)
            att = mem_heads[0]
            attend(att, -1, mem_scale(0))
            split(U_V0[0] + 2)
            act.wait_ge(used, U_V0[1] + 1)
            j = A_V[0]
            act_copy(mv[:, 0, :], A[j % 2][0][:, :]).then_inc(a_free[j % 2], 1)
            attend(att, 0, mem_scale(0))
            split(U_V0[1] + 2)
            attend(att, 1, mem_scale(0))
            split(U_GV[1][0] + 2)
            attend(att, 2, mem_scale(0))
            split(U_GV[1][1] + 2)
            gelu(U_GV[1][1], A_GV[1], gv, 1)
            attend(att, 3, mem_scale(0))
            split(U_GU[0][0] + 2)
            attend(att, 4, mem_scale(0))
            gelu(U_GU[0][1], A_GU, gu, 0)
            split(U_GU[0][1] + 2)
            split(U_GU[1][0] + 2)
            gelu(U_GU[1][1], A_GU + 1, gu, 1)
            split(U_GU[1][1] + 2)

            def gated_hi(b):
                for t in range(NT):
                    t_hi(T_U + 2 * b + t, xTv[0][:, 4 * b:4 * b + 4, t * P:(t + 1) * P])

            def residual_in(j0):
                for j in (j0, j0 + 1):
                    act.wait_ge(a_free[j % 2], 2 * (j // 2 + 1))

            (a0, a1), (b0, b1), (c0, c1) = U_OUT[0]
            gated_hi(0)
            split(a0 + 2)
            gated_hi(1)
            for u in (a1, b0, b1, c0):
                split(u + 2)
            half_hi(T_FN[0], xTv, 0)
            residual_in(A_OUT[0])
            square_sums(N_FN[0], h)
            half_hi(T_FN[0], xTv, 1)
            split(c1 + 2)
            act.wait_ge(rstd_done, N_FN[0] + 1)
            for hf in range(2):
                gu_units, down_units = U_FF[hf]
                j0, tj = A_FF[hf], T_FH[hf]

                def hidden_hi(i, b0, n):
                    for t in range(NT):
                        t_hi(tj + 2 * i + t, wkv[0][:, b0:b0 + n, t * P:(t + 1) * P], n)

                for c in range(4):
                    g, u = gu_units[c]
                    act.wait_ge(used, g + 1)
                    if c or hf:
                        j = j0 + 2 * c - 1 if c else A_FF[0] + 7
                        act.wait_ge(a_free[j % 2], 2 * (j // 2 + 1))
                    j = j0 + 2 * c
                    for t in range(NT):
                        nc.scalar.activation(fsilu[:, t, :], A[j % 2][t][:, 0:FCH], ACT.Silu,
                                             scale=scaled(N_FN[0], t)).then_inc(a_free[j % 2], 1)
                    if c >= 2:
                        hidden_hi(c - 2, 4 * (c - 2), 4)
                    split(g + 2)
                    split(u + 2)
                hidden_hi(2, 8, 3)
                for c in range(4):
                    if hf == 1 and c == 3:
                        half_hi(T_MEM[1], xTv, 1)
                    split(down_units[c] + 2)
                    if hf == 0 and c == 3:
                        act.wait_ge(rope_ang, 1)
                        nc.scalar.activation(cs[:, :, :, :], cs[:, :, :, :], ACT.Sin).then_inc(rope_cs, 1)
                    if hf == 1 and c == 0:
                        act.wait_ge(mem2_in, 16)
                        square_sums(N_MEM[1], memt)
                    if hf == 1 and c == 2:
                        half_hi(T_MEM[1], xTv, 0)
            residual_in(A_FF[1] + 10)
            for j in (A_FF[1] + 8, A_FF[1] + 9):
                act.wait_ge(a_free[j % 2], 2 * (j // 2 + 1))
            square_sums(N_X[1], h)
            for i in range(2):
                two_heads(U_K1[i], A_K[1] + i, mk[:, 2 * i:2 * i + 2, :])
                split(U_K1[i] + 2)
            split(U_V1[0] + 2)
            half_hi(T_X[1], wkv, 0)
            act.wait_ge(used, U_V1[1] + 1)
            j = A_V[1]
            act_copy(mv[:, 0, :], A[j % 2][0][:, :]).then_inc(a_free[j % 2], 1)
            half_hi(T_X[1], wkv, 1)
            split(U_V1[1] + 2)
            act.wait_ge(rstd_done, N_X[1] + 1)
            for i, (c0, n) in enumerate(C_CHUNKS):
                j = A_C + i
                act.wait_ge(used, U_C[i] + 1)
                if c0 + n > D:
                    nc.scalar.activation(kraw[:, 0, :], A[j % 2][0][:, D - c0:n], ACT.Copy,
                                         scale=scaled(N_X[1], 0))
                    n = D - c0
                nc.scalar.activation(lat[:, 0, c0:c0 + n], A[j % 2][0][:, 0:n], ACT.Copy,
                                     scale=scaled(N_X[1], 0)).then_inc(a_free[j % 2], 1)
                split(U_C[i] + 2)
            for j in range(A_C, A_C + 3):
                act.wait_ge(a_free[j % 2], 2 * (j // 2 + 1))
            square_sums(N_CQ, lat, QL)
            square_sums(N_CKV, lat, KVL, QL)
            two_heads(U_Q1[0], A_Q[1], mq[:, 0:2, :])
            split(U_Q1[0] + 2)
            half_hi(T_C, xTv, 0)
            two_heads(U_Q1[1], A_Q[1] + 1, mq[:, 2:4, :])
            half_hi(T_C, xTv, 1)
            split(U_Q1[1] + 2)
            att = mem_heads[1]
            act.wait_ge(used, U_QR + 1)
            act_copy(qr[:, 0, :, :], A[A_UQ % 2][0][:, :].rearrange("p (h r) -> p h r", h=HEADS)
                     ).then_inc(a_free[A_UQ % 2], 1)
            attend(att, -1, mem_scale(1))
            split(U_QR + 2)
            for i in range(2):
                u, j = U_UQ[i], A_UQ + 1 + i
                attend(att, 2 * i, mem_scale(1))
                act.wait_ge(used, u + 1)
                act_copy(qn[:, 4 * i:4 * i + 2, :], A[j % 2][0][:, :].rearrange("p (h s) -> p h s", h=2)
                         ).then_inc(a_free[j % 2], 1)
                attend(att, 2 * i + 1, mem_scale(1))
                split(u + 2)

            def keys_values(i):
                u, j = U_UKV[i], A_UKV + 2 * i
                act.wait_ge(used, u + 1)
                act_copy(kn[:, 4 * i:4 * i + 2, :], A[j % 2][0][:, :].rearrange("p (h s) -> p h s", h=2)
                         ).then_inc(a_free[j % 2], 1)
                j += 1
                act_copy(lv[:, 0, i * 512:(i + 1) * 512], A[j % 2][0][:, :]).then_inc(a_free[j % 2], 1)

            act.wait_ge(s_done, S_MEM[1] + 4)
            keys_values(0)
            for t in range(NT):
                act_copy(qrT[:, :, t * P:(t + 1) * P], t_bank(T_ROPE + t)
                         ).then_inc(t_free[(T_ROPE + t) % 2], 2)
            j = T_ROPE + 2
            act.wait_ge(t_done, j + 1)
            act_copy(krT[:, :, :].rearrange("p b s -> p (b s)"), T[j % 2][:, :]).then_inc(t_free[j % 2], 2)
            attend(att, 4, mem_scale(1))
            att = lat_heads
            attend(att, -1, lat_scale)
            split(U_UKV[0] + 2)
            keys_values(1)
            attend(att, 0, lat_scale)
            split(U_UKV[1] + 2)
            (a0, a1), (b0, b1), (c0, c1) = U_OUT[1]
            for stages, u in (((1,), a0), ((2, 3), a1), ((4,), b0), ((5, 6), b1), ((), c0)):
                for g in stages:
                    attend(att, g, lat_scale)
                split(u + 2)

            def router_in(half):
                for t in range(NT):
                    j = T_FN[1] + 2 * half + t
                    act_copy(xnT[:, 4 * half:4 * half + 4, t * P:(t + 1) * P], t_bank(j)
                             ).then_inc(t_free[j % 2], 2)

            router_in(0)
            residual_in(A_OUT[1])
            square_sums(N_FN[1], h)
            router_in(1)
            act.wait_ge(rstd_done, N_FN[1] + 1)
            for t in range(NT):
                nc.scalar.activation(xs[0][:, t, :], xn[:, t, :], ACT.Copy, scale=scaled(N_FN[1], t)
                                     ).then_inc(xs_hi, 1)
            act.wait_ge(rt_exp_in, 1)
            nc.scalar.activation(r1[:, 3, :], r1[:, 2, :], ACT.Exp).then_inc(rt_exp, 1)
            split(c1 + 2)

            def gathered_hi(tj, it):
                for b in range(2):
                    j = tj + b
                    act.wait_ge(t_done, it * 8 + j + 1)
                    act_copy(xg[0][:, b * 512:(b + 1) * 512], T[j % 2][:, :]).then_inc(t_free[j % 2], 1)

            def output_hi(c, it):
                act.wait_ge(used, it * MU + U_MOE - 1 + c)
                act.wait_ge(scat_done, 1)
                act_copy(ys[0][:, c * 512:(c + 1) * 512], S[(S_MOE + c) % 2][:, :]).then_inc(y_hi, 1)

            def silu(c, ve):
                act.wait_ge(used, ve * MU + U_MOE + 4 * c + 2)
                j = A_MOE + 2 * c - 1
                act.wait_ge(a_free[j % 2], ve * 4 + 2 * (j // 2 + 1))
                j = A_MOE + 2 * c
                for b in range(2):
                    nc.scalar.activation(esilu[:, b * EN:(b + 1) * EN], A[j % 2][b][:, 0:EN], ACT.Silu
                                         ).then_inc(a_free[j % 2], 1)

            def hidden_hi(c, tj, ve):
                for n, blocks in enumerate((4, 3)):
                    j, at = tj + n, (7 * c + 4 * n) * P
                    act.wait_ge(t_done, ve * 8 + j + 1)
                    act_copy(hT[0][:, at:at + blocks * P], T[j % 2][:, 0:blocks * P]
                             ).then_inc(t_free[j % 2], 1)

            gathered_hi(T_MOE, 0)
            act.wait_ge(route_done, 1)
            rounds = act.value_load(nround[0:1, 0:1], min_val=E, max_val=2 * E)
            U, t1 = U_MOE, T_MOE + 2
            with act.Fori(0, rounds) as ve:
                output_hi(0, ve)
                output_hi(1, ve)
                split(U + 2, ve)
                split(U + 3, ve)
                silu(0, ve)
                split(U + 4, ve)
                for t in range(NT):
                    j = t1 + t
                    act.wait_ge(t_done, ve * 8 + j + 1)
                    act_copy(selT[:, t * P:(t + 1) * P], T[j % 2][:, 0:P]).then_inc(t_free[j % 2], 2)
                split(U + 5, ve)
                split(U + 6, ve)
                split(U + 7, ve)
                silu(1, ve)
                hidden_hi(0, t1 + 2, ve)
                split(U + 8, ve)
                split(U + 9, ve)
                hidden_hi(1, t1 + 4, ve)
                split(U + 10, ve)
                split(U + 11, ve)
                with act.If(ve < rounds - 1):
                    gathered_hi(t1 + 6, ve)
                    split(U, ve + 1)
                    split(U + 1, ve + 1)
            output_hi(0, rounds)
            output_hi(1, rounds)
            for t in range(NT):
                for c in range(2):
                    s = S_MOE + 2 + 2 * t + c
                    act.wait_ge(s_free[s % 2], rounds * 3 + s // 2 + 1)
                if t:
                    act.wait_ge(ssum_done, 2 * N_FINAL + 1)
                nc.scalar.activation(junk_end, h[:, t, :], ACT.Square,
                                     accum_out=ssum[:, N_FINAL, t:t + 1]).then_inc(ssum_done, 1)

        @block.vector
        def _(dve):
            steps = [0]

            def step(ins):
                steps[0] += 1
                ins.then_inc(dve_step, 1)
                dve.wait_ge(dve_step, steps[0])

            def split(u, it=0):
                for i in range(2):
                    dve.wait_ge(hi_done, it * (2 * MU) + 2 * u + i + 1)
                    nc.vector.tensor_tensor(piece(lo, SPLIT, u, i), piece(raw, RAW, u, i),
                                            piece(hi, SPLIT, u, i).bitcast(F32), ALU.subtract
                                            ).then_inc(lo_done, 1)

            def normalise(n, src, dst, gain):
                dve.wait_ge(rstd_done, n + 1)
                for t in range(NT):
                    nc.vector.scalar_tensor_tensor(dst[:, t, :], src[:, t, :], rstd[:, n, t:t + 1],
                                                   gain[:, :], ALU.mult, ALU.mult).then_inc(xn_done, 1)

            def times_gain(half, gain):
                cols = slice(half * 512, (half + 1) * 512)
                for t in range(NT):
                    nc.vector.tensor_tensor(xn[:, t, cols], h[:, t, cols], gain[:, cols], ALU.mult
                                            ).then_inc(xn_done, 1)

            def memory_scale(layer):
                dve.wait_ge(rstd_done, N_X[layer] + 1)
                step(nc.vector.tensor_scalar(qscale[:, layer, :], rstd[:, N_X[layer], :], MEM_SCALE, None,
                                             ALU.mult))

            def t_lo(j, out, hi_part, n=4):
                dve.wait_ge(t_free[j % 2], 2 * (j // 2) + 1)
                nc.vector.tensor_tensor(out, T[j % 2][:, 0:n * P].rearrange("p (k s) -> p k s", k=n),
                                        hi_part.bitcast(F32), ALU.subtract).then_inc(t_free[j % 2], 1)

            def half_lo(j0, acts, half):
                for t in range(NT):
                    hi_part, lo_part = [a[:, 4 * half:4 * half + 4, t * P:(t + 1) * P] for a in acts]
                    t_lo(j0 + 2 * half + t, lo_part, hi_part)

            def maxima(a, g, scale_of, causal):
                if g + 1 < a.n:
                    t, hs, n = a.groups[g + 1]
                    gg = a.s0 + g + 1
                    bank = S[gg % 2][:, :].rearrange("p (h s) -> p h s", h=len(hs))
                    dve.wait_ge(s_done, gg + 1)
                    if causal:
                        own = bank[:, :, n - P:n]
                        step(nc.vector.tensor_tensor(own, own, cmask[:, :].unsqueeze(1).to_broadcast(
                            [P, len(hs), P]), ALU.add))
                    step(nc.vector.tensor_reduce(mx[:, gg, 0:len(hs)], bank, AX.X, ALU.max, negate=True))
                    nc.vector.tensor_scalar(nb[:, gg, 0:len(hs)], mx[:, gg, 0:len(hs)], scale_of(t), None,
                                            ALU.mult).then_inc(max_done, 1)
                if g >= 1:
                    t, hs, _ = a.groups[g - 1]
                    blocks = slice(a.cat0 + hs[0], a.cat0 + hs[0] + len(hs))
                    t_lo(a.t_out(g - 1), xTv[1][:, blocks, t * P:(t + 1) * P],
                         xTv[0][:, blocks, t * P:(t + 1) * P], len(hs))

            def probabilities(a, g):
                if g + 1 < a.n:
                    t, hs, n = a.groups[g + 1]
                    gg = a.s0 + g + 1
                    dve.wait_ge(s_free[gg % 2], gg // 2 + 1)
                    step(nc.vector.reciprocal(rden[:, gg, 0:len(hs)], den[:, gg, 0:len(hs)]))
                    p = PP[:, (g + 1) % 2, :].rearrange("p (h s) -> p h s", h=len(hs))
                    nc.vector.tensor_tensor(p, p, rden[:, gg, 0:len(hs)].unsqueeze(2).to_broadcast(
                        [P, len(hs), n]), ALU.mult).then_inc(prob_done, 1)

            def mem_stage(layer, g, u):
                maxima(mem_heads[layer], g, lambda t: qscale[:, layer, t:t + 1], False)
                if u:
                    split(u)
                probabilities(mem_heads[layer], g)

            def lat_stage(g):
                maxima(lat_heads, g, lambda t: MLA_SCALE, True)
                probabilities(lat_heads, g)

            def memory_values(layer, us):
                j = A_V[layer]
                dve.wait_ge(used, us[1] + 1)
                nc.vector.tensor_copy(mv[:, 1, :], A[j % 2][1][:, :]).then_inc(a_free[j % 2], 1)

            def add_residual(j, c0, n, u):
                dve.wait_ge(used, u + 1)
                for t in range(NT):
                    nc.vector.tensor_tensor(h[:, t, c0:c0 + n], A[j % 2][t][:, 0:n], h[:, t, c0:c0 + n],
                                            ALU.add).then_inc(a_free[j % 2], 1)

            def added(j):
                dve.wait_ge(a_free[j % 2], 2 * (j // 2 + 1))

            dve.wait_ge(gb2_first, 16)
            dve.wait_ge(x_in[0], 16)
            times_gain(0, GB2)
            dve.wait_ge(x_in[1], 16)
            times_gain(1, GB2)
            half_lo(T_X[0], xTv, 0)
            split(0)
            half_lo(T_X[0], xTv, 1)
            split(1)
            split(U_Q0[0] + 2)
            dve.wait_ge(gb1_first, 16)
            dve.wait_ge(mem_in, 16)
            normalise(N_MEM[0], memt, memt, GB1)
            split(U_Q0[1] + 2)
            half_lo(T_MEM[0], wkv, 0)
            split(U_GV[0][0] + 2)
            half_lo(T_MEM[0], wkv, 1)
            dve.wait_ge(consts, 1)
            dve.wait_ge(ssum_done, 2 * N_X[0] + 2)
            for i in range(2):
                j = T_WS + i
                dve.wait_ge(t_done, j + 1)
                nc.vector.tensor_tensor(wsT[:, 4 * i:4 * i + 4, :],
                                        T[j % 2][:, :].rearrange("p (k s) -> p k s", k=4),
                                        tri[:, :].unsqueeze(1).to_broadcast([P, 4, P]), ALU.mult
                                        ).then_inc(t_free[j % 2], 2)
            split(U_GV[0][1] + 2)
            split(U_K0[0] + 2)
            split(U_K0[1] + 2)
            memory_scale(0)
            mem_stage(0, -1, U_V0[0] + 2)
            memory_values(0, U_V0)
            mem_stage(0, 0, U_V0[1] + 2)
            mem_stage(0, 1, U_GV[1][0] + 2)
            mem_stage(0, 2, 0)
            split(U_GV[1][1] + 2)
            for j in A_GV:
                added(j)
            for t in range(NT):
                step(nc.vector.tensor_tensor(junk_v, gv[:, t, :], gv[:, t, :], ALU.mult))
                red = nc.vector.tensor_reduce(vss[:, t, :], junk_v.rearrange("p (g c) -> p g c", g=NG),
                                              AX.X, ALU.add)
                if t == 0:
                    step(red)
                else:
                    red.then_inc(vss_done, 1)
            mem_stage(0, 3, U_GU[0][0] + 2)
            dve.wait_ge(vrs_done, 1)
            dve.wait_ge(gb1_in, 16)
            for t in range(NT):
                for g in range(NG):
                    v = gv[:, t, g * P:(g + 1) * P]
                    last = nc.vector.scalar_tensor_tensor(v, v, vrs[:, t, g:g + 1], GB1[:, g * P:(g + 1) * P],
                                                          ALU.mult, ALU.mult)
                last.then_inc(vn_done, 1)
            mem_stage(0, 4, U_GU[0][1] + 2)
            split(U_GU[1][0] + 2)
            dve.wait_ge(gbs_in, 16)

            def gate(jj):
                added(A_GU + jj)
                j = A_MIX + jj
                dve.wait_ge(mixed_done, jj + 1)
                for i in range(4):
                    g = 4 * jj + i
                    u_g = gu[:, :, g * P:(g + 1) * P]
                    mixed = A[j % 2][i // 2][:, (i % 2) * SEQ:(i % 2 + 1) * SEQ]
                    last = nc.vector.scalar_tensor_tensor(u_g, mixed.rearrange("p (t c) -> p t c", t=NT),
                                                          gbs[:, g:g + 1], u_g, ALU.add, ALU.mult)
                last.then_inc(a_free[j % 2], 2)

            gate(0)
            split(U_GU[1][1] + 2)

            def gated_lo(b):
                for t in range(NT):
                    hi_part, lo_part = [a[:, 4 * b:4 * b + 4, t * P:(t + 1) * P] for a in xTv]
                    t_lo(T_U + 2 * b + t, lo_part, hi_part)

            (a0, a1), (b0, b1), (c0, c1) = U_OUT[0]
            gated_lo(0)
            gate(1)
            split(a0 + 2)
            gated_lo(1)
            split(a1 + 2)
            split(b0 + 2)
            split(b1 + 2)
            dve.wait_ge(gb2_in, 16)
            add_residual(A_OUT[0], 0, 512, c0)
            added(A_OUT[0])
            times_gain(0, GB2)
            split(c0 + 2)
            half_lo(T_FN[0], xTv, 0)
            add_residual(A_OUT[0] + 1, 512, 512, c1)
            added(A_OUT[0] + 1)
            times_gain(1, GB2)
            half_lo(T_FN[0], xTv, 1)
            split(c1 + 2)
            dve.wait_ge(rstd_done, N_FN[0] + 1)

            def rotary_angles():
                dve.wait_ge(rope_in, 32)
                step(nc.vector.tensor_copy(posf[:, :], posi[:, :]))
                ang, turns = rt[:, 0:4].rearrange("p i t e -> p (i t e)"), rt[:, 4:8].rearrange(
                    "p i t e -> p (i t e)")
                for t in range(NT):
                    step(nc.vector.tensor_scalar(ang[:, t * 32:(t + 1) * 32], freq[:, :], posf[:, t:t + 1],
                                                 None, ALU.mult))
                for i, quarter in enumerate((np.pi / 2, 0.0)):
                    step(nc.vector.tensor_scalar(turns, ang, float(quarter), float(1 / TWO_PI), ALU.add,
                                                 ALU.mult))
                    step(nc.vector.tensor_scalar(turns, turns, MAGIC, None, ALU.add))
                    step(nc.vector.tensor_scalar(turns, turns, -MAGIC, None, ALU.add))
                    csv = cs[:, i].rearrange("p t r -> p (t r)")
                    src = ang
                    for c in two_pi_parts():
                        step(nc.vector.scalar_tensor_tensor(csv, turns, -c, src, ALU.mult, ALU.add))
                        src = csv
                    step(nc.vector.tensor_scalar(csv, csv, float(quarter), 3.1415925, ALU.add, ALU.min))
                    last = nc.vector.tensor_scalar(csv, csv, -3.1415925, None, ALU.max)
                    if i == 0:
                        step(last)
                last.then_inc(rope_ang, 1)

            for hf in range(2):
                gu_units, down_units = U_FF[hf]
                j0, tj = A_FF[hf], T_FH[hf]

                def hidden_lo(i, b0, n):
                    for t in range(NT):
                        hi_part, lo_part = [a[:, b0:b0 + n, t * P:(t + 1) * P] for a in wkv]
                        t_lo(tj + 2 * i + t, lo_part, hi_part, n)

                for c in range(4):
                    g, u = gu_units[c]
                    if c >= 2:
                        hidden_lo(c - 2, 4 * (c - 2), 4)
                    split(g + 2)
                    dve.wait_ge(used, u + 1)
                    jg, ju = j0 + 2 * c, j0 + 2 * c + 1
                    dve.wait_ge(a_free[jg % 2], 2 * (jg // 2 + 1))
                    for t in range(NT):
                        nc.vector.scalar_tensor_tensor(fhid[:, t, c * FCH:(c + 1) * FCH],
                                                       A[ju % 2][t][:, 0:FCH], rstd[:, N_FN[0], t:t + 1],
                                                       fsilu[:, t, :], ALU.mult, ALU.mult
                                                       ).then_inc(a_free[ju % 2], 1)
                    split(u + 2)
                hidden_lo(2, 8, 3)
                for c in range(4):
                    if hf == 1 and c == 3:
                        half_lo(T_MEM[1], xTv, 1)
                    add_residual(j0 + 8 + c, c * 256, 256, down_units[c])
                    if hf == 1 and c == 1:
                        dve.wait_ge(gb1_in, 32)
                        dve.wait_ge(mem2_in, 16)
                        normalise(N_MEM[1], memt, memt, GB1)
                    split(down_units[c] + 2)
                    if hf == 0 and c == 1:
                        rotary_angles()
                    if hf == 1 and c == 2:
                        half_lo(T_MEM[1], xTv, 0)

            dve.wait_ge(gb2_in, 32)
            for c in range(4):
                added(A_FF[1] + 8 + c)
            times_gain(0, GB2)
            times_gain(1, GB2)
            split(U_K1[0] + 2)
            split(U_K1[1] + 2)
            split(U_V1[0] + 2)
            half_lo(T_X[1], wkv, 0)
            memory_values(1, U_V1)
            half_lo(T_X[1], wkv, 1)
            split(U_V1[1] + 2)
            memory_scale(1)
            for i, (c0, n) in enumerate(C_CHUNKS):
                j = A_C + i
                dve.wait_ge(used, U_C[i] + 1)
                if c0 + n > D:
                    nc.vector.tensor_scalar(kraw[:, 1, :], A[j % 2][1][:, D - c0:n], rstd[:, N_X[1], 1:2],
                                            None, ALU.mult)
                    n = D - c0
                nc.vector.tensor_scalar(lat[:, 1, c0:c0 + n], A[j % 2][1][:, 0:n], rstd[:, N_X[1], 1:2], None,
                                        ALU.mult).then_inc(a_free[j % 2], 1)
                split(U_C[i] + 2)
            dve.wait_ge(rstd_done, N_CKV + 1)
            dve.wait_ge(gb1_in, 64)
            for t in range(NT):
                for n, c0, c1 in ((N_CQ, 0, QL), (N_CKV, QL, D)):
                    last = nc.vector.scalar_tensor_tensor(lat[:, t, c0:c1], lat[:, t, c0:c1],
                                                          rstd[:, n, t:t + 1], GB1[:, c0:c1],
                                                          ALU.mult, ALU.mult)
                last.then_inc(c_ready, 1)
            split(U_Q1[0] + 2)
            half_lo(T_C, xTv, 0)
            half_lo(T_C, xTv, 1)
            split(U_Q1[1] + 2)
            added(A_C + 2)

            def rotate(src, dst, scratch, heads):
                c, s_ = [cs[:, i].unsqueeze(2).to_broadcast([P, NT, heads, 32]) for i in range(2)]
                x1, x2 = src[:, :, :, 0:32], src[:, :, :, 32:64]
                for i, (a, b) in enumerate(((x1, c), (x2, s_), (x2, c), (x1, s_))):
                    step(nc.vector.tensor_tensor(scratch[i], a, b, ALU.mult))
                step(nc.vector.tensor_tensor(dst[:, :, :, 0:32], scratch[0], scratch[1], ALU.subtract))
                return nc.vector.tensor_tensor(dst[:, :, :, 32:64], scratch[2], scratch[3], ALU.add)

            small = rt[:, 0:8].rearrange("p i t e -> p (i t e)").rearrange("p (a t o r) -> p a t o r", a=2, t=NT, o=1)
            small2 = rt[:, 8:12].rearrange("p i t e -> p (i t e)").rearrange("p (t o r) -> p t o r", t=NT, o=1)
            small3 = rsm[:, :].rearrange("p (t o r) -> p t o r", t=NT, o=1)
            dve.wait_ge(rope_cs, 1)
            step(nc.vector.memset(kr[:, :, :, :], 0.0))
            for b in range(2):
                last = rotate(kraw[:, :, :].unsqueeze(2), kr[:, b, :, b * 64:(b + 1) * 64].unsqueeze(2),
                              [small[:, 0], small[:, 1], small2, small3], 1)
                if b == 0:
                    step(last)
            last.then_inc(rope_done, 1)
            dve.wait_ge(used, U_QR + 1)
            nc.vector.tensor_copy(qr[:, 1, :, :], A[A_UQ % 2][1][:, :].rearrange("p (h r) -> p h r", h=HEADS)
                                  ).then_inc(a_free[A_UQ % 2], 1)
            mem_stage(1, -1, 0)
            split(U_QR + 2)
            added(A_UQ)
            for i in range(2):
                u, j = U_UQ[i], A_UQ + 1 + i
                mem_stage(1, 2 * i, 0)
                if i:
                    dve.wait_ge(rope_done, 2)
                heads4 = qr[:, :, 4 * i:4 * i + 4, :]
                rotate(heads4, heads4, [tmp[:, i_] for i_ in range(4)], 4).then_inc(rope_done, 1)
                dve.wait_ge(used, u + 1)
                nc.vector.tensor_copy(qn[:, 4 * i + 2:4 * i + 4, :],
                                      A[j % 2][1][:, :].rearrange("p (h s) -> p h s", h=2)
                                      ).then_inc(a_free[j % 2], 1)
                mem_stage(1, 2 * i + 1, 0)
                split(u + 2)

            def keys_values(i):
                u, j = U_UKV[i], A_UKV + 2 * i
                dve.wait_ge(used, u + 1)
                nc.vector.tensor_copy(kn[:, 4 * i + 2:4 * i + 4, :],
                                      A[j % 2][1][:, :].rearrange("p (h s) -> p h s", h=2)
                                      ).then_inc(a_free[j % 2], 1)
                j += 1
                nc.vector.tensor_copy(lv[:, 1, i * 512:(i + 1) * 512], A[j % 2][1][:, :]
                                      ).then_inc(a_free[j % 2], 1)

            dve.wait_ge(rope_done, 3)
            keys_values(0)
            mem_stage(1, 4, 0)
            lat_stage(-1)
            split(U_UKV[0] + 2)
            keys_values(1)
            lat_stage(0)
            split(U_UKV[1] + 2)
            (a0, a1), (b0, b1), (c0, c1) = U_OUT[1]
            for stages, u in (((1,), a0), ((2, 3), a1), ((4,), b0), ((5, 6), b1)):
                for g in stages:
                    lat_stage(g)
                split(u + 2)
            dve.wait_ge(gb1_in, 80)
            add_residual(A_OUT[1], 0, 512, c0)
            added(A_OUT[1])
            times_gain(0, GB1)
            split(c0 + 2)
            add_residual(A_OUT[1] + 1, 512, 512, c1)
            added(A_OUT[1] + 1)
            times_gain(1, GB1)
            step(nc.vector.memset(gate_of[:, :, :], 0.0))
            step(nc.vector.memset(slot_of[:, :, :], -1.0))

            def bc(a):
                return a.unsqueeze(2).to_broadcast([P, NT, E])

            mask, lg, eq, oh1, oh2, g = (rt[:, i] for i in range(6))
            j = A_RT
            dve.wait_ge(rstd_done, N_FN[1] + 1)
            dve.wait_ge(rout_in, 32)
            dve.wait_ge(route_mm, 1)
            for t in range(NT):
                last = nc.vector.scalar_tensor_tensor(lg[:, t, :], A[j % 2][t][:, 0:E],
                                                      rstd[:, N_FN[1], t:t + 1], br[:, :], ALU.mult, ALU.add)
            last.then_inc(a_free[j % 2], 2)
            dve.wait_ge(a_free[j % 2], 2 * (j // 2 + 1))
            pr = prio[:, :].unsqueeze(1).to_broadcast([P, NT, E])
            for i, oh in enumerate((oh1, oh2)):
                step(nc.vector.tensor_reduce(r1[:, i, :], lg, AX.X, ALU.max))
                step(nc.vector.tensor_tensor(eq, lg, bc(r1[:, i, :]), ALU.is_equal))
                step(nc.vector.tensor_tensor(eq, eq, pr, ALU.mult))
                step(nc.vector.tensor_reduce(r1[:, 9, :], eq, AX.X, ALU.max))
                step(nc.vector.tensor_tensor(oh, eq, bc(r1[:, 9, :]), ALU.is_equal))
                if i == 0:
                    step(nc.vector.scalar_tensor_tensor(lg, oh, NEG, lg, ALU.mult, ALU.add))
            nc.vector.tensor_tensor(r1[:, 2, :], r1[:, 1, :], r1[:, 0, :], ALU.subtract).then_inc(rt_exp_in, 1)
            nc.vector.tensor_tensor(mask, oh1, oh2, ALU.add).then_inc(mask_done, 1)
            for t in range(NT):
                dve.wait_ge(xs_hi, t + 1)
                nc.vector.scalar_tensor_tensor(xs[1][:, t, :], xn[:, t, :], rstd[:, N_FN[1], t:t + 1],
                                               xs[0][:, t, :].bitcast(F32), ALU.mult, ALU.subtract
                                               ).then_inc(xs_done, 1)
            j = A_RT + 1
            dve.wait_ge(route_mm, 2)
            for t in range(NT):
                step(nc.vector.scalar_tensor_tensor(slot_of[:, t, 0:E], A[j % 2][t][:, 0:E], 1e4,
                                                    mask[:, t, :], ALU.add, ALU.mult))
            nc.vector.tensor_reduce(r1[:, 7, 0:1], A[j % 2][0][:, E:2 * E], AX.X, ALU.max
                                    ).then_inc(a_free[j % 2], 2)
            dve.wait_ge(a_free[j % 2], 2 * (j // 2 + 1))
            step(nc.vector.tensor_scalar(slot_of[:, :, E:2 * E], slot_of[:, :, 0:E], -1e4 - P, None, ALU.add))
            step(nc.vector.tensor_scalar(slot_of[:, :, 0:E], slot_of[:, :, 0:E], -1e4, None, ALU.add))

            def one_hot(ve):
                for t in range(NT):
                    last = nc.vector.tensor_scalar(sel[:, t * P:(t + 1) * P], iota,
                                                   slot_of[:, t, bass.ds(ve, 1)], None, ALU.is_equal)
                last.then_inc(sel_done, 1)

            def gathered_lo(tj, it):
                for b in range(2):
                    j, cols = tj + b, slice(b * 512, (b + 1) * 512)
                    dve.wait_ge(t_free[j % 2], it * 8 + 2 * (j // 2) + 1)
                    nc.vector.tensor_tensor(xg[1][:, cols], T[j % 2][:, :], xg[0][:, cols].bitcast(F32),
                                            ALU.subtract).then_inc(t_free[j % 2], 1)

            def output_lo(c, it):
                dve.wait_ge(y_hi, it * 2 + c + 1)
                cols = slice(c * 512, (c + 1) * 512)
                nc.vector.tensor_tensor(ys[1][:, cols], S[(S_MOE + c) % 2][:, :], ys[0][:, cols].bitcast(F32),
                                        ALU.subtract).then_inc(s_free[(S_MOE + c) % 2], 1)

            def add_outputs(t, ve):
                for c in range(2):
                    s = S_MOE + 2 + 2 * t + c
                    dve.wait_ge(scat_done, ve * 4 + 2 * t + c + 2)
                    cols = slice(c * 512, (c + 1) * 512)
                    nc.vector.scalar_tensor_tensor(h[:, t, cols], S[s % 2][:, :],
                                                   gate_of[:, t, bass.ds(ve, 1)], h[:, t, cols],
                                                   ALU.mult, ALU.add).then_inc(s_free[s % 2], 1)

            def multiply(c, ve, t_before):
                jg, ju = A_MOE + 2 * c, A_MOE + 2 * c + 1
                dve.wait_ge(used, ve * MU + U_MOE + 4 * c + 4)
                dve.wait_ge(a_free[jg % 2], ve * 4 + 2 * (jg // 2 + 1))
                dve.wait_ge(t_done, ve * 8 + t_before)
                for b in range(2):
                    cols = slice(b * EN, (b + 1) * EN)
                    nc.vector.tensor_tensor(ehid[:, cols], A[ju % 2][b][:, 0:EN], esilu[:, cols],
                                            ALU.mult).then_inc(a_free[ju % 2], 1)

            def hidden_lo(c, tj, ve):
                for n, blocks in enumerate((4, 3)):
                    j, at = tj + n, (7 * c + 4 * n) * P
                    dve.wait_ge(t_free[j % 2], ve * 8 + 2 * (j // 2) + 1)
                    nc.vector.tensor_tensor(hT[1][:, at:at + blocks * P], T[j % 2][:, 0:blocks * P],
                                            hT[0][:, at:at + blocks * P].bitcast(F32), ALU.subtract
                                            ).then_inc(t_free[j % 2], 1)

            dve.wait_ge(consts, 2)
            one_hot(0)
            step(nc.vector.tensor_scalar(r1[:, 7, 1:2], r1[:, 7, 0:1], P + 0.5, float(E), ALU.is_gt, ALU.mult))
            nc.vector.tensor_scalar(nround[:, :], r1[:, 7, 1:2], float(E), None, ALU.add).then_inc(route_done, 1)
            dve.wait_ge(rt_exp, 1)
            step(nc.vector.tensor_scalar(r1[:, 4, :], r1[:, 3, :], 1.0, None, ALU.add))
            step(nc.vector.reciprocal(r1[:, 5, :], r1[:, 4, :]))
            step(nc.vector.tensor_tensor(r1[:, 6, :], r1[:, 3, :], r1[:, 5, :], ALU.mult))
            step(nc.vector.tensor_tensor(oh1, oh1, bc(r1[:, 5, :]), ALU.mult))
            step(nc.vector.tensor_tensor(oh2, oh2, bc(r1[:, 6, :]), ALU.mult))
            for r in range(2):
                step(nc.vector.tensor_tensor(gate_of[:, :, 1 + r * E:1 + (r + 1) * E], oh1, oh2, ALU.add))
            gathered_lo(T_MOE, 0)
            split(c1 + 2)
            rounds = dve.value_load(nround[0:1, 0:1], min_val=E, max_val=2 * E)
            U, t1 = U_MOE, T_MOE + 2
            with dve.Fori(0, rounds) as ve:
                output_lo(0, ve)
                output_lo(1, ve)
                split(U + 2, ve)
                add_outputs(0, ve)
                split(U + 3, ve)
                add_outputs(1, ve)
                split(U + 4, ve)
                multiply(0, ve, t1)
                split(U + 5, ve)
                dve.wait_ge(t_done, ve * 8 + t1 + 2)
                one_hot(ve + 1)
                split(U + 6, ve)
                split(U + 7, ve)
                hidden_lo(0, t1 + 2, ve)
                split(U + 8, ve)
                multiply(1, ve, t1 + 4)
                split(U + 9, ve)
                hidden_lo(1, t1 + 4, ve)
                split(U + 10, ve)
                split(U + 11, ve)
                with dve.If(ve < rounds - 1):
                    gathered_lo(t1 + 6, ve)
                    split(U, ve + 1)
                    split(U + 1, ve + 1)
            output_lo(0, rounds)
            output_lo(1, rounds)
            add_outputs(0, rounds)
            add_outputs(1, rounds)
            dve.wait_ge(gb2_in, 48)
            for t in range(NT):
                dve.wait_ge(rstd_done, N_FINAL + t + 1)
                nc.vector.scalar_tensor_tensor(xn[:, t, :], h[:, t, :], rstd[:, N_FINAL, t:t + 1],
                                               GB2[:, :], ALU.mult, ALU.mult).then_inc(xn_done, 1)

        @block.gpsimd
        def _(pool):
            steps = [0]

            def step(ins):
                steps[0] += 1
                ins.then_inc(pool_step, 1)
                pool.wait_ge(pool_step, steps[0])

            def gain(dst, vector, done, n=D):
                pool.dma_start(dst, vector.partition_broadcast(P)).then_inc(done, 16)

            def inverse_rms(out, sums, n_values, done, cols):
                step(nc.gpsimd.tensor_scalar(out, sums, 1.0 / n_values, EPS, ALU.mult, ALU.add))
                nc.gpsimd.tensor_tensor(out, out, mhalf[:, 0:cols], ALU.pow).then_inc(done, 1)

            def norm(n, n_values=D):
                pool.wait_ge(ssum_done, 2 * n + 2)
                inverse_rms(rstd[:, n, :], ssum[:, n, :], n_values, rstd_done, NT)

            step(nc.gpsimd.memset(mhalf[:, :], -0.5))
            for a, v in ((ident, 0.0), (ones, 1.0), (tri, 1.0), (tris, 1.0), (cmask, 0.0)):
                step(nc.gpsimd.memset(a[:, :], v))
            step(nc.gpsimd.affine_select(out=ident[:, :], in_=ident[:, :], pattern=[[-1, P]],
                                         compare_op=ALU.not_equal, fill=1.0, base=0, channel_multiplier=1))
            step(nc.gpsimd.affine_select(out=tri[:, :], in_=tri[:, :], pattern=[[1, P]],
                                         compare_op=ALU.is_ge, fill=0.0, base=0, channel_multiplier=-1))
            step(nc.gpsimd.affine_select(out=tris[:, :], in_=tris[:, :], pattern=[[1, P]],
                                         compare_op=ALU.is_gt, fill=0.0, base=0, channel_multiplier=-1))
            step(nc.gpsimd.affine_select(out=cmask[:, :], in_=cmask[:, :], pattern=[[-1, P]],
                                         compare_op=ALU.is_ge, fill=NEG, base=0, channel_multiplier=1))
            nc.gpsimd.iota(prio[:, :], pattern=[[-1, E]], base=E, channel_multiplier=0,
                           allow_small_or_imprecise_dtypes=True).then_inc(consts, 1)
            norm(N_MEM[0])
            norm(N_X[0])
            pool.wait_ge(xn_done, XN_OF["mem0"])
            gain(GB2[:, :], ffn_norm[0], gb2_in)
            pool.wait_ge(xn_done, XN_OF["fn0"])
            gain(GB1[:, :], gm_v_norm[0], gb1_in)
            pool.wait_ge(vss_done, 1)
            inverse_rms(vrs[:, :, :].rearrange("p t g -> p (t g)"), vss[:, :, :].rearrange("p t g -> p (t g)"),
                        P, vrs_done, NT * NG)
            pool.wait_ge(vn_done, NT)
            gain(GB1[:, :], mem_norm[1], gb1_in)
            norm(N_FN[0])
            pool.wait_ge(xn_done, XN_OF["mem1"])
            gain(GB2[:, :], attn_norm[1], gb2_in)
            j = A_FF[1] + 7
            pool.wait_ge(a_free[j % 2], 2 * (j // 2 + 1))
            pool.dma_start(memt, mem[0].rearrange("(t p) d -> p t d", p=P)).then_inc(mem2_in, 16)
            norm(N_MEM[1])
            norm(N_X[1])
            pool.wait_ge(xn_done, XN_OF["x1"])
            gain(GB1[:, 0:QL], mla_q_norm[0], gb1_in)
            gain(GB1[:, QL:D], mla_kv_norm[0], gb1_in)
            norm(N_CQ, QL)
            norm(N_CKV, KVL)
            pool.wait_ge(t_done, T_ROPE + 2)
            gain(GB1[:, :], ffn_norm[1], gb1_in)
            pool.wait_ge(t_done, T_FN[1])
            gain(GB2[:, :], final_norm, gb2_in)
            norm(N_FN[1])
            nc.gpsimd.iota(iota, pattern=[[1, P]], base=0, channel_multiplier=0,
                           allow_small_or_imprecise_dtypes=True).then_inc(consts, 1)
            for a in (selT[:, :], ys[0], ys[1]):
                last = nc.gpsimd.memset(a.bitcast(F32), 0.0)
            last.then_inc(moe_const, 1)
            for t in range(NT):
                pool.wait_ge(ssum_done, 2 * N_FINAL + t + 1)
                inverse_rms(rstd[:, N_FINAL, t:t + 1], ssum[:, N_FINAL, t:t + 1], D, rstd_done, 1)


INPUTS = ["x", "mem", "positions", "attn_norm", "mem_norm", "w_mem_kv", "ffn_norm", "final_norm",
          "gm_w_in", "gm_v_norm", "gm_w_s", "gm_b_s", "gm_w_out",
          "mla_w_in", "mla_q_norm", "mla_w_uq", "mla_kv_norm", "mla_w_ukv", "mla_w_out",
          "ff_w_gate", "ff_w_up", "ff_w_down",
          "moe_w_router", "moe_b_router", "moe_w_gate", "moe_w_up", "moe_w_down"]


def kernel(**inputs):
    import concourse.bacc as bacc
    from concourse.bass_utils import run_bass_kernel_spmd

    nc = bacc.Bacc("TRN2", target_bir_lowering=False, num_devices=1)
    arrays = {f"in_{name}": np.ascontiguousarray(inputs[name]) for name in INPUTS}
    steps = np.arange(0, ROPE, 2, dtype=np.float32) / np.float32(ROPE)
    arrays["in_rope_freq"] = (1.0 / np.float32(10000.0) ** steps).astype(np.float32)
    args = [nc.dram_tensor(name, a.shape, mybir.dt.from_np(a.dtype), kind="ExternalInput").ap()
            for name, a in arrays.items()]
    out = nc.dram_tensor("out_0", (1, SEQ, D), F32, kind="ExternalOutput").ap()
    build(nc, *args, out)
    got = run_bass_kernel_spmd(nc, [arrays], core_ids=[0])
    return got.results[0]["out_0"]
```
